# Optimizing a Trainium2 kernel written in Bass

```python
import jax, jax.numpy as jnp
from jax import lax
import numpy as np

D_MODEL = 2048
BATCH = 1
SEQ = 512
DEPTH = 1

CHUNK = 64
D_MIX = D_MODEL
D_RWKV = D_MIX // 2
RWKV_HEAD = 64
RWKV_HEADS = D_RWKV // RWKV_HEAD
D_CONV = D_MIX - D_RWKV
CONV_WIDTH = 3
D_IN = 3 * D_RWKV + 3 * D_CONV
LORA_DECAY = 64
LORA_AAA = 64
LORA_GATE = 160
GN_EPS = 64e-5
RMS_EPS = 1e-6
PEER_HEADS = 8
PEER_NKEYS = 128
PEER_EXPERTS = PEER_NKEYS * PEER_NKEYS
PEER_QDIM = 512
PEER_HALF = PEER_QDIM // 2
PEER_TOPK = 16
PEER_BLOCK = 128

kernel_name = "hymba_rwkv7_shortconv_peer_block"

def rms_norm(x, gain):
    xf = x.astype(jnp.float32)
    y = xf * lax.rsqrt(jnp.mean(xf * xf, axis=-1, keepdims=True) + RMS_EPS)
    return (y * gain.astype(jnp.float32)).astype(x.dtype)

def token_shift(t):
    return jnp.pad(t, ((0, 0), (1, 0), (0, 0)))[:, :-1]

def rwkv7_scan(r, w, k, v, kk, a):
    B, S, H, N = r.shape
    nc = S // CHUNK

    def to_chunks(t):
        return jnp.moveaxis(t.reshape(B, nc, CHUNK, H, N), (1, 2), (0, 1))

    def step(state, inp):
        r_t, w_t, k_t, v_t, kk_t, a_t = inp
        sa = jnp.einsum('bhvk,bhk->bhv', state, -kk_t)
        state = (state * w_t[:, :, None, :]
                 + sa[..., None] * (kk_t * a_t)[:, :, None, :]
                 + v_t[..., None] * k_t[:, :, None, :])
        y_t = jnp.einsum('bhvk,bhk->bhv', state, r_t)
        return state, y_t

    def chunk_step(state, chunk_inp):
        return lax.scan(step, state, chunk_inp)

    state0 = jnp.zeros((B, H, N, N), jnp.float32)
    _, y = lax.scan(chunk_step, state0, tuple(to_chunks(t) for t in (r, w, k, v, kk, a)))
    return jnp.moveaxis(y, (0, 1), (1, 2)).reshape(B, S, H, N)

def causal_depthwise_conv(u, conv_w):
    S = u.shape[1]
    up = jnp.pad(u, ((0, 0), (CONV_WIDTH - 1, 0), (0, 0)))
    out = up[:, 0:S] * conv_w[0]
    for j in range(1, CONV_WIDTH):
        out = out + up[:, j:j + S] * conv_w[j]
    return out

def peer_ffn(h, wq, keys, u_tab, v_tab):
    B, S, D = h.shape
    q = (h @ wq).reshape(B, S, PEER_HEADS, 2, PEER_HALF)
    s = jnp.einsum('bshcd,hcnd->bshcn', q, keys).astype(jnp.float32)
    top_s, top_i = lax.top_k(s, PEER_TOPK)
    cand = top_s[..., 0, :, None] + top_s[..., 1, None, :]
    cand_s, cand_i = lax.top_k(cand.reshape(B, S, PEER_HEADS, PEER_TOPK * PEER_TOPK), PEER_TOPK)
    e1 = jnp.take_along_axis(top_i[..., 0, :], cand_i // PEER_TOPK, axis=-1)
    e2 = jnp.take_along_axis(top_i[..., 1, :], cand_i % PEER_TOPK, axis=-1)
    expert = e1 * PEER_NKEYS + e2
    gates = jax.nn.softmax(cand_s, axis=-1).astype(h.dtype)

    T = B * S
    nb = T // PEER_BLOCK
    hk = PEER_HEADS * PEER_TOPK
    xb = h.reshape(nb, PEER_BLOCK, D)
    ib = expert.reshape(nb, PEER_BLOCK, hk)
    gb = gates.reshape(nb, PEER_BLOCK, hk)

    def block(args):
        xt, it, gt = args
        u = jnp.take(u_tab, it, axis=0)
        act = jax.nn.gelu(jnp.einsum('pd,pkd->pk', xt, u)) * gt
        vv = jnp.take(v_tab, it, axis=0)
        return jnp.einsum('pk,pkd->pd', act, vv)

    out = lax.map(block, (xb, ib, gb))
    return out.reshape(B, S, D)

def setup_inputs(seed: int = 0) -> dict:
    key = jax.random.key(seed)
    ks = jax.random.split(key, 32)
    f32 = jnp.float32
    L, D = DEPTH, D_MODEL

    def nrm(k, shape, scale):
        return jax.random.normal(k, shape, f32) * scale

    x = jax.random.normal(ks[0], (BATCH, SEQ, D), f32)
    norm_mix = 1.0 + nrm(ks[1], (L, D), 0.02)
    w_in = nrm(ks[2], (L, D, D_IN), D ** -0.5)
    mu_rkv = jax.random.uniform(ks[3], (L, 3 * D_RWKV), f32)
    mu_lora = jax.random.uniform(ks[4], (L, 3, D), f32)
    w0 = -3.0 + nrm(ks[5], (L, D_RWKV), 1.0)
    w1 = nrm(ks[6], (L, D, LORA_DECAY), D ** -0.5)
    w2 = nrm(ks[7], (L, LORA_DECAY, D_RWKV), 0.5 * LORA_DECAY ** -0.5)
    a0 = nrm(ks[8], (L, D_RWKV), 0.5)
    a1 = nrm(ks[9], (L, D, LORA_AAA), D ** -0.5)
    a2 = nrm(ks[10], (L, LORA_AAA, D_RWKV), 0.5 * LORA_AAA ** -0.5)
    g1 = nrm(ks[11], (L, D, LORA_GATE), D ** -0.5)
    g2 = nrm(ks[12], (L, LORA_GATE, D_RWKV), LORA_GATE ** -0.5)
    k_k = 0.85 + nrm(ks[13], (L, D_RWKV), 0.05)
    k_a = 1.0 + nrm(ks[14], (L, D_RWKV), 0.05)
    r_k = nrm(ks[15], (L, RWKV_HEADS, RWKV_HEAD), 0.1)
    gn_w = 1.0 + nrm(ks[16], (L, D_RWKV), 0.02)
    gn_b = nrm(ks[17], (L, D_RWKV), 0.02)
    conv_w = nrm(ks[18], (L, CONV_WIDTH, D_CONV), CONV_WIDTH ** -0.5)
    w_out = nrm(ks[19], (L, D_MIX, D), D_MIX ** -0.5)
    norm_ffn = 1.0 + nrm(ks[20], (L, D), 0.02)
    peer_wq = nrm(ks[21], (L, D, PEER_HEADS * PEER_QDIM), D ** -0.5)
    peer_keys = nrm(ks[22], (L, PEER_HEADS, 2, PEER_NKEYS, PEER_HALF), PEER_HALF ** -0.5)
    peer_u = nrm(ks[23], (L, PEER_EXPERTS, D), D ** -0.5)
    peer_v = nrm(ks[24], (L, PEER_EXPERTS, D), 0.05)
    norm_final = 1.0 + nrm(ks[25], (D,), 0.02)
    return {"x": x, "norm_mix": norm_mix, "w_in": w_in, "mu_rkv": mu_rkv, "mu_lora": mu_lora,
            "w0": w0, "w1": w1, "w2": w2, "a0": a0, "a1": a1, "a2": a2, "g1": g1, "g2": g2,
            "k_k": k_k, "k_a": k_a, "r_k": r_k, "gn_w": gn_w, "gn_b": gn_b, "conv_w": conv_w,
            "w_out": w_out, "norm_ffn": norm_ffn, "peer_wq": peer_wq, "peer_keys": peer_keys,
            "peer_u": peer_u, "peer_v": peer_v, "norm_final": norm_final}

def reference(x, norm_mix, w_in, mu_rkv, mu_lora, w0, w1, w2, a0, a1, a2, g1, g2,
              k_k, k_a, r_k, gn_w, gn_b, conv_w, w_out, norm_ffn, peer_wq, peer_keys,
              peer_u, peer_v, norm_final):
    B, S, _ = x.shape
    H, N = RWKV_HEADS, RWKV_HEAD
    f32 = jnp.float32
    for l in range(DEPTH):
        h = rms_norm(x, norm_mix[l])
        proj = h @ w_in[l]
        rkv = proj[..., :3 * D_RWKV]
        rkv = rkv + (token_shift(rkv) - rkv) * mu_rkv[l]
        r, k, v = jnp.split(rkv, 3, axis=-1)
        b_gate, c_gate, xc = jnp.split(proj[..., 3 * D_RWKV:], 3, axis=-1)

        dh = token_shift(h) - h
        xw = h + dh * mu_lora[l, 0]
        xa = h + dh * mu_lora[l, 1]
        xg = h + dh * mu_lora[l, 2]
        w_log = -jax.nn.softplus(-(w0[l] + jnp.tanh(xw @ w1[l]) @ w2[l])) - 0.5
        decay = jnp.exp(-jnp.exp(w_log.astype(f32)))
        a = jax.nn.sigmoid(a0[l] + (xa @ a1[l]) @ a2[l])
        g = jax.nn.sigmoid(xg @ g1[l]) @ g2[l]

        kk = (k * k_k[l]).astype(f32).reshape(B, S, H, N)
        kk = kk / jnp.maximum(jnp.sqrt(jnp.sum(kk * kk, axis=-1, keepdims=True)), 1e-12)
        k = k * (1.0 + (a - 1.0) * k_a[l])

        rh = r.astype(f32).reshape(B, S, H, N)
        kh = k.astype(f32).reshape(B, S, H, N)
        vh = v.astype(f32).reshape(B, S, H, N)
        ah = a.astype(f32).reshape(B, S, H, N)
        y = rwkv7_scan(rh, decay.reshape(B, S, H, N), kh, vh, kk, ah)

        mean = jnp.mean(y, axis=-1, keepdims=True)
        var = jnp.mean(jnp.square(y - mean), axis=-1, keepdims=True)
        y = (y - mean) * lax.rsqrt(var + GN_EPS)
        y = y * gn_w[l].reshape(H, N).astype(f32) + gn_b[l].reshape(H, N).astype(f32)
        y = y + jnp.sum(rh * kh * r_k[l].astype(f32), axis=-1, keepdims=True) * vh
        y_rwkv = (y.reshape(B, S, D_RWKV) * g.astype(f32)).astype(x.dtype)

        y_conv = b_gate * causal_depthwise_conv(c_gate * xc, conv_w[l])

        mix = jnp.concatenate([y_rwkv, y_conv], axis=-1) @ w_out[l]
        x = x + mix

        h2 = rms_norm(x, norm_ffn[l])
        x = x + peer_ffn(h2, peer_wq[l], peer_keys[l], peer_u[l], peer_v[l])
    return rms_norm(x, norm_final)


_drawn_inputs = setup_inputs


def setup_inputs(seed=0):
    import zlib

    import numpy as np

    out = dict(_drawn_inputs(seed))
    spreads = {}
    factors = {'w1': 6.065,
     'w2': 6.091,
     'k_k': 5.28,
     'k_a': 3.438,
     'gn_w': 8.0,
     'gn_b': 8.0,
     'norm_ffn': 8.0,
     'peer_wq': 2.991,
     'peer_keys': 3.007,
     'peer_u': 3.329,
     'peer_v': 2.988,
     'norm_final': 2.724}
    for name, (base, spread) in spreads.items():
        noise = np.random.default_rng([zlib.crc32(name.encode()), seed]).standard_normal(out[name].shape)
        drawn = base * np.exp(spread * noise) if base else spread * noise
        out[name] = __import__('jax').numpy.asarray(drawn.astype(out[name].dtype))
    for name, factor in factors.items():
        out[name] = (out[name] * factor).astype(out[name].dtype)
    return out
```

```python
from contextlib import ExitStack

import concourse.bass as bass
from concourse import mybir

F32 = mybir.dt.float32
I32 = mybir.dt.int32
U32 = mybir.dt.uint32
ALU = mybir.AluOpType
ACT = mybir.ActivationFunctionType
AX_X = mybir.AxisListType.X

P = 128
T, D = 512, 2048
SPAN = 256
SPANS = T // SPAN
BLOCKS = SPAN // P
KT = D // P
CHUNK = 64
CHUNKS = SPAN // CHUNK
HALF = 64
D_RWKV = D // 2
PAIRS = D_RWKV // P
CONVS = D_RWKV // P
LEVELS = 6
W_TILES = 6 * PAIRS
LORA_W, LORA_A, LORA_G = 64, 64, 160
LORA = LORA_W + LORA_A + LORA_G
HEADS, HALVES, NKEYS, TOPK = 8, 2, 128, 16
SIDES = HEADS * HALVES
Q_TILES = 2 * SIDES
PICKS = HEADS * TOPK
RMS_EPS, GN_EPS = 1e-6, 64e-5
EXP_M_HALF = 0.6065306597126334
FAR = -3.0e38
GELU_C, GELU_S = 0.044715, 0.7978845608028654
PAD = 2

VEC = {}
for _name, _n in (("norm_mix", KT), ("mu_rkv", 3 * PAIRS), ("w0", PAIRS), ("a0", PAIRS), ("k_k", PAIRS),
                  ("k_a", PAIRS), ("r_k", PAIRS), ("gn_w", PAIRS), ("gn_b", PAIRS), ("conv_w", 3 * CONVS),
                  ("mu_lora", 3 * KT), ("eps", 2)):
    VEC[_name] = (sum(n for _, n in VEC.values()), _n)
N_VEC = sum(n for _, n in VEC.values())
CON = {}
for _name, _n in (("ident", P), ("head_ones", P), ("head_mean", P), ("eye", CHUNK), ("before", CHUNK),
                  ("upto", CHUNK), ("low0", CHUNK), ("up", LEVELS * CHUNK), ("keep", SPAN), ("iota16", TOPK)):
    CON[_name] = (sum(n for _, n in CON.values()), _n)
N_CON = sum(n for _, n in CON.values())

RING = 3
RING_PER_SPAN = W_TILES + 1 + KT + Q_TILES
GATHERS = 4


class Steps:

    def __init__(self, *names):
        self.names = list(names)

    def __len__(self):
        return len(self.names)

    def after(self, n, name):
        return n * len(self.names) + self.names.index(name) + 1


MIX = Steps("log_decay", "log_prod", "log_prev", "r_step", "r", "k_step", "k", "v_step", "v", "kk_raw", "kk_sq",
            "a_gain", "k_new", "bonus_raw", "R", "K", "p_end", "norm", "inv_norm", "kk", "B", "B_scaled", "A",
            "bonus")
CONV = Steps("u", "tap0", "tap1", "tap2", "gate")
OUTN = Steps("center", "inv", "scaled", "affine", "plus_bonus", "gated")
NORM1 = Steps("mean_sq", "inv", "scaled")
NORM2 = Steps("sum0", "sum1", "sum2", "sum3", "mean_sq", "inv", "scaled")
PICKED = Steps("shifted", "expert_parts", "row", "row_f", "row_hot", "row_part", "row_expert", "col", "col_f", "col_hot",
               "col_part", "col_expert", "expert", "gate_sum", "gate_inv", "gates")
GELU = Steps("square", "cube", "inner", "half", "coef")
FIN = Steps("mean_sq", "inv", "out")


def scan_order():
    order = []
    for pair in range(CHUNKS // 2):
        both = (2 * pair, 2 * pair + 1)
        for name in ("B_t", "K_t", "V_t", "L_T", "L", "LK_T", "RB_T", "RK_T"):
            order += [(c, name, 0) for c in both]
        for l in range(1, LEVELS):
            for name in ("W", "X", "X_T") if l < LEVELS - 1 else ("W", "X_T"):
                order += [(c, name, l) for c in both]
        for c in both:
            order += [(c, name, 0) for name in ("rhs", "SA", "Y", "dS")]
    return order


ORDER = scan_order()
BY_ACT = ("B_t", "K_t", "V_t", "W", "rhs", "SA", "Y")
ACT_STEPS = [s for s in ORDER if s[1] in BY_ACT]
DVE_STEPS = [s for s in ORDER if s[1] not in BY_ACT]


def hymba(nc, A):
    with ExitStack() as ctx:
        def sb(name, shape, dt=F32):
            return ctx.enter_context(nc.sbuf_tensor(name, shape, dt))

        def sem(name):
            return ctx.enter_context(nc.semaphore(name))

        hT = sb("hT", [P, KT * (PAD + SPAN)])
        hT_v = hT[:, :].rearrange("p (k t) -> p k t", k=KT)
        h_pad = sb("h_pad", [P, KT, PAD])
        yT = sb("yT", [P, KT, SPAN])
        ring = sb("ring", [P, RING, D])
        gath = sb("gath", [P, GATHERS, D])
        acc = sb("acc", [P, BLOCKS, D])
        h2 = sb("h2", [P, BLOCKS, D])
        S_COLS = 33 * CHUNK * PAIRS
        S = sb("S", [P, S_COLS])
        w2a2 = sb("w2a2", [P, D_RWKV])
        vec = sb("vec", [P, N_VEC])
        con = sb("con", [P, N_CON])
        wa_in = sb("wa_in", [P, SPAN])
        g_in = sb("g_in", [P, 2, SPAN])
        state = sb("state", [P, 2, PAIRS * CHUNK])
        ssq = sb("ssq", [P, 8])
        rstd = sb("rstd", [P, 8])
        pick_i = sb("pick_i", [P, BLOCKS, PICKS], I32)
        gates = sb("gates", [P, BLOCKS, PICKS])
        dots = sb("dots", [P, BLOCKS, PICKS])
        gel = sb("gel", [P, 2, PICKS])
        p_end = sb("p_end", [P, PAIRS, CHUNKS])
        banks = [ctx.enter_context(nc.psum_tensor(f"bank{i}", [P, 512], F32)) for i in range(8)]

        def v(name, i, n=1):
            return vec[:, VEC[name][0] + i:VEC[name][0] + i + n]

        def c_(name, i=0, n=None):
            o, w = CON[name]
            return con[:, o + i:o + i + (w if n is None else n)]

        ident = c_("ident")

        x_in = S[:, 0:BLOCKS * D].rearrange("p (b d) -> p b d", b=BLOCKS)
        lora_cur = S[:, BLOCKS * D:BLOCKS * D + KT * LORA].rearrange("p (k n) -> p k n", k=KT)
        lora_prev = S[:, BLOCKS * D + KT * LORA:BLOCKS * D + 2 * KT * LORA].rearrange("p (k n) -> p k n", k=KT)
        chan = [S[:, i * PAIRS * SPAN:(i + 1) * PAIRS * SPAN].rearrange("p (h t) -> p h t", h=PAIRS)
                for i in range(5)]
        R_c, A_c, B_c, K_c, bonus = chan
        BUF = PAIRS * CHUNK
        wide = [S[:, 5 * PAIRS * SPAN + i * BUF:5 * PAIRS * SPAN + (i + 1) * BUF] for i in range(13)]
        spare = [hT[:, i * BUF:(i + 1) * BUF] for i in range(8)]
        tmp0 = 5 * PAIRS * SPAN
        WID = PAD + SPAN
        TMP = [S[:, tmp0 + i * WID:tmp0 + (i + 1) * WID] for i in range(24)]
        raw = [[TMP[3 * (i % 2) + j] for j in range(3)] for i in range(2)]
        sig_w, sig_a = TMP[6][:, 0:SPAN], TMP[7][:, 0:SPAN]
        lw, lp, lm = (TMP[8 + i][:, 0:SPAN] for i in range(3))
        diff, r_s, k_s, kk_raw, kk_sq, a_gain, k_new, rk = (TMP[11 + i][:, 0:SPAN] for i in range(8))
        e_p, e_n, e_m = (TMP[19 + i][:, 0:SPAN] for i in range(3))
        nrm, kk = TMP[22][:, 0:SPAN], TMP[23][:, 0:SPAN]
        c_raw, u_c, conv_o = TMP[0], TMP[1], [TMP[2 + i][:, 0:SPAN] for i in range(3)]
        bufs = spare + wide
        B_t, K_t, V_t, L_T, LK_T, X, X_T, W_b, M_b = ([bufs[9 * q + i] for q in range(2)] for i in range(9))
        rhs_b, SA_b, sum_b = bufs[18:21]
        y_c = [wide[0][:, 0:SPAN], wide[1][:, 0:SPAN]]
        y_sq = [wide[2][:, 0:SPAN], wide[3][:, 0:SPAN]]
        y_sd = [wide[4][:, 0:SPAN], wide[5][:, 0:SPAN]]
        y_t = [wide[6 + i][:, 0:SPAN] for i in range(4)]
        x_res = S[:, 0:BLOCKS * D].rearrange("p (b d) -> p b d", b=BLOCKS)
        gain_f = S[:, BLOCKS * D:(BLOCKS + 1) * D]
        keys = S[:, (BLOCKS + 1) * D:(BLOCKS + 3) * D].rearrange("p (s k n) -> p s k n", s=SIDES, k=2)
        q0 = (BLOCKS + 3) * D
        q_T = [S[:, q0 + i * SPAN:q0 + (i + 1) * SPAN] for i in range(4)]
        sc = [S[:, q0 + 4 * SPAN + i * SPAN:q0 + 4 * SPAN + (i + 1) * SPAN].rearrange("p (b n) -> p b n", b=BLOCKS)
              for i in range(2)]
        t0 = 0

        def take(n):
            nonlocal t0
            t0 += n
            return S[:, t0 - n:t0]

        top_s = take(BLOCKS * SIDES * TOPK).rearrange("p (b s k) -> p b s k", b=BLOCKS, s=SIDES)
        top_i = take(BLOCKS * SIDES * TOPK).bitcast(U32).rearrange("p (b s k) -> p b s k", b=BLOCKS, s=SIDES)
        cand_s = take(BLOCKS * PICKS).rearrange("p (b n) -> p b n", b=BLOCKS)
        cand_i = take(BLOCKS * PICKS).bitcast(U32).rearrange("p (b n) -> p b n", b=BLOCKS)
        rest = take(BLOCKS * NKEYS).rearrange("p (b n) -> p b n", b=BLOCKS)
        cand = take(BLOCKS * TOPK * TOPK).rearrange("p (b n) -> p b n", b=BLOCKS)
        cand2 = take(BLOCKS * TOPK * TOPK).rearrange("p (b n) -> p b n", b=BLOCKS)
        assert t0 <= BLOCKS * D
        p0 = BLOCKS * D
        hot = S[:, p0:p0 + PICKS * TOPK]
        hot_v = S[:, p0 + PICKS * TOPK:p0 + 2 * PICKS * TOPK]
        p1 = p0 + 2 * PICKS * TOPK
        top_f = S[:, p1:p1 + SIDES * TOPK]
        sl_u = S[:, p1 + 256:p1 + 256 + PICKS].bitcast(U32)
        sl_f = S[:, p1 + 384:p1 + 384 + PICKS]
        e_1 = S[:, p1 + 512:p1 + 512 + PICKS]
        e_2 = S[:, p1 + 640:p1 + 640 + PICKS]
        g_e = S[:, p1 + 768:p1 + 768 + PICKS]
        g_s = S[:, p1 + 896:p1 + 896 + HEADS]
        g_r = S[:, p1 + 912:p1 + 912 + HEADS]
        assert p1 + 920 <= q0

        consts_in = sem("consts_in")
        x_loaded = sem("x_loaded")
        lora_loaded = sem("lora_loaded")
        ring_ready = [sem(f"ring_ready{i}") for i in range(RING)]
        ring_used = sem("ring_used")
        norm_act, norm_dve = sem("norm_act"), sem("norm_dve")
        turned = sem("turned")
        turned_out = sem("turned_out")
        lora_split = sem("lora_split")
        lora_mm, lora_act = sem("lora_mm"), sem("lora_act")
        tile_out = sem("tile_out")
        z_mm, z_act = sem("z_mm"), sem("z_act")
        exp_act = sem("exp_act")
        mix = sem("mix")
        sums_mm, sqrt_act = sem("sums_mm"), sem("sqrt_act")
        conv = sem("conv")
        pad_set, pad_saved = sem("pad_set"), sem("pad_saved")
        scan_mm, scan_act, scan_dve, scan_pool = sem("scan_mm"), sem("scan_act"), sem("scan_dve"), sem("scan_pool")
        mean_mm, var_mm, gate_mm = sem("mean_mm"), sem("var_mm"), sem("gate_mm")
        outn, outn_act = sem("outn"), sem("outn_act")
        wout_mm = sem("wout_mm")
        res_loaded = sem("res_loaded")
        norm2_act, norm2_dve = sem("norm2_act"), sem("norm2_dve")
        turned2, turned2_out = sem("turned2"), sem("turned2_out")
        score_mm, score_out = sem("score_mm"), sem("score_out")
        pick = sem("pick")
        pick_act = sem("pick_act")
        gathered = [sem(f"gathered{i}") for i in range(GATHERS)]
        row_used = sem("row_used")
        gelu, gelu_act = sem("gelu"), sem("gelu_act")
        fin_dve, fin_act = sem("fin_dve"), sem("fin_act")
        fin_gain = sem("fin_gain")
        stored = sem("stored")
        zeroed = sem("zeroed")

        NB8 = BLOCKS * 4
        TK_SIDE = 5 * BLOCKS
        TK_HEAD = 6 * BLOCKS
        TK_SPAN = SIDES * TK_SIDE + HEADS * TK_HEAD
        PICK_SPAN = TK_SPAN + BLOCKS * len(PICKED)
        ACT_TILES = 3 * PAIRS + CONVS + Q_TILES

        def picked(span, b, name):
            return span * PICK_SPAN + TK_SPAN + PICKED.after(b, name)

        def tile_taken(span, i):
            if i < 3 * PAIRS:
                return tile_out, span * ACT_TILES + i + 1
            if i < W_TILES:
                t, j = divmod(i - 3 * PAIRS, 3)
                if j == 0:
                    return tile_out, span * ACT_TILES + 3 * PAIRS + t + 1
                return conv, CONV.after(span * CONVS + t, "u" if j == 1 else "gate")
            return tile_out, span * ACT_TILES + 3 * PAIRS + CONVS + (i - W_TILES) + 1

        def side_after(span, side):
            return span * PICK_SPAN + (side + 1) * TK_SIDE + (side // 2) * TK_HEAD

        def scan_done(span, c, name, l=0):
            if name in BY_ACT:
                return scan_act, span * len(ACT_STEPS) + ACT_STEPS.index((c, name, l)) + 1
            extra = sum(1 for s in DVE_STEPS[:DVE_STEPS.index((c, name, l)) + 1] if s[1] in ("L", "dS"))
            total = len(DVE_STEPS) + sum(1 for s in DVE_STEPS if s[1] in ("L", "dS"))
            return scan_dve, span * total + DVE_STEPS.index((c, name, l)) + 1 + extra

        def pool_done(span, c, l):
            pair, q = divmod(c, 2)
            per_pair = 2 * (LEVELS + 1)
            n = span * (CHUNKS // 2) * per_pair + pair * per_pair
            return n + (2 * (q + 1) if l == 0 else 4 + 2 * (l - 1) + q + 1)

        def ring_item(span, i):
            m = span * RING_PER_SPAN + i
            return m, m % RING, 16 * (m // RING + 1)

        block = ctx.enter_context(nc.Block())

        @block.sync
        def _(sp):
            sp.dma_start(con[:, :], A["consts"]).then_inc(consts_in, 16)
            sp.dma_start(vec[:, :], A["vecs"]).then_inc(consts_in, 16)
            sp.dma_start(w2a2[:, :], A["w2a2"]).then_inc(consts_in, 16)

            for span in range(SPANS):
                rows = slice(span * SPAN, (span + 1) * SPAN)
                if span:
                    sp.wait_ge(pick, span * PICK_SPAN)
                    sp.wait_ge(pick_act, span * BLOCKS)
                xs = A["x"][rows, :].rearrange("(b p) d -> b p d", p=P)
                for b in range(BLOCKS):
                    sp.dma_start(x_in[:, b, :], xs[b]).then_inc(x_loaded, 16)
                sp.dma_start(lora_cur, A["lora_in"]).then_inc(lora_loaded, 16)
                for i in range(W_TILES):
                    m, slot, _ = ring_item(span, i)
                    if m >= RING:
                        sp.wait_ge(ring_used, m - RING + 1)
                    sp.dma_start(ring[:, slot, :], A["w_in"][i]).then_inc(ring_ready[slot], 16)
                m, slot, _ = ring_item(span, W_TILES)
                sp.wait_ge(ring_used, m - RING + 1)
                sp.dma_start(ring[:, slot, :], A["g2"]).then_inc(ring_ready[slot], 16)
                for k in range(KT):
                    m, slot, _ = ring_item(span, W_TILES + 1 + k)
                    sp.wait_ge(ring_used, m - RING + 1)
                    sp.dma_start(ring[:, slot, :], A["w_out"][k * P:(k + 1) * P, :]).then_inc(ring_ready[slot], 16)
                    if k == 0:
                        sp.wait_ge(outn, (span + 1) * PAIRS * len(OUTN))
                        for b in range(BLOCKS):
                            sp.dma_start(x_res[:, b, :], xs[b]).then_inc(res_loaded, 16)
                        sp.dma_start(gain_f, A["norm_ffn"].partition_broadcast(P)).then_inc(res_loaded, 16)
                        sp.dma_start(keys, A["keys"]).then_inc(res_loaded, 16)
                for i in range(Q_TILES):
                    m, slot, _ = ring_item(span, W_TILES + 1 + KT + i)
                    sp.wait_ge(ring_used, m - RING + 1)
                    sp.dma_start(ring[:, slot, :], A["wq"][i]).then_inc(ring_ready[slot], 16)
                sp.wait_ge(row_used, span * BLOCKS * 2 * PICKS + BLOCKS * PICKS)
                sp.dma_start(h2[:, 1, :], A["norm_final"].partition_broadcast(P)).then_inc(fin_gain, 16)
                for b in range(BLOCKS):
                    n = span * BLOCKS + b
                    sp.wait_ge(fin_dve, FIN.after(n, "out"))
                    sp.dma_start(A["out"][n * P:(n + 1) * P, :], acc[:, b, :]).then_inc(stored, 16)
            sp.wait_ge(stored, 16 * SPANS * BLOCKS)

        @block.tensor
        def _(pe):
            pe.wait_ge(consts_in, 48)

            def tile(span, i, item, rhs, n):
                _, slot, ready = ring_item(span, item)
                if i >= 4:
                    pe.wait_ge(*tile_taken(span, i - 4))
                pe.wait_ge(ring_ready[slot], ready)
                for k in range(KT):
                    mm = pe.matmul(banks[i % 4][:, 0:n], ring[:, slot, k * P:(k + 1) * P], rhs(k),
                                   start=(k == 0), stop=(k == KT - 1))
                mm.then_inc(ring_used, 1)

            def turn(src, sem_in, ready, done):
                for n in range(NB8):
                    b, k4 = divmod(n, 4)
                    if k4 == 0:
                        pe.wait_ge(sem_in, ready(b))
                    for j in range(4):
                        k = 4 * k4 + j
                        mm = pe.transpose(banks[n][:, j * P:(j + 1) * P], src[:, b, k * P:(k + 1) * P], ident)
                    mm.then_inc(done, 1)

            def pair_mm(bank, lhsT, rhs, terms=1):
                for h in range(PAIRS):
                    for q in range(2):
                        rows = slice(q * HALF, (q + 1) * HALF)
                        for i in range(terms):
                            mm = pe.matmul(bank[rows, h * CHUNK:(h + 1) * CHUNK], lhsT[i](h)[rows, :],
                                           rhs[i](h, q)[rows, :], start=(i == 0), stop=(i == terms - 1))
                return mm

            for span in range(SPANS):
                if span:
                    pe.wait_ge(*tile_taken(span - 1, W_TILES + Q_TILES - 1))
                    pe.wait_ge(score_out, span * SIDES)
                turn(x_in, norm_dve, lambda b: NORM1.after(span * BLOCKS + b, "scaled"), turned)

                pe.wait_ge(turned_out, NB8 * (span + 1))
                pe.wait_ge(lora_split, 4 * (span + 1))
                pe.wait_ge(pad_set, span + 1)
                for n, (c0, c1) in enumerate(((0, P), (P, 2 * P), (2 * P, LORA))):
                    out = banks[4 + n][0:c1 - c0, 0:SPAN]
                    for k in range(KT):
                        pe.matmul(out, lora_cur[:, k, c0:c1], hT_v[:, k, PAD:PAD + SPAN], start=(k == 0), stop=False)
                        mm = pe.matmul(out, lora_prev[:, k, c0:c1], hT_v[:, k, PAD - 1:PAD - 1 + SPAN],
                                       start=False, stop=(k == KT - 1))
                    mm.then_inc(lora_mm, 1)

                def sums(h):
                    n = span * PAIRS + h
                    pe.wait_ge(mix, MIX.after(n, "bonus_raw"))
                    if n >= 1:
                        pe.wait_ge(mix, MIX.after(n - 1, "bonus"))
                    pe.matmul(banks[5][:, 0:SPAN], c_("head_ones"), kk_sq, start=True, stop=True)
                    pe.matmul(banks[6][:, 0:SPAN], c_("head_ones"), rk, start=True, stop=True).then_inc(sums_mm, 1)

                pe.wait_ge(lora_act, 4 * (span + 1))
                for h in range(PAIRS):
                    n = span * PAIRS + h
                    zb = banks[4 if h % 2 else 7]
                    if h >= 2:
                        pe.wait_ge(z_act, 2 * (n - 1))
                    pe.matmul(zb[:, 0:SPAN], w2a2[0:HALF, h * P:(h + 1) * P], wa_in[0:HALF, :],
                              start=True, stop=True).then_inc(z_mm, 1)
                    pe.wait_ge(z_mm, 2 * n + 1)
                    pe.matmul(zb[:, SPAN:2 * SPAN], w2a2[HALF:P, h * P:(h + 1) * P], wa_in[HALF:P, :],
                              start=True, stop=True).then_inc(z_mm, 1)
                    for j in range(3):
                        tile(span, 3 * h + j, 3 * h + j, lambda k: hT_v[:, k, :], WID)
                        if j == 0 and h:
                            sums(h - 1)
                for t in range(CONVS):
                    for j in range(3):
                        i = 3 * PAIRS + 3 * t + j
                        tile(span, i, i, lambda k: hT_v[:, k, :], WID)
                        if t == 0 and j == 0:
                            sums(PAIRS - 1)

                pe.wait_ge(mix, MIX.after(span * PAIRS + PAIRS - 1, "bonus"))
                pe.wait_ge(conv, CONV.after(span * CONVS + CONVS - 1, "gate"))
                for i, (c, name, l) in enumerate(ORDER):
                    q = c % 2
                    n = span * CHUNKS + c
                    ts = slice(c * CHUNK, (c + 1) * CHUNK)
                    bank = banks[i % 8]
                    if i >= 8:
                        pe.wait_ge(*scan_done(span, *ORDER[i - 8]))

                    def cols(buf):
                        return lambda h, _=0: buf[:, h * CHUNK:(h + 1) * CHUNK]

                    def chn(buf):
                        return lambda h, _=0: buf[:, h, ts]

                    def eye(h, par):
                        return con[:, CON["ident"][0] + par * HALF:CON["ident"][0] + (par + 1) * HALF]

                    if name == "B_t":
                        mm = pair_mm(bank, [chn(B_c)], [eye])
                    elif name == "K_t":
                        mm = pair_mm(bank, [chn(K_c)], [eye])
                    elif name == "V_t":
                        mm = pair_mm(bank, [chn(yT)], [eye])
                    elif name == "L_T":
                        mm = pair_mm(bank, [chn(B_c)], [chn(A_c)])
                    elif name == "L":
                        mm = pair_mm(bank, [chn(A_c)], [chn(B_c)])
                    elif name == "LK_T":
                        mm = pair_mm(bank, [chn(K_c)], [chn(A_c)])
                    elif name == "RB_T":
                        mm = pair_mm(bank, [chn(B_c)], [chn(R_c)])
                    elif name == "RK_T":
                        mm = pair_mm(bank, [chn(K_c)], [chn(R_c)])
                    elif name == "W":
                        pe.wait_ge(scan_pool, pool_done(span, c, l))
                        pe.wait_ge(*scan_done(span, c, "X" if l > 1 else "L", l - 1 if l > 1 else 0))
                        mm = pair_mm(bank, [cols(M_b[q])], [cols(X[q])])
                    elif name == "X":
                        pe.wait_ge(*scan_done(span, c, "W", l))
                        if l > 1:
                            pe.wait_ge(*scan_done(span, c, "X_T", l - 1))
                        mm = pair_mm(bank, [cols(X_T[q])], [cols(W_b[q])])
                    elif name == "X_T":
                        pe.wait_ge(*scan_done(span, c, "W", l))
                        if l > 1:
                            pe.wait_ge(*scan_done(span, c, "X_T", l - 1))
                        mm = pair_mm(bank, [cols(W_b[q])], [cols(X_T[q])])
                    elif name == "rhs":
                        if c:
                            pe.wait_ge(*scan_done(span, c - 1, "dS"))
                        pe.wait_ge(*scan_done(span, c, "LK_T"))
                        pe.wait_ge(*scan_done(span, c, "V_t"))
                        mm = pair_mm(bank, [chn(A_c), cols(LK_T[q])], [cols(state[:, n % 2, :]), cols(V_t[q])], 2)
                    elif name == "SA":
                        pe.wait_ge(*scan_done(span, c, "rhs"))
                        pe.wait_ge(*scan_done(span, c, "X_T", LEVELS - 1))
                        mm = pair_mm(bank, [cols(X_T[q])], [cols(rhs_b)])
                    elif name == "Y":
                        pe.wait_ge(*scan_done(span, c, "SA"))
                        mm = pair_mm(bank, [cols(state[:, n % 2, :]), cols(SA_b), cols(V_t[q])],
                                     [chn(R_c), chn(B_c), chn(K_c)], 3)
                    elif name == "dS":
                        mm = pair_mm(bank, [cols(B_t[q]), cols(K_t[q])], [cols(SA_b), cols(V_t[q])], 2)
                    mm.then_inc(scan_mm, 1)

                _, g_slot, g_ready = ring_item(span, W_TILES)
                pe.wait_ge(ring_ready[g_slot], g_ready)
                pe.wait_ge(*scan_done(span, CHUNKS - 1, "Y"))
                pe.wait_ge(*scan_done(span, CHUNKS - 1, "dS"))

                def variance(h):
                    n = span * PAIRS + h
                    pe.wait_ge(outn_act, 2 * n + 1)
                    if h >= 2:
                        pe.wait_ge(outn_act, 2 * (n - 2) + 2)
                    pe.matmul(banks[2 + h % 2][:, 0:SPAN], c_("head_mean"), y_sq[h % 2],
                              start=True, stop=True).then_inc(var_mm, 1)

                for h in range(PAIRS):
                    n = span * PAIRS + h
                    if h >= 2:
                        pe.wait_ge(outn, OUTN.after(n - 2, "gated"))
                    pe.matmul(banks[h % 2][:, 0:SPAN], c_("head_mean"), yT[:, h, :],
                              start=True, stop=True).then_inc(mean_mm, 1)
                    if h:
                        variance(h - 1)
                    pe.matmul(banks[4 + h % 2][:, 0:SPAN], ring[:, g_slot, h * P:(h + 1) * P], g_in[:, 0, :],
                              start=True, stop=False)
                    mm = pe.matmul(banks[4 + h % 2][:, 0:SPAN], ring[0:32, g_slot, D_RWKV + h * P:D_RWKV + (h + 1) * P],
                                   g_in[0:32, 1, :], start=False, stop=True)
                    mm.then_inc(gate_mm, 1)
                variance(PAIRS - 1)
                pe.wait_ge(outn, (span + 1) * PAIRS * len(OUTN))
                pe.wait_ge(outn_act, 2 * (span + 1) * PAIRS)

                for k in range(KT):
                    _, slot, ready = ring_item(span, W_TILES + 1 + k)
                    pe.wait_ge(ring_ready[slot], ready)
                    for b in range(BLOCKS):
                        for n in range(4):
                            mm = pe.matmul(banks[4 * b + n][:, :], yT[:, k, b * P:(b + 1) * P],
                                           ring[:, slot, n * 512:(n + 1) * 512], start=(k == 0), stop=(k == KT - 1))
                            if k == 0 and b == 0 and n == 0:
                                mm.then_inc(ring_used, 1)
                    mm.then_inc(ring_used, 1)

                turn(h2, norm2_dve, lambda b: NORM2.after(span * BLOCKS + b, "scaled"), turned2)

                def scores(s):
                    n = span * SIDES + s
                    pe.wait_ge(*tile_taken(span, W_TILES + 2 * s + 1))
                    if s >= 2:
                        pe.wait_ge(score_out, n - 1)
                    for b in range(BLOCKS):
                        for j in range(2):
                            mm = pe.matmul(banks[4 + s % 2][:, b * P:(b + 1) * P], q_T[(2 * s + j) % 4][:, b * P:(b + 1) * P],
                                           keys[:, s, j, :], start=(j == 0), stop=(j == 1))
                    mm.then_inc(score_mm, 1)

                pe.wait_ge(turned2_out, NB8 * (span + 1))
                pe.wait_ge(res_loaded, 16 * 4 * (span + 1))
                for i in range(Q_TILES):
                    tile(span, W_TILES + i, W_TILES + 1 + KT + i, lambda k: hT_v[:, k, PAD:PAD + SPAN], SPAN)
                    if i % 2 == 0 and i:
                        scores(i // 2 - 1)
                scores(SIDES - 1)

        @block.scalar
        def _(act):
            act.wait_ge(consts_in, 48)
            for span in range(SPANS):
                for b in range(BLOCKS):
                    act.wait_ge(x_loaded, 16 * BLOCKS * (span + 1))
                    if span:
                        act.wait_ge(turned2_out, NB8 * span)
                    act.activation(yT[:, 8 * b:8 * b + 8, :], x_in[:, b, :].rearrange("p (k t) -> p k t", k=8),
                                   ACT.Square, accum_out=ssq[:, b:b + 1]).then_inc(norm_act, 1)
                for b in range(BLOCKS):
                    act.wait_ge(norm_dve, NORM1.after(span * BLOCKS + b, "mean_sq"))
                    act.activation(rstd[:, b:b + 1], ssq[:, 2 + b:3 + b], ACT.Sqrt).then_inc(norm_act, 1)
                act.wait_ge(lora_mm, 3 * span + 1)
                if span:
                    act.wait_ge(gate_mm, span * PAIRS)
                act.activation(wa_in[0:HALF, :], banks[4][0:HALF, 0:SPAN], ACT.Tanh).then_inc(lora_act, 1)
                act.activation(wa_in[HALF:P, :], banks[4][HALF:P, 0:SPAN], ACT.Copy).then_inc(lora_act, 1)
                act.wait_ge(lora_mm, 3 * span + 2)
                act.activation(g_in[:, 0, :], banks[5][:, 0:SPAN], ACT.Sigmoid).then_inc(lora_act, 1)
                act.wait_ge(lora_mm, 3 * span + 3)
                act.activation(g_in[0:32, 1, :], banks[6][0:32, 0:SPAN], ACT.Sigmoid).then_inc(lora_act, 1)
                for h in range(PAIRS):
                    n = span * PAIRS + h
                    zb = banks[4 if h % 2 else 7]
                    act.wait_ge(z_mm, 2 * n + 2)
                    if h:
                        act.wait_ge(mix, MIX.after(n - 1, "bonus"))
                    act.activation(sig_w, zb[:, 0:SPAN], ACT.Sigmoid, bias=v("w0", h)).then_inc(z_act, 1)
                    act.activation(sig_a, zb[:, SPAN:2 * SPAN], ACT.Sigmoid, bias=v("a0", h)).then_inc(z_act, 1)
                    for j in range(3):
                        act.wait_ge(ring_used, span * RING_PER_SPAN + 3 * h + j + 1)
                        act.activation(raw[h % 2][j], banks[(3 * h + j) % 4][:, 0:WID], ACT.Copy).then_inc(tile_out, 1)
                    act.wait_ge(mix, MIX.after(n, "log_prod"))
                    act.activation(e_p, lp, ACT.Exp).then_inc(exp_act, 1)
                    act.activation(e_n, lp, ACT.Exp, scale=-1.0).then_inc(exp_act, 1)
                    act.wait_ge(mix, MIX.after(n, "log_prev"))
                    act.activation(e_m, lm, ACT.Exp).then_inc(exp_act, 1)
                    act.wait_ge(sums_mm, n + 1)
                    act.activation(nrm, banks[5][:, 0:SPAN], ACT.Sqrt).then_inc(sqrt_act, 1)
                act.wait_ge(mix, MIX.after(span * PAIRS + PAIRS - 1, "bonus"))
                for t in range(CONVS):
                    if t:
                        act.wait_ge(conv, CONV.after(span * CONVS + t - 1, "u"))
                    act.wait_ge(ring_used, span * RING_PER_SPAN + 3 * PAIRS + 3 * t + 1)
                    act.activation(c_raw, banks[(3 * PAIRS + 3 * t) % 4][:, 0:WID], ACT.Copy).then_inc(tile_out, 1)
                for i, (c, name, l) in enumerate(ORDER):
                    if name not in BY_ACT:
                        continue
                    q = c % 2
                    act.wait_ge(scan_mm, span * len(ORDER) + i + 1)
                    src = banks[i % 8][:, :]
                    if name == "Y":
                        dst = yT[:, 0:PAIRS, c * CHUNK:(c + 1) * CHUNK]
                        src = src.rearrange("p (h t) -> p h t", h=PAIRS)
                    else:
                        dst = {"B_t": B_t[q], "K_t": K_t[q], "V_t": V_t[q], "W": W_b[q], "rhs": rhs_b, "SA": SA_b}[name]
                    if i < 4:
                        act.wait_ge(pad_saved, span + 1)
                    act.activation(dst, src, ACT.Copy).then_inc(scan_act, 1)
                for h in range(PAIRS):
                    n = span * PAIRS + h
                    act.wait_ge(outn, OUTN.after(n, "center"))
                    act.activation(y_sq[h % 2], y_c[h % 2], ACT.Square).then_inc(outn_act, 1)
                    act.wait_ge(var_mm, n + 1)
                    act.activation(y_sd[h % 2], banks[2 + h % 2][:, 0:SPAN], ACT.Sqrt, bias=v("eps", 1)).then_inc(outn_act, 1)
                for b in range(BLOCKS):
                    act.wait_ge(norm2_dve, NORM2.after(span * BLOCKS + b, "sum3"))
                    act.activation(h2[:, b, :], acc[:, b, :], ACT.Square, accum_out=ssq[:, b:b + 1]).then_inc(norm2_act, 1)
                    act.wait_ge(norm2_dve, NORM2.after(span * BLOCKS + b, "mean_sq"))
                    act.activation(rstd[:, b:b + 1], ssq[:, 2 + b:3 + b], ACT.Sqrt).then_inc(norm2_act, 1)
                for n in range(NB8):
                    b, k4 = divmod(n, 4)
                    act.wait_ge(turned2, span * NB8 + n + 1)
                    act.activation(hT_v[:, 4 * k4:4 * k4 + 4, PAD + b * P:PAD + (b + 1) * P],
                                   banks[n][:, :].rearrange("p (k t) -> p k t", k=4), ACT.Copy).then_inc(turned2_out, 1)
                def score_copy(s):
                    n = span * SIDES + s
                    act.wait_ge(score_mm, n + 1)
                    if s >= 2:
                        act.wait_ge(pick, side_after(span, s - 2))
                    act.activation(sc[s % 2], banks[4 + s % 2][:, 0:SPAN].rearrange("p (b n) -> p b n", b=BLOCKS),
                                   ACT.Copy).then_inc(score_out, 1)

                for i in range(Q_TILES):
                    act.wait_ge(ring_used, span * RING_PER_SPAN + W_TILES + 1 + KT + i + 1)
                    if i >= 4:
                        act.wait_ge(score_mm, span * SIDES + (i - 4) // 2 + 1)
                    act.activation(q_T[i % 4], banks[i % 4][:, 0:SPAN], ACT.Copy).then_inc(tile_out, 1)
                    if i % 2 == 0 and i:
                        score_copy(i // 2 - 1)
                score_copy(SIDES - 1)
                for b in range(BLOCKS):
                    act.wait_ge(pick, picked(span, b, "shifted"))
                    act.activation(g_e, g_e, ACT.Exp).then_inc(pick_act, 1)
                for b in range(BLOCKS):
                    n = span * BLOCKS + b
                    act.wait_ge(gelu, GELU.after(n, "inner"))
                    act.activation(gel[:, 0, :], gel[:, 0, :], ACT.Tanh, scale=GELU_S).then_inc(gelu_act, 1)
                for b in range(BLOCKS):
                    n = span * BLOCKS + b
                    act.wait_ge(row_used, span * BLOCKS * 2 * PICKS + (BLOCKS + b + 1) * PICKS)
                    if b:
                        act.wait_ge(fin_act, 2 * n)
                    act.activation(h2[:, 0, :], acc[:, b, :], ACT.Square, accum_out=ssq[:, 4 + b:5 + b]).then_inc(fin_act, 1)
                    act.wait_ge(fin_dve, FIN.after(n, "mean_sq"))
                    act.activation(rstd[:, 4 + b:5 + b], ssq[:, 6 + b:7 + b], ACT.Sqrt).then_inc(fin_act, 1)

        @block.vector
        def _(dve):
            def chain(signal, start):
                n = [start]

                def step(ins):
                    n[0] += 1
                    ins.then_inc(signal, 1)
                    dve.wait_ge(signal, n[0])
                step.count = n
                return step

            dve.wait_ge(consts_in, 48)
            dve.memset(state[:, 0, :], 0.0).then_inc(zeroed, 1)
            dve.memset(h_pad[:, :, :], 0.0).then_inc(zeroed, 1)
            dve.wait_ge(zeroed, 2)
            for span in range(SPANS):
                step = chain(lora_split, 4 * span)
                dve.wait_ge(lora_loaded, 16 * (span + 1))
                for j, (c0, c1) in enumerate(((0, 64), (64, 128), (128, LORA))):
                    mu = v("mu_lora", j * KT, KT).unsqueeze(2).to_broadcast([P, KT, c1 - c0])
                    step(dve.tensor_tensor(lora_prev[:, :, c0:c1], lora_cur[:, :, c0:c1], mu, ALU.mult))
                step(dve.tensor_tensor(lora_cur, lora_cur, lora_prev, ALU.subtract))
                if span:
                    dve.wait_ge(ring_used, span * RING_PER_SPAN)
                dve.tensor_copy(hT_v[:, :, 0:PAD], h_pad[:, :, :]).then_inc(pad_set, 1)
                step = chain(norm_dve, span * BLOCKS * len(NORM1))
                for b in range(BLOCKS):
                    n = span * 2 * BLOCKS
                    dve.wait_ge(norm_act, n + b + 1)
                    step(dve.tensor_scalar(ssq[:, 2 + b:3 + b], ssq[:, b:b + 1], 1.0 / D, RMS_EPS, ALU.mult, ALU.add))
                    dve.wait_ge(norm_act, n + BLOCKS + b + 1)
                    step(dve.reciprocal(rstd[:, 2 + b:3 + b], rstd[:, b:b + 1]))
                    step(dve.tensor_scalar(x_in[:, b, :], x_in[:, b, :], rstd[:, 2 + b:3 + b], None, ALU.mult))
                for n in range(NB8):
                    b, k4 = divmod(n, 4)
                    dve.wait_ge(turned, span * NB8 + n + 1)
                    gain = v("norm_mix", 4 * k4, 4).unsqueeze(2).to_broadcast([P, 4, P])
                    dve.tensor_tensor(hT_v[:, 4 * k4:4 * k4 + 4, PAD + b * P:PAD + (b + 1) * P],
                                      banks[n][:, :].rearrange("p (k t) -> p k t", k=4), gain, ALU.mult)\
                       .then_inc(turned_out, 1)
                step = chain(mix, span * PAIRS * len(MIX))
                for h in range(PAIRS):
                    n = span * PAIRS + h
                    if h == 0:
                        dve.wait_ge(lora_mm, 3 * (span + 1))
                    dve.wait_ge(z_act, 2 * n + 1)
                    step(dve.tensor_scalar(lw, sig_w, -EXP_M_HALF, None, ALU.mult))
                    step(dve.tensor_tensor_scan(lp, c_("keep"), lw, 0.0, ALU.mult, ALU.add))
                    step(dve.tensor_tensor(lm, lp, lw, ALU.subtract))
                    outs = (r_s, k_s, yT[:, h, :])
                    for j in range(3):
                        src = raw[h % 2][j]
                        dve.wait_ge(*tile_taken(span, 3 * h + j))
                        step(dve.tensor_tensor(diff, src[:, PAD - 1:PAD - 1 + SPAN], src[:, PAD:PAD + SPAN], ALU.subtract))
                        step(dve.scalar_tensor_tensor(out=outs[j], in0=diff, scalar=v("mu_rkv", j * PAIRS + h),
                                                      in1=src[:, PAD:PAD + SPAN], op0=ALU.mult, op1=ALU.add))
                    step(dve.tensor_scalar(kk_raw, k_s, v("k_k", h), None, ALU.mult))
                    step(dve.tensor_tensor(kk_sq, kk_raw, kk_raw, ALU.mult))
                    dve.wait_ge(z_act, 2 * n + 2)
                    step(dve.tensor_scalar(a_gain, sig_a, 1.0, v("k_a", h), ALU.subtract, ALU.mult))
                    step(dve.scalar_tensor_tensor(out=k_new, in0=a_gain, scalar=1.0, in1=k_s, op0=ALU.add, op1=ALU.mult))
                    step(dve.scalar_tensor_tensor(out=rk, in0=r_s, scalar=v("r_k", h), in1=k_new, op0=ALU.mult, op1=ALU.mult))
                    dve.wait_ge(exp_act, 3 * n + 3)
                    step(dve.tensor_tensor(R_c[:, h, :], r_s, e_p, ALU.mult))
                    step(dve.tensor_tensor(K_c[:, h, :], k_new, e_n, ALU.mult))
                    step(dve.tensor_copy(p_end[:, h, :], e_p[:, CHUNK - 1:SPAN:CHUNK]))
                    dve.wait_ge(sqrt_act, n + 1)
                    step(dve.tensor_scalar(nrm, nrm, 1e-12, None, ALU.max))
                    step(dve.reciprocal(nrm, nrm))
                    step(dve.tensor_tensor(kk, kk_raw, nrm, ALU.mult))
                    step(dve.tensor_tensor(kk_sq, kk, sig_a, ALU.mult))
                    step(dve.tensor_tensor(B_c[:, h, :], kk_sq, e_n, ALU.mult))
                    step(dve.scalar_tensor_tensor(out=A_c[:, h, :], in0=kk, scalar=-1.0, in1=e_m, op0=ALU.mult, op1=ALU.mult))
                    dve.wait_ge(sums_mm, n + 1)
                    step(dve.tensor_tensor(bonus[:, h, :], banks[6][:, 0:SPAN], yT[:, h, :], ALU.mult))
                assert step.count[0] == (span + 1) * PAIRS * len(MIX)
                step = chain(conv, span * CONVS * len(CONV))
                for t in range(CONVS):
                    n = span * CONVS + t
                    i = 3 * PAIRS + 3 * t
                    bx, bb = (i + 1) % 4, (i + 2) % 4
                    dve.wait_ge(*tile_taken(span, i))
                    dve.wait_ge(ring_used, span * RING_PER_SPAN + 3 * PAIRS + 3 * t + 2)
                    step(dve.tensor_tensor(u_c, banks[bx][:, 0:WID], c_raw, ALU.mult))
                    step(dve.tensor_scalar(conv_o[0], u_c[:, 0:SPAN], v("conv_w", t), None, ALU.mult))
                    step(dve.scalar_tensor_tensor(out=conv_o[1], in0=u_c[:, 1:1 + SPAN], scalar=v("conv_w", CONVS + t),
                                                  in1=conv_o[0], op0=ALU.mult, op1=ALU.add))
                    step(dve.scalar_tensor_tensor(out=conv_o[2], in0=u_c[:, 2:2 + SPAN], scalar=v("conv_w", 2 * CONVS + t),
                                                  in1=conv_o[1], op0=ALU.mult, op1=ALU.add))
                    dve.wait_ge(ring_used, span * RING_PER_SPAN + 3 * PAIRS + 3 * t + 3)
                    step(dve.tensor_tensor(yT[:, PAIRS + t, :], banks[bb][:, PAD:PAD + SPAN], conv_o[2], ALU.mult))
                dve.tensor_copy(h_pad[:, :, :], hT_v[:, :, SPAN:SPAN + PAD]).then_inc(pad_saved, 1)
                dve.wait_ge(pad_saved, span + 1)
                total = len(DVE_STEPS) + sum(1 for s in DVE_STEPS if s[1] in ("L", "dS"))
                step = chain(scan_dve, span * total)
                wide_mask = lambda name: c_(name).unsqueeze(1).to_broadcast([P, PAIRS, CHUNK])
                r3 = lambda ap: ap.rearrange("p (h t) -> p h t", h=PAIRS)
                for i, (c, name, l) in enumerate(ORDER):
                    if name in BY_ACT:
                        continue
                    q, n = c % 2, span * CHUNKS + c
                    ts = slice(c * CHUNK, (c + 1) * CHUNK)
                    dve.wait_ge(scan_mm, span * len(ORDER) + i + 1)
                    src = banks[i % 8][:, :]
                    if name == "L_T":
                        if c >= 2:
                            dve.wait_ge(scan_pool, pool_done(span, c - 2, LEVELS - 1))
                        step(dve.tensor_tensor(r3(L_T[q]), r3(src), wide_mask("before"), ALU.mult))
                    elif name == "L":
                        step(dve.tensor_tensor(r3(X[q]), r3(src), wide_mask("low0"), ALU.mult))
                        step(dve.tensor_tensor(r3(X[q]), r3(X[q]), wide_mask("eye"), ALU.add))
                    elif name == "LK_T":
                        step(dve.tensor_tensor(r3(LK_T[q]), r3(src), wide_mask("before"), ALU.mult))
                    elif name == "RB_T":
                        step(dve.tensor_tensor(B_c[:, :, ts], r3(src), wide_mask("upto"), ALU.mult))
                    elif name == "RK_T":
                        step(dve.tensor_tensor(K_c[:, :, ts], r3(src), wide_mask("upto"), ALU.mult))
                    elif name == "X":
                        step(dve.tensor_tensor(X[q], src, X[q], ALU.add))
                    elif name == "X_T":
                        if l == 1:
                            dve.wait_ge(scan_pool, pool_done(span, c, 0))
                        step(dve.tensor_tensor(X_T[q], src, X_T[q], ALU.add))
                    elif name == "dS":
                        end = p_end[:, :, c:c + 1].to_broadcast([P, PAIRS, CHUNK])
                        step(dve.tensor_tensor(sum_b, src, state[:, n % 2, :], ALU.add))
                        step(dve.tensor_tensor(r3(state[:, (n + 1) % 2, :]), r3(sum_b), end, ALU.mult))
                assert step.count[0] == (span + 1) * total
                step = chain(outn, span * PAIRS * len(OUTN))
                for h in range(PAIRS):
                    n = span * PAIRS + h
                    dve.wait_ge(mean_mm, n + 1)
                    step(dve.tensor_tensor(y_c[h % 2], yT[:, h, :], banks[h % 2][:, 0:SPAN], ALU.subtract))
                    dve.wait_ge(outn_act, 2 * n + 2)
                    step(dve.reciprocal(y_t[0], y_sd[h % 2]))
                    step(dve.tensor_tensor(y_t[1], y_c[h % 2], y_t[0], ALU.mult))
                    step(dve.tensor_scalar(y_t[2], y_t[1], v("gn_w", h), v("gn_b", h), ALU.mult, ALU.add))
                    step(dve.tensor_tensor(y_t[3], y_t[2], bonus[:, h, :], ALU.add))
                    dve.wait_ge(gate_mm, n + 1)
                    step(dve.tensor_tensor(yT[:, h, :], y_t[3], banks[4 + h % 2][:, 0:SPAN], ALU.mult))
                if span:
                    dve.wait_ge(stored, 16 * BLOCKS * span)
                step = chain(norm2_dve, span * BLOCKS * len(NORM2))
                dve.wait_ge(res_loaded, 16 * 4 * (span + 1))
                dve.wait_ge(ring_used, span * RING_PER_SPAN + W_TILES + 1 + KT)
                for b in range(BLOCKS):
                    for n in range(4):
                        cs = slice(n * 512, (n + 1) * 512)
                        step(dve.tensor_tensor(acc[:, b, cs], banks[4 * b + n][:, :], x_res[:, b, cs], ALU.add))
                    n = span * 2 * BLOCKS + 2 * b
                    dve.wait_ge(norm2_act, n + 1)
                    step(dve.tensor_scalar(ssq[:, 2 + b:3 + b], ssq[:, b:b + 1], 1.0 / D, RMS_EPS, ALU.mult, ALU.add))
                    dve.wait_ge(norm2_act, n + 2)
                    step(dve.reciprocal(rstd[:, 2 + b:3 + b], rstd[:, b:b + 1]))
                    step(dve.scalar_tensor_tensor(out=h2[:, b, :], in0=acc[:, b, :], scalar=rstd[:, 2 + b:3 + b],
                                                  in1=gain_f, op0=ALU.mult, op1=ALU.mult))
                step = chain(pick, span * PICK_SPAN)
                eights = (slice(0, 8), slice(8, 16))
                for s in range(SIDES):
                    dve.wait_ge(score_out, span * SIDES + s + 1)
                    src = sc[s % 2]
                    for b in range(BLOCKS):
                        step(dve.max(top_s[:, b, s, 0:8], src[:, b, :]))
                    for b in range(BLOCKS):
                        step(dve.match_replace(rest[:, b, :], top_s[:, b, s, 0:8], src[:, b, :], FAR))
                    for b in range(BLOCKS):
                        step(dve.max(top_s[:, b, s, 8:16], rest[:, b, :]))
                    for b in range(BLOCKS):
                        step(dve.max_index(top_i[:, b, s, 0:8], top_s[:, b, s, 0:8], src[:, b, :]))
                    for b in range(BLOCKS):
                        step(dve.max_index(top_i[:, b, s, 8:16], top_s[:, b, s, 8:16], rest[:, b, :]))
                    if s % 2 == 0:
                        continue
                    hs = slice((s // 2) * TOPK, (s // 2) * TOPK + 8), slice((s // 2) * TOPK + 8, (s // 2 + 1) * TOPK)
                    for b in range(BLOCKS):
                        first = top_s[:, b, s - 1, :].unsqueeze(2).to_broadcast([P, TOPK, TOPK])
                        second = top_s[:, b, s, :].unsqueeze(1).to_broadcast([P, TOPK, TOPK])
                        step(dve.tensor_tensor(cand[:, b, :].rearrange("p (i j) -> p i j", i=TOPK), first, second, ALU.add))
                    for b in range(BLOCKS):
                        step(dve.max(cand_s[:, b, hs[0]], cand[:, b, :]))
                    for b in range(BLOCKS):
                        step(dve.match_replace(cand2[:, b, :], cand_s[:, b, hs[0]], cand[:, b, :], FAR))
                    for b in range(BLOCKS):
                        step(dve.max(cand_s[:, b, hs[1]], cand2[:, b, :]))
                    for b in range(BLOCKS):
                        step(dve.max_index(cand_i[:, b, hs[0]], cand_s[:, b, hs[0]], cand[:, b, :]))
                    for b in range(BLOCKS):
                        step(dve.max_index(cand_i[:, b, hs[1]], cand_s[:, b, hs[1]], cand2[:, b, :]))
                dve.wait_ge(score_mm, span * SIDES + SIDES)
                kview = lambda ap: ap.rearrange("p (h k) -> p h k", h=HEADS)
                for b in range(BLOCKS):
                    top = cand_s[:, b, 0:PICKS:TOPK].unsqueeze(2).to_broadcast([P, HEADS, TOPK])
                    step(dve.tensor_tensor(kview(g_e), kview(cand_s[:, b, :]), top, ALU.subtract))
                    step(dve.tensor_copy(top_f, top_i[:, b, :, :].rearrange("p s k -> p (s k)")))
                    for half, dst in ((0, e_1), (1, e_2)):
                        if half == 0:
                            step(dve.tensor_scalar(sl_u, cand_i[:, b, :], 4, None, ALU.logical_shift_right))
                        else:
                            step(dve.tensor_scalar(sl_u, cand_i[:, b, :], TOPK - 1, None, ALU.bitwise_and))
                        step(dve.tensor_copy(sl_f, sl_u))
                        step(dve.tensor_tensor(hot.rearrange("p (n j) -> p n j", j=TOPK),
                                               sl_f.unsqueeze(2).to_broadcast([P, PICKS, TOPK]),
                                               c_("iota16").unsqueeze(1).to_broadcast([P, PICKS, TOPK]), ALU.is_equal))
                        part = top_f.rearrange("p (h c j) -> p h c j", h=HEADS, c=2)[:, :, half, :]\
                            .unsqueeze(2).to_broadcast([P, HEADS, TOPK, TOPK])
                        step(dve.tensor_tensor(hot_v.rearrange("p (h k j) -> p h k j", h=HEADS, k=TOPK),
                                               hot.rearrange("p (h k j) -> p h k j", h=HEADS, k=TOPK), part, ALU.mult))
                        step(dve.tensor_reduce(dst, hot_v.rearrange("p (n j) -> p n j", j=TOPK), AX_X, ALU.add))
                    step(dve.scalar_tensor_tensor(out=pick_i[:, b, :], in0=e_1, scalar=float(NKEYS), in1=e_2,
                                                  op0=ALU.mult, op1=ALU.add))
                    dve.wait_ge(pick_act, span * BLOCKS + b + 1)
                    step(dve.tensor_reduce(g_s, kview(g_e), AX_X, ALU.add))
                    step(dve.reciprocal(g_r, g_s))
                    step(dve.tensor_tensor(kview(gates[:, b, :]), kview(g_e),
                                           g_r.unsqueeze(2).to_broadcast([P, HEADS, TOPK]), ALU.mult))
                assert step.count[0] == (span + 1) * PICK_SPAN
                rows = span * BLOCKS * 2 * PICKS
                for b in range(BLOCKS):
                    for k in range(PICKS):
                        slot, n = rows % GATHERS, rows // GATHERS
                        dve.wait_ge(gathered[slot], 16 * (n + 1))
                        dve.tensor_tensor_reduce(gath[:, slot, :], gath[:, slot, :], h2[:, b, :], 1.0, 0.0,
                                                 ALU.mult, ALU.add, dots[:, b, k:k + 1]).then_inc(row_used, 1)
                        rows += 1
                for b in range(BLOCKS):
                    n = span * BLOCKS + b
                    step = chain(gelu, n * len(GELU))
                    if b == 0:
                        dve.wait_ge(row_used, rows)
                    x, g0, g1 = dots[:, b, :], gel[:, 0, :], gel[:, 1, :]
                    step(dve.tensor_tensor(g0, x, x, ALU.mult))
                    step(dve.tensor_tensor(g1, g0, x, ALU.mult))
                    step(dve.scalar_tensor_tensor(out=g0, in0=g1, scalar=GELU_C, in1=x, op0=ALU.mult, op1=ALU.add))
                    dve.wait_ge(gelu_act, n + 1)
                    step(dve.scalar_tensor_tensor(out=g1, in0=g0, scalar=1.0, in1=x, op0=ALU.add, op1=ALU.mult))
                    step(dve.scalar_tensor_tensor(out=gates[:, b, :], in0=g1, scalar=0.5, in1=gates[:, b, :],
                                                  op0=ALU.mult, op1=ALU.mult))
                for b in range(BLOCKS):
                    n = span * BLOCKS + b
                    for k in range(PICKS):
                        slot, m = rows % GATHERS, rows // GATHERS
                        dve.wait_ge(gathered[slot], 16 * (m + 1))
                        dve.wait_ge(row_used, rows)
                        dve.scalar_tensor_tensor(out=acc[:, b, :], in0=gath[:, slot, :], scalar=gates[:, b, k:k + 1],
                                                 in1=acc[:, b, :], op0=ALU.mult, op1=ALU.add).then_inc(row_used, 1)
                        rows += 1
                    step = chain(fin_dve, n * len(FIN))
                    dve.wait_ge(fin_act, 2 * n + 1)
                    step(dve.tensor_scalar(ssq[:, 6 + b:7 + b], ssq[:, 4 + b:5 + b], 1.0 / D, RMS_EPS, ALU.mult, ALU.add))
                    dve.wait_ge(fin_act, 2 * n + 2)
                    step(dve.reciprocal(rstd[:, 6 + b:7 + b], rstd[:, 4 + b:5 + b]))
                    dve.wait_ge(fin_gain, 16 * (span + 1))
                    step(dve.scalar_tensor_tensor(out=acc[:, b, :], in0=acc[:, b, :], scalar=rstd[:, 6 + b:7 + b],
                                                  in1=h2[:, 1, :], op0=ALU.mult, op1=ALU.mult))

        @block.gpsimd
        def _(pool):
            pool.wait_ge(consts_in, 48)
            n_pool = 0
            for span in range(SPANS):
                r3 = lambda ap: ap.rearrange("p (h t) -> p h t", h=PAIRS)
                for pair in range(CHUNKS // 2):
                    for l in range(LEVELS):
                        for q in range(2):
                            c = 2 * pair + q
                            mask = c_("up", l * CHUNK, CHUNK).unsqueeze(1).to_broadcast([P, PAIRS, CHUNK])
                            if l == 0:
                                pool.wait_ge(*scan_done(span, c, "L_T"))
                            elif l > 1:
                                pool.wait_ge(scan_mm, span * len(ORDER) + ORDER.index((c, "W", l - 1)) + 1)
                            if n_pool:
                                pool.wait_ge(scan_pool, n_pool)
                            pool.tensor_tensor(r3(M_b[q]), r3(L_T[q]), mask, ALU.mult).then_inc(scan_pool, 1)
                            n_pool += 1
                            if l == 0:
                                eye = c_("eye").unsqueeze(1).to_broadcast([P, PAIRS, CHUNK])
                                pool.wait_ge(scan_pool, n_pool)
                                pool.tensor_tensor(r3(X_T[q]), r3(M_b[q]), eye, ALU.add).then_inc(scan_pool, 1)
                                n_pool += 1
                rows = span * BLOCKS * 2 * PICKS
                for table in ("peer_u", "peer_v"):
                    for b in range(BLOCKS):
                        if table == "peer_u":
                            pool.wait_ge(pick, picked(span, b, "expert"))
                        for k in range(PICKS):
                            slot = rows % GATHERS
                            if rows >= GATHERS:
                                pool.wait_ge(row_used, rows - GATHERS + 1)
                            pool.indirect_dma_start(gath[:, slot, :], None, A[table],
                                                    bass.IndirectOffsetOnAxis(ap=pick_i[:, b, k:k + 1], axis=0))\
                                .then_inc(gathered[slot], 16)
                            rows += 1


def _layouts(inp):
    import numpy as np

    f = np.float32

    def col(a, n):
        return np.asarray(a, f).reshape(n, P).T

    def tiles(w, cols):
        w = np.asarray(w, f).reshape(KT, P, -1, P)[:, :, cols, :]
        return np.ascontiguousarray(w.transpose(2, 1, 0, 3)).reshape(len(cols), P, D)

    order = [g * PAIRS + h for h in range(PAIRS) for g in range(3)]
    order += [3 * PAIRS + g * CONVS + t for t in range(CONVS) for g in (1, 2, 0)]
    vecs = {"norm_mix": col(inp["norm_mix"], KT), "mu_rkv": col(inp["mu_rkv"], 3 * PAIRS), "w0": col(inp["w0"], PAIRS),
            "a0": col(inp["a0"], PAIRS), "k_k": col(inp["k_k"], PAIRS), "k_a": col(inp["k_a"], PAIRS),
            "r_k": col(inp["r_k"], PAIRS), "gn_w": col(inp["gn_w"], PAIRS), "gn_b": col(inp["gn_b"], PAIRS),
            "conv_w": col(inp["conv_w"], 3 * CONVS), "mu_lora": col(inp["mu_lora"], 3 * KT),
            "eps": np.tile(np.array([[RMS_EPS, GN_EPS]], f), (P, 1))}
    lora = np.concatenate([np.asarray(inp[n], f)[0] for n in ("w1", "a1", "g1")], axis=1)
    g2 = np.asarray(inp["g2"], f)[0]
    g2p = np.zeros((P, D), f)
    g2p[:, :D_RWKV] = g2[:P]
    g2p[:LORA_G - P, D_RWKV:] = g2[P:]
    keys = np.asarray(inp["peer_keys"], f)[0].reshape(SIDES, NKEYS, 2, P).transpose(3, 0, 2, 1)

    i = np.arange(CHUNK)
    s_, t_ = np.meshgrid(i, i, indexing="ij")

    def low(l):
        return ((s_ >> (l + 1) == t_ >> (l + 1)) & (s_ >> l & 1 == 1) & (t_ >> l & 1 == 0)).astype(f)

    two = lambda m: np.tile(m.astype(f), (2, 1))
    head = np.kron(np.eye(2), np.ones((HALF, HALF)))
    cons = {"ident": np.eye(P), "head_ones": head, "head_mean": head / HALF, "eye": two(np.eye(CHUNK)),
            "before": two(s_ < t_), "upto": two(s_ <= t_), "low0": two(low(0)),
            "up": np.concatenate([two(low(l).T) for l in range(LEVELS)], axis=1),
            "keep": np.tile((np.arange(SPAN) % CHUNK != 0)[None], (P, 1)), "iota16": np.tile(np.arange(TOPK)[None], (P, 1))}
    return {
        "x": np.asarray(inp["x"], f).reshape(T, D),
        "vecs": np.ascontiguousarray(np.concatenate([vecs[n] for n in VEC], axis=1)),
        "consts": np.ascontiguousarray(np.concatenate([cons[n].astype(f) for n in CON], axis=1)),
        "w_in": tiles(np.asarray(inp["w_in"])[0], order),
        "lora_in": np.ascontiguousarray(lora.reshape(KT, P, LORA).transpose(1, 0, 2)),
        "w2a2": np.ascontiguousarray(np.concatenate([np.asarray(inp["w2"], f)[0], np.asarray(inp["a2"], f)[0]])),
        "g2": g2p,
        "w_out": np.asarray(inp["w_out"], f)[0],
        "norm_ffn": np.asarray(inp["norm_ffn"], f).reshape(D),
        "wq": tiles(np.asarray(inp["peer_wq"])[0], list(range(Q_TILES))),
        "keys": np.ascontiguousarray(keys),
        "peer_u": np.asarray(inp["peer_u"], f)[0],
        "peer_v": np.asarray(inp["peer_v"], f)[0],
        "norm_final": np.asarray(inp["norm_final"], f).reshape(D),
    }


def kernel(**inputs):
    import concourse.bacc as bacc
    from concourse.bass_utils import run_bass_kernel_spmd

    arrays = _layouts(inputs)
    nc = bacc.Bacc("TRN2", target_bir_lowering=False, num_devices=1)
    A = {n: nc.dram_tensor("in_" + n, a.shape, F32, kind="ExternalInput").ap() for n, a in arrays.items()}
    A["out"] = nc.dram_tensor("out", (T, D), F32, kind="ExternalOutput").ap()
    hymba(nc, A)
    r = run_bass_kernel_spmd(nc, [{"in_" + n: a for n, a in arrays.items()}], core_ids=[0])
    return r.results[0]["out"].reshape(1, T, D)
```

```python
from contextlib import ExitStack

import concourse.bass as bass
from concourse import mybir

F32 = mybir.dt.float32
I32 = mybir.dt.int32
U32 = mybir.dt.uint32
ALU = mybir.AluOpType
ACT = mybir.ActivationFunctionType
AX_X = mybir.AxisListType.X

P = 128
T, D = 512, 2048
SPAN = 256
SPANS = T // SPAN
BLOCKS = SPAN // P
KT = D // P
CHUNK = 64
CHUNKS = SPAN // CHUNK
HALF = 64
D_RWKV = D // 2
PAIRS = D_RWKV // P
CONVS = D_RWKV // P
LEVELS = 6
W_TILES = 6 * PAIRS
LORA_W, LORA_A, LORA_G = 64, 64, 160
LORA = LORA_W + LORA_A + LORA_G
HEADS, HALVES, NKEYS, TOPK = 8, 2, 128, 16
SIDES = HEADS * HALVES
Q_TILES = 2 * SIDES
PICKS = HEADS * TOPK
RMS_EPS, GN_EPS = 1e-6, 64e-5
EXP_M_HALF = 0.6065306597126334
FAR = -3.0e38
GELU_C, GELU_S = 0.044715, 0.7978845608028654
PAD = 2

VEC = {}
for _name, _n in (("norm_mix", KT), ("mu_rkv", 3 * PAIRS), ("w0", PAIRS), ("a0", PAIRS), ("k_k", PAIRS),
                  ("k_a", PAIRS), ("r_k", PAIRS), ("gn_w", PAIRS), ("gn_b", PAIRS), ("conv_w", 3 * CONVS),
                  ("mu_lora", 3 * KT), ("eps", 2)):
    VEC[_name] = (sum(n for _, n in VEC.values()), _n)
N_VEC = sum(n for _, n in VEC.values())
CON = {}
for _name, _n in (("ident", P), ("head_ones", P), ("head_mean", P), ("eye", CHUNK), ("before", CHUNK),
                  ("upto", CHUNK), ("low0", CHUNK), ("up", LEVELS * CHUNK), ("keep", SPAN), ("iota16", TOPK)):
    CON[_name] = (sum(n for _, n in CON.values()), _n)
N_CON = sum(n for _, n in CON.values())

RING = 3
RING_PER_SPAN = W_TILES + 1 + KT + Q_TILES
GATHERS = 4
ROWS_SPAN = BLOCKS * 2 * PICKS
ROWS = {"lora": 8, "turn": 8, "head": 10, "conv": 9, "scan": 88, "outn": 4, "w_out": 40, "side": 11, "norm2": 8}
assert ROWS["lora"] + ROWS["turn"] + PAIRS * ROWS["head"] + CONVS * ROWS["conv"] + ROWS["scan"] == ROWS_SPAN // 2
assert PAIRS * ROWS["outn"] + ROWS["w_out"] + ROWS["norm2"] + SIDES * ROWS["side"] == ROWS_SPAN // 2


class Steps:

    def __init__(self, *names):
        self.names = list(names)

    def __len__(self):
        return len(self.names)

    def after(self, n, name):
        return n * len(self.names) + self.names.index(name) + 1


MIX = Steps("log_decay", "log_prod", "log_prev", "r_step", "r", "k_step", "k", "v_step", "v", "kk_raw", "kk_sq",
            "a_gain", "k_new", "bonus_raw", "R", "K", "p_end", "norm", "inv_norm", "kk", "B", "B_scaled", "A",
            "bonus")
CONV = Steps("u", "tap0", "tap1", "tap2", "gate")
OUTN = Steps("center", "inv", "scaled", "affine", "plus_bonus", "gated")
NORM1 = Steps("mean_sq", "inv", "scaled")
NORM2 = Steps("sum0", "sum1", "sum2", "sum3", "mean_sq", "inv", "scaled")
PICKED = Steps("shifted", "expert_parts", "row", "row_f", "row_hot", "row_part", "row_expert", "col", "col_f", "col_hot",
               "col_part", "col_expert", "expert", "gate_sum", "gate_inv", "gates")
GELU = Steps("square", "cube", "inner", "half", "coef")
FIN = Steps("mean_sq", "inv", "out")


def scan_order():
    order = []
    for pair in range(CHUNKS // 2):
        both = (2 * pair, 2 * pair + 1)
        for name in ("B_t", "K_t", "V_t", "L_T", "L", "LK_T", "RB_T", "RK_T"):
            order += [(c, name, 0) for c in both]
        for l in range(1, LEVELS):
            for name in ("W", "X", "X_T") if l < LEVELS - 1 else ("W", "X_T"):
                order += [(c, name, l) for c in both]
        for c in both:
            order += [(c, name, 0) for name in ("rhs", "SA", "Y", "dS")]
    return order


ORDER = scan_order()
BY_ACT = ("B_t", "K_t", "V_t", "W", "rhs", "SA", "Y")
ACT_STEPS = [s for s in ORDER if s[1] in BY_ACT]


def dve_ops():
    ops = []
    for c, name, l in ORDER:
        if name in BY_ACT:
            if name == "W" and l < LEVELS - 1:
                ops.append(("mask", c, "M", l + 1))
            continue
        ops.append(("take", c, name, l))
        if name == "L_T":
            ops += [("mask", c, "M", 0), ("eye", c, "X_T", 0), ("mask", c, "M", 1)]
        elif name == "L":
            ops.append(("eye", c, "L", 0))
        elif name == "dS":
            ops.append(("decay", c, "dS", 0))
    return ops


DVE_OPS = dve_ops()


def hymba(nc, A):
    with ExitStack() as ctx:
        def sb(name, shape, dt=F32):
            return ctx.enter_context(nc.sbuf_tensor(name, shape, dt))

        def sem(name):
            return ctx.enter_context(nc.semaphore(name))

        hT = sb("hT", [P, KT * (PAD + SPAN)])
        hT_v = hT[:, :].rearrange("p (k t) -> p k t", k=KT)
        h_pad = sb("h_pad", [P, KT, PAD])
        yT = sb("yT", [P, KT, SPAN])
        ring = sb("ring", [P, RING, D])
        gath = sb("gath", [P, GATHERS, D])
        acc = sb("acc", [P, BLOCKS, D])
        h2 = sb("h2", [P, BLOCKS, D])
        S_COLS = 33 * CHUNK * PAIRS
        S = sb("S", [P, S_COLS])
        w2a2 = sb("w2a2", [P, D_RWKV])
        vec = sb("vec", [P, N_VEC])
        con = sb("con", [P, N_CON])
        wa_in = sb("wa_in", [P, SPAN])
        g_in = sb("g_in", [P, 2, SPAN])
        state = sb("state", [P, 2, PAIRS * CHUNK])
        ssq = sb("ssq", [P, 8])
        rstd = sb("rstd", [P, 8])
        pick_i = sb("pick_i", [P, BLOCKS, PICKS], I32)
        gates = sb("gates", [P, BLOCKS, PICKS])
        dots = sb("dots", [P, BLOCKS, PICKS])
        gel = sb("gel", [P, 2, PICKS])
        p_end = sb("p_end", [P, PAIRS, CHUNKS])
        banks = [ctx.enter_context(nc.psum_tensor(f"bank{i}", [P, 512], F32)) for i in range(8)]

        def v(name, i, n=1):
            return vec[:, VEC[name][0] + i:VEC[name][0] + i + n]

        def c_(name, i=0, n=None):
            o, w = CON[name]
            return con[:, o + i:o + i + (w if n is None else n)]

        ident = c_("ident")

        x_in = S[:, 0:BLOCKS * D].rearrange("p (b d) -> p b d", b=BLOCKS)
        lora_cur = S[:, BLOCKS * D:BLOCKS * D + KT * LORA].rearrange("p (k n) -> p k n", k=KT)
        lora_prev = S[:, BLOCKS * D + KT * LORA:BLOCKS * D + 2 * KT * LORA].rearrange("p (k n) -> p k n", k=KT)
        chan = [S[:, i * PAIRS * SPAN:(i + 1) * PAIRS * SPAN].rearrange("p (h t) -> p h t", h=PAIRS)
                for i in range(5)]
        R_c, A_c, B_c, K_c, bonus = chan
        BUF = PAIRS * CHUNK
        wide = [S[:, 5 * PAIRS * SPAN + i * BUF:5 * PAIRS * SPAN + (i + 1) * BUF] for i in range(13)]
        spare = [hT[:, i * BUF:(i + 1) * BUF] for i in range(8)]
        tmp0 = 5 * PAIRS * SPAN
        WID = PAD + SPAN
        TMP = [S[:, tmp0 + i * WID:tmp0 + (i + 1) * WID] for i in range(24)]
        raw = [[TMP[3 * (i % 2) + j] for j in range(3)] for i in range(2)]
        sig_w, sig_a = TMP[6][:, 0:SPAN], TMP[7][:, 0:SPAN]
        lw, lp, lm = (TMP[8 + i][:, 0:SPAN] for i in range(3))
        diff, r_s, k_s, kk_raw, kk_sq, a_gain, k_new, rk = (TMP[11 + i][:, 0:SPAN] for i in range(8))
        e_p, e_n, e_m = (TMP[19 + i][:, 0:SPAN] for i in range(3))
        nrm, kk = TMP[22][:, 0:SPAN], TMP[23][:, 0:SPAN]
        c_raw, u_c, conv_o = TMP[0], TMP[1], [TMP[2 + i][:, 0:SPAN] for i in range(3)]
        bufs = spare + wide
        B_t, K_t, V_t, L_T, LK_T, X, X_T, W_b, M_b = ([bufs[9 * q + i] for q in range(2)] for i in range(9))
        rhs_b, SA_b, sum_b = bufs[18:21]
        y_c = [wide[0][:, 0:SPAN], wide[1][:, 0:SPAN]]
        y_sq = [wide[2][:, 0:SPAN], wide[3][:, 0:SPAN]]
        y_sd = [wide[4][:, 0:SPAN], wide[5][:, 0:SPAN]]
        y_t = [wide[6 + i][:, 0:SPAN] for i in range(4)]
        x_mid = S[:, 0:BLOCKS * D].rearrange("p (b d) -> p b d", b=BLOCKS)
        gain_f = S[:, BLOCKS * D:(BLOCKS + 1) * D]
        keys = S[:, (BLOCKS + 1) * D:(BLOCKS + 3) * D].rearrange("p (s k n) -> p s k n", s=SIDES, k=2)
        q0 = (BLOCKS + 3) * D
        q_T = [S[:, q0 + i * SPAN:q0 + (i + 1) * SPAN] for i in range(4)]
        sc = [S[:, q0 + 4 * SPAN + i * SPAN:q0 + 4 * SPAN + (i + 1) * SPAN].rearrange("p (b n) -> p b n", b=BLOCKS)
              for i in range(2)]
        t0 = q0 + 6 * SPAN

        def take(n):
            nonlocal t0
            t0 += n
            return S[:, t0 - n:t0]

        top_s = take(BLOCKS * SIDES * TOPK).rearrange("p (b s k) -> p b s k", b=BLOCKS, s=SIDES)
        top_i = take(BLOCKS * SIDES * TOPK).bitcast(U32).rearrange("p (b s k) -> p b s k", b=BLOCKS, s=SIDES)
        cand_s = take(BLOCKS * PICKS).rearrange("p (b n) -> p b n", b=BLOCKS)
        cand_i = take(BLOCKS * PICKS).bitcast(U32).rearrange("p (b n) -> p b n", b=BLOCKS)
        rest = take(BLOCKS * NKEYS).rearrange("p (b n) -> p b n", b=BLOCKS)
        cand = take(BLOCKS * TOPK * TOPK).rearrange("p (b n) -> p b n", b=BLOCKS)
        cand2 = take(BLOCKS * TOPK * TOPK).rearrange("p (b n) -> p b n", b=BLOCKS)
        assert t0 <= S_COLS
        p0 = BLOCKS * D
        hot = S[:, p0:p0 + PICKS * TOPK]
        hot_v = S[:, p0 + PICKS * TOPK:p0 + 2 * PICKS * TOPK]
        p1 = p0 + 2 * PICKS * TOPK
        top_f = S[:, p1:p1 + SIDES * TOPK]
        sl_u = S[:, p1 + 256:p1 + 256 + PICKS].bitcast(U32)
        sl_f = S[:, p1 + 384:p1 + 384 + PICKS]
        e_1 = S[:, p1 + 512:p1 + 512 + PICKS]
        e_2 = S[:, p1 + 640:p1 + 640 + PICKS]
        g_e = S[:, p1 + 768:p1 + 768 + PICKS]
        g_s = S[:, p1 + 896:p1 + 896 + HEADS]
        g_r = S[:, p1 + 912:p1 + 912 + HEADS]
        assert p1 + 920 <= q0

        fin_junk = yT[:, 0:KT // 2, :]
        gain_last = yT[:, KT // 2:KT, :].rearrange("p k t -> p (k t)")

        consts_in = sem("consts_in")
        x_loaded = sem("x_loaded")
        lora_loaded = sem("lora_loaded")
        ring_ready = [sem(f"ring_ready{i}") for i in range(RING)]
        ring_used = sem("ring_used")
        norm_act, norm_dve = sem("norm_act"), sem("norm_dve")
        turned = sem("turned")
        turned_out = sem("turned_out")
        lora_split = sem("lora_split")
        lora_mm, lora_act = sem("lora_mm"), sem("lora_act")
        tile_out = sem("tile_out")
        z_mm, z_act = sem("z_mm"), sem("z_act")
        exp_act = sem("exp_act")
        mix = sem("mix")
        sums_mm, sqrt_act = sem("sums_mm"), sem("sqrt_act")
        conv = sem("conv")
        pad_set, pad_saved = sem("pad_set"), sem("pad_saved")
        scan_mm, scan_act, scan_dve = sem("scan_mm"), sem("scan_act"), sem("scan_dve")
        mean_mm, var_mm, gate_mm = sem("mean_mm"), sem("var_mm"), sem("gate_mm")
        outn, outn_act = sem("outn"), sem("outn_act")
        wout_mm = sem("wout_mm")
        res_loaded = sem("res_loaded")
        norm2_act, norm2_dve = sem("norm2_act"), sem("norm2_dve")
        turned2, turned2_out = sem("turned2"), sem("turned2_out")
        score_mm, score_out = sem("score_mm"), sem("score_out")
        pick = sem("pick")
        pick_act = sem("pick_act")
        gathered = [sem(f"gathered{i}") for i in range(GATHERS)]
        row_used = sem("row_used")
        gelu, gelu_act = sem("gelu"), sem("gelu_act")
        fin_dve, fin_act = sem("fin_dve"), sem("fin_act")
        fin_gain = sem("fin_gain")
        acc_set = sem("acc_set")
        stored = sem("stored")
        zeroed = sem("zeroed")

        NB8 = BLOCKS * 4
        TK_SIDE = 5 * BLOCKS
        TK_HEAD = 6 * BLOCKS
        TK_SPAN = SIDES * TK_SIDE + HEADS * TK_HEAD
        PICK_SPAN = TK_SPAN + BLOCKS * len(PICKED)
        ACT_TILES = 3 * PAIRS + CONVS + Q_TILES

        def picked(span, b, name):
            return span * PICK_SPAN + TK_SPAN + PICKED.after(b, name)

        def tile_taken(span, i):
            if i < 3 * PAIRS:
                return tile_out, span * ACT_TILES + i + 1
            if i < W_TILES:
                t, j = divmod(i - 3 * PAIRS, 3)
                if j == 0:
                    return tile_out, span * ACT_TILES + 3 * PAIRS + t + 1
                return conv, CONV.after(span * CONVS + t, "u" if j == 1 else "gate")
            return tile_out, span * ACT_TILES + 3 * PAIRS + CONVS + (i - W_TILES) + 1

        def side_after(span, side):
            return span * PICK_SPAN + (side + 1) * TK_SIDE + (side // 2) * TK_HEAD

        def scan_done(span, c, name, l=0):
            if name in BY_ACT:
                return scan_act, span * len(ACT_STEPS) + ACT_STEPS.index((c, name, l)) + 1
            return scan_dve, span * len(DVE_OPS) + max(i for i, o in enumerate(DVE_OPS) if o[1:] == (c, name, l)) + 1

        def ring_item(span, i):
            m = span * RING_PER_SPAN + i
            return m, m % RING, 16 * (m // RING + 1)

        block = ctx.enter_context(nc.Block())

        @block.sync
        def _(sp):
            sp.dma_start(con[:, :], A["consts"]).then_inc(consts_in, 16)
            sp.dma_start(vec[:, :], A["vecs"]).then_inc(consts_in, 16)
            sp.dma_start(w2a2[:, :], A["w2a2"]).then_inc(consts_in, 16)

            def gain_and_store(span, front):
                sp.wait_ge(ring_used, front * RING_PER_SPAN + W_TILES + 1 + KT)
                sp.dma_start(gain_last, A["norm_final"].partition_broadcast(P)).then_inc(fin_gain, 16)
                for b in range(BLOCKS):
                    n = span * BLOCKS + b
                    sp.wait_ge(fin_dve, FIN.after(n, "out"))
                    sp.dma_start(A["out"][n * P:(n + 1) * P, :], acc[:, b, :]).then_inc(stored, 16)

            for span in range(SPANS):
                rows = slice(span * SPAN, (span + 1) * SPAN)
                if span:
                    sp.wait_ge(pick, span * PICK_SPAN)
                    sp.wait_ge(acc_set, span * BLOCKS)
                xs = A["x"][rows, :].rearrange("(b p) d -> b p d", p=P)
                for b in range(BLOCKS):
                    sp.dma_start(x_in[:, b, :], xs[b]).then_inc(x_loaded, 16)
                sp.dma_start(lora_cur, A["lora_in"]).then_inc(lora_loaded, 16)
                for i in range(W_TILES):
                    m, slot, _ = ring_item(span, i)
                    if m >= RING:
                        sp.wait_ge(ring_used, m - RING + 1)
                    sp.dma_start(ring[:, slot, :], A["w_in"][i]).then_inc(ring_ready[slot], 16)
                m, slot, _ = ring_item(span, W_TILES)
                sp.wait_ge(ring_used, m - RING + 1)
                sp.dma_start(ring[:, slot, :], A["g2"]).then_inc(ring_ready[slot], 16)
                for k in range(KT):
                    m, slot, _ = ring_item(span, W_TILES + 1 + k)
                    sp.wait_ge(ring_used, m - RING + 1)
                    sp.dma_start(ring[:, slot, :], A["w_out"][k * P:(k + 1) * P, :]).then_inc(ring_ready[slot], 16)
                    if k == 0:
                        sp.wait_ge(outn, (span + 1) * PAIRS * len(OUTN))
                        for b in range(BLOCKS):
                            sp.dma_start(x_mid[:, b, :], xs[b]).then_inc(res_loaded, 16)
                        sp.dma_start(gain_f, A["norm_ffn"].partition_broadcast(P)).then_inc(res_loaded, 16)
                        sp.dma_start(keys, A["keys"]).then_inc(res_loaded, 16)
                for i in range(Q_TILES):
                    m, slot, _ = ring_item(span, W_TILES + 1 + KT + i)
                    sp.wait_ge(ring_used, m - RING + 1)
                    sp.dma_start(ring[:, slot, :], A["wq"][i]).then_inc(ring_ready[slot], 16)
                if span:
                    gain_and_store(span - 1, span)
            gain_and_store(SPANS - 1, SPANS - 1)
            sp.wait_ge(stored, 16 * SPANS * BLOCKS)

        @block.tensor
        def _(pe):
            pe.wait_ge(consts_in, 48)

            def tile(span, i, item, rhs, n):
                _, slot, ready = ring_item(span, item)
                if i >= 4:
                    pe.wait_ge(*tile_taken(span, i - 4))
                pe.wait_ge(ring_ready[slot], ready)
                for k in range(KT):
                    mm = pe.matmul(banks[i % 4][:, 0:n], ring[:, slot, k * P:(k + 1) * P], rhs(k),
                                   start=(k == 0), stop=(k == KT - 1))
                mm.then_inc(ring_used, 1)

            def turn(src, sem_in, ready, done):
                for n in range(NB8):
                    b, k4 = divmod(n, 4)
                    if k4 == 0:
                        pe.wait_ge(sem_in, ready(b))
                    for j in range(4):
                        k = 4 * k4 + j
                        mm = pe.transpose(banks[n][:, j * P:(j + 1) * P], src[:, b, k * P:(k + 1) * P], ident)
                    mm.then_inc(done, 1)

            def pair_mm(bank, lhsT, rhs, terms=1):
                for h in range(PAIRS):
                    for q in range(2):
                        rows = slice(q * HALF, (q + 1) * HALF)
                        for i in range(terms):
                            mm = pe.matmul(bank[rows, h * CHUNK:(h + 1) * CHUNK], lhsT[i](h)[rows, :],
                                           rhs[i](h, q)[rows, :], start=(i == 0), stop=(i == terms - 1))
                return mm

            for span in range(SPANS):
                if span:
                    pe.wait_ge(*tile_taken(span - 1, W_TILES + Q_TILES - 1))
                    pe.wait_ge(score_out, span * SIDES)
                turn(x_in, norm_dve, lambda b: NORM1.after(span * BLOCKS + b, "scaled"), turned)

                pe.wait_ge(turned_out, NB8 * (span + 1))
                pe.wait_ge(lora_split, 4 * (span + 1))
                pe.wait_ge(pad_set, span + 1)
                for n, (c0, c1) in enumerate(((0, P), (P, 2 * P), (2 * P, LORA))):
                    out = banks[4 + n][0:c1 - c0, 0:SPAN]
                    for k in range(KT):
                        pe.matmul(out, lora_cur[:, k, c0:c1], hT_v[:, k, PAD:PAD + SPAN], start=(k == 0), stop=False)
                        mm = pe.matmul(out, lora_prev[:, k, c0:c1], hT_v[:, k, PAD - 1:PAD - 1 + SPAN],
                                       start=False, stop=(k == KT - 1))
                    mm.then_inc(lora_mm, 1)

                def sums(h):
                    n = span * PAIRS + h
                    pe.wait_ge(mix, MIX.after(n, "bonus_raw"))
                    if n >= 1:
                        pe.wait_ge(mix, MIX.after(n - 1, "bonus"))
                    pe.matmul(banks[5][:, 0:SPAN], c_("head_ones"), kk_sq, start=True, stop=True)
                    pe.matmul(banks[6][:, 0:SPAN], c_("head_ones"), rk, start=True, stop=True).then_inc(sums_mm, 1)

                pe.wait_ge(lora_act, 4 * (span + 1))
                for h in range(PAIRS):
                    n = span * PAIRS + h
                    zb = banks[4 if h % 2 else 7]
                    if h >= 2:
                        pe.wait_ge(z_act, 2 * (n - 1))
                    pe.matmul(zb[:, 0:SPAN], w2a2[0:HALF, h * P:(h + 1) * P], wa_in[0:HALF, :],
                              start=True, stop=True).then_inc(z_mm, 1)
                    pe.wait_ge(z_mm, 2 * n + 1)
                    pe.matmul(zb[:, SPAN:2 * SPAN], w2a2[HALF:P, h * P:(h + 1) * P], wa_in[HALF:P, :],
                              start=True, stop=True).then_inc(z_mm, 1)
                    for j in range(3):
                        tile(span, 3 * h + j, 3 * h + j, lambda k: hT_v[:, k, :], WID)
                        if j == 0 and h:
                            sums(h - 1)
                for t in range(CONVS):
                    for j in range(3):
                        i = 3 * PAIRS + 3 * t + j
                        tile(span, i, i, lambda k: hT_v[:, k, :], WID)
                        if t == 0 and j == 0:
                            sums(PAIRS - 1)

                pe.wait_ge(mix, MIX.after(span * PAIRS + PAIRS - 1, "bonus"))
                pe.wait_ge(conv, CONV.after(span * CONVS + CONVS - 1, "gate"))
                for i, (c, name, l) in enumerate(ORDER):
                    q = c % 2
                    n = span * CHUNKS + c
                    ts = slice(c * CHUNK, (c + 1) * CHUNK)
                    bank = banks[i % 8]
                    if i >= 8:
                        pe.wait_ge(*scan_done(span, *ORDER[i - 8]))

                    def cols(buf):
                        return lambda h, _=0: buf[:, h * CHUNK:(h + 1) * CHUNK]

                    def chn(buf):
                        return lambda h, _=0: buf[:, h, ts]

                    def eye(h, par):
                        return con[:, CON["ident"][0] + par * HALF:CON["ident"][0] + (par + 1) * HALF]

                    if name == "B_t":
                        mm = pair_mm(bank, [chn(B_c)], [eye])
                    elif name == "K_t":
                        mm = pair_mm(bank, [chn(K_c)], [eye])
                    elif name == "V_t":
                        mm = pair_mm(bank, [chn(yT)], [eye])
                    elif name == "L_T":
                        mm = pair_mm(bank, [chn(B_c)], [chn(A_c)])
                    elif name == "L":
                        mm = pair_mm(bank, [chn(A_c)], [chn(B_c)])
                    elif name == "LK_T":
                        mm = pair_mm(bank, [chn(K_c)], [chn(A_c)])
                    elif name == "RB_T":
                        mm = pair_mm(bank, [chn(B_c)], [chn(R_c)])
                    elif name == "RK_T":
                        mm = pair_mm(bank, [chn(K_c)], [chn(R_c)])
                    elif name == "W":
                        pe.wait_ge(*scan_done(span, c, "M", l))
                        pe.wait_ge(*scan_done(span, c, "X" if l > 1 else "L", l - 1 if l > 1 else 0))
                        mm = pair_mm(bank, [cols(M_b[q])], [cols(X[q])])
                    elif name == "X":
                        pe.wait_ge(*scan_done(span, c, "W", l))
                        if l > 1:
                            pe.wait_ge(*scan_done(span, c, "X_T", l - 1))
                        mm = pair_mm(bank, [cols(X_T[q])], [cols(W_b[q])])
                    elif name == "X_T":
                        pe.wait_ge(*scan_done(span, c, "W", l))
                        if l > 1:
                            pe.wait_ge(*scan_done(span, c, "X_T", l - 1))
                        mm = pair_mm(bank, [cols(W_b[q])], [cols(X_T[q])])
                    elif name == "rhs":
                        if c:
                            pe.wait_ge(*scan_done(span, c - 1, "dS"))
                        pe.wait_ge(*scan_done(span, c, "LK_T"))
                        pe.wait_ge(*scan_done(span, c, "V_t"))
                        mm = pair_mm(bank, [chn(A_c), cols(LK_T[q])], [cols(state[:, n % 2, :]), cols(V_t[q])], 2)
                    elif name == "SA":
                        pe.wait_ge(*scan_done(span, c, "rhs"))
                        pe.wait_ge(*scan_done(span, c, "X_T", LEVELS - 1))
                        mm = pair_mm(bank, [cols(X_T[q])], [cols(rhs_b)])
                    elif name == "Y":
                        pe.wait_ge(*scan_done(span, c, "SA"))
                        mm = pair_mm(bank, [cols(state[:, n % 2, :]), cols(SA_b), cols(V_t[q])],
                                     [chn(R_c), chn(B_c), chn(K_c)], 3)
                    elif name == "dS":
                        mm = pair_mm(bank, [cols(B_t[q]), cols(K_t[q])], [cols(SA_b), cols(V_t[q])], 2)
                    mm.then_inc(scan_mm, 1)

                _, g_slot, g_ready = ring_item(span, W_TILES)
                pe.wait_ge(ring_ready[g_slot], g_ready)
                pe.wait_ge(*scan_done(span, CHUNKS - 1, "Y"))
                pe.wait_ge(*scan_done(span, CHUNKS - 1, "dS"))

                def variance(h):
                    n = span * PAIRS + h
                    pe.wait_ge(outn_act, 2 * n + 1)
                    if h >= 2:
                        pe.wait_ge(outn_act, 2 * (n - 2) + 2)
                    pe.matmul(banks[2 + h % 2][:, 0:SPAN], c_("head_mean"), y_sq[h % 2],
                              start=True, stop=True).then_inc(var_mm, 1)

                for h in range(PAIRS):
                    n = span * PAIRS + h
                    if h >= 2:
                        pe.wait_ge(outn, OUTN.after(n - 2, "gated"))
                    pe.matmul(banks[h % 2][:, 0:SPAN], c_("head_mean"), yT[:, h, :],
                              start=True, stop=True).then_inc(mean_mm, 1)
                    if h:
                        variance(h - 1)
                    pe.matmul(banks[4 + h % 2][:, 0:SPAN], ring[:, g_slot, h * P:(h + 1) * P], g_in[:, 0, :],
                              start=True, stop=False)
                    mm = pe.matmul(banks[4 + h % 2][:, 0:SPAN], ring[0:32, g_slot, D_RWKV + h * P:D_RWKV + (h + 1) * P],
                                   g_in[0:32, 1, :], start=False, stop=True)
                    mm.then_inc(gate_mm, 1)
                variance(PAIRS - 1)
                pe.wait_ge(outn, (span + 1) * PAIRS * len(OUTN))
                pe.wait_ge(outn_act, 2 * (span + 1) * PAIRS)

                for k in range(KT):
                    _, slot, ready = ring_item(span, W_TILES + 1 + k)
                    pe.wait_ge(ring_ready[slot], ready)
                    for b in range(BLOCKS):
                        for n in range(4):
                            mm = pe.matmul(banks[4 * b + n][:, :], yT[:, k, b * P:(b + 1) * P],
                                           ring[:, slot, n * 512:(n + 1) * 512], start=(k == 0), stop=(k == KT - 1))
                            if k == 0 and b == 0 and n == 0:
                                mm.then_inc(ring_used, 1)
                    mm.then_inc(ring_used, 1)

                turn(h2, norm2_dve, lambda b: NORM2.after(span * BLOCKS + b, "scaled"), turned2)

                def scores(s):
                    n = span * SIDES + s
                    pe.wait_ge(*tile_taken(span, W_TILES + 2 * s + 1))
                    if s >= 2:
                        pe.wait_ge(score_out, n - 1)
                    for b in range(BLOCKS):
                        for j in range(2):
                            mm = pe.matmul(banks[4 + s % 2][:, b * P:(b + 1) * P], q_T[(2 * s + j) % 4][:, b * P:(b + 1) * P],
                                           keys[:, s, j, :], start=(j == 0), stop=(j == 1))
                    mm.then_inc(score_mm, 1)

                pe.wait_ge(turned2_out, NB8 * (span + 1))
                pe.wait_ge(res_loaded, 16 * 4 * (span + 1))
                for i in range(Q_TILES):
                    tile(span, W_TILES + i, W_TILES + 1 + KT + i, lambda k: hT_v[:, k, PAD:PAD + SPAN], SPAN)
                    if i % 2 == 0 and i:
                        scores(i // 2 - 1)
                scores(SIDES - 1)

        @block.scalar
        def _(act):
            def gelu_tanhs(span):
                for b in range(BLOCKS):
                    n = span * BLOCKS + b
                    act.wait_ge(gelu, GELU.after(n, "inner"))
                    act.activation(gel[:, 0, :], gel[:, 0, :], ACT.Tanh, scale=GELU_S).then_inc(gelu_act, 1)

            def final_roots(span):
                for b in range(BLOCKS):
                    n = span * BLOCKS + b
                    act.wait_ge(row_used, span * ROWS_SPAN + (BLOCKS + b + 1) * PICKS)
                    if b:
                        act.wait_ge(fin_act, 2 * n)
                    act.activation(fin_junk, acc[:, b, :].rearrange("p (k t) -> p k t", t=SPAN), ACT.Square,
                                   accum_out=ssq[:, 4 + b:5 + b]).then_inc(fin_act, 1)
                    act.wait_ge(fin_dve, FIN.after(n, "mean_sq"))
                    act.activation(rstd[:, 4 + b:5 + b], ssq[:, 6 + b:7 + b], ACT.Sqrt).then_inc(fin_act, 1)

            act.wait_ge(consts_in, 48)
            for span in range(SPANS):
                for b in range(BLOCKS):
                    act.wait_ge(x_loaded, 16 * BLOCKS * (span + 1))
                    if span:
                        act.wait_ge(turned2_out, NB8 * span)
                    act.activation(yT[:, 8 * b:8 * b + 8, :], x_in[:, b, :].rearrange("p (k t) -> p k t", k=8),
                                   ACT.Square, accum_out=ssq[:, b:b + 1]).then_inc(norm_act, 1)
                for b in range(BLOCKS):
                    act.wait_ge(norm_dve, NORM1.after(span * BLOCKS + b, "mean_sq"))
                    act.activation(rstd[:, b:b + 1], ssq[:, 2 + b:3 + b], ACT.Sqrt).then_inc(norm_act, 1)
                act.wait_ge(lora_mm, 3 * span + 1)
                if span:
                    act.wait_ge(gate_mm, span * PAIRS)
                act.activation(wa_in[0:HALF, :], banks[4][0:HALF, 0:SPAN], ACT.Tanh).then_inc(lora_act, 1)
                act.activation(wa_in[HALF:P, :], banks[4][HALF:P, 0:SPAN], ACT.Copy).then_inc(lora_act, 1)
                act.wait_ge(lora_mm, 3 * span + 2)
                act.activation(g_in[:, 0, :], banks[5][:, 0:SPAN], ACT.Sigmoid).then_inc(lora_act, 1)
                act.wait_ge(lora_mm, 3 * span + 3)
                act.activation(g_in[0:32, 1, :], banks[6][0:32, 0:SPAN], ACT.Sigmoid).then_inc(lora_act, 1)
                for h in range(PAIRS):
                    n = span * PAIRS + h
                    zb = banks[4 if h % 2 else 7]
                    act.wait_ge(z_mm, 2 * n + 2)
                    if h:
                        act.wait_ge(mix, MIX.after(n - 1, "bonus"))
                    act.activation(sig_w, zb[:, 0:SPAN], ACT.Sigmoid, bias=v("w0", h)).then_inc(z_act, 1)
                    act.activation(sig_a, zb[:, SPAN:2 * SPAN], ACT.Sigmoid, bias=v("a0", h)).then_inc(z_act, 1)
                    for j in range(3):
                        act.wait_ge(ring_used, span * RING_PER_SPAN + 3 * h + j + 1)
                        act.activation(raw[h % 2][j], banks[(3 * h + j) % 4][:, 0:WID], ACT.Copy).then_inc(tile_out, 1)
                    act.wait_ge(mix, MIX.after(n, "log_prod"))
                    act.activation(e_p, lp, ACT.Exp).then_inc(exp_act, 1)
                    act.activation(e_n, lp, ACT.Exp, scale=-1.0).then_inc(exp_act, 1)
                    act.wait_ge(mix, MIX.after(n, "log_prev"))
                    act.activation(e_m, lm, ACT.Exp).then_inc(exp_act, 1)
                    act.wait_ge(sums_mm, n + 1)
                    act.activation(nrm, banks[5][:, 0:SPAN], ACT.Sqrt).then_inc(sqrt_act, 1)
                act.wait_ge(mix, MIX.after(span * PAIRS + PAIRS - 1, "bonus"))
                for t in range(CONVS):
                    if t:
                        act.wait_ge(conv, CONV.after(span * CONVS + t - 1, "u"))
                    act.wait_ge(ring_used, span * RING_PER_SPAN + 3 * PAIRS + 3 * t + 1)
                    act.activation(c_raw, banks[(3 * PAIRS + 3 * t) % 4][:, 0:WID], ACT.Copy).then_inc(tile_out, 1)
                for i, (c, name, l) in enumerate(ORDER):
                    if name not in BY_ACT:
                        continue
                    q = c % 2
                    act.wait_ge(scan_mm, span * len(ORDER) + i + 1)
                    src = banks[i % 8][:, :]
                    if name == "Y":
                        dst = yT[:, 0:PAIRS, c * CHUNK:(c + 1) * CHUNK]
                        src = src.rearrange("p (h t) -> p h t", h=PAIRS)
                    else:
                        dst = {"B_t": B_t[q], "K_t": K_t[q], "V_t": V_t[q], "W": W_b[q], "rhs": rhs_b, "SA": SA_b}[name]
                    if i < 4:
                        act.wait_ge(pad_saved, span + 1)
                    act.activation(dst, src, ACT.Copy).then_inc(scan_act, 1)
                if span:
                    gelu_tanhs(span - 1)
                for h in range(PAIRS):
                    n = span * PAIRS + h
                    act.wait_ge(outn, OUTN.after(n, "center"))
                    act.activation(y_sq[h % 2], y_c[h % 2], ACT.Square).then_inc(outn_act, 1)
                    act.wait_ge(var_mm, n + 1)
                    act.activation(y_sd[h % 2], banks[2 + h % 2][:, 0:SPAN], ACT.Sqrt, bias=v("eps", 1)).then_inc(outn_act, 1)
                for b in range(BLOCKS):
                    act.wait_ge(norm2_dve, NORM2.after(span * BLOCKS + b, "sum3"))
                    act.activation(h2[:, b, :], x_mid[:, b, :], ACT.Square, accum_out=ssq[:, b:b + 1]).then_inc(norm2_act, 1)
                    act.wait_ge(norm2_dve, NORM2.after(span * BLOCKS + b, "mean_sq"))
                    act.activation(rstd[:, b:b + 1], ssq[:, 2 + b:3 + b], ACT.Sqrt).then_inc(norm2_act, 1)
                for n in range(NB8):
                    b, k4 = divmod(n, 4)
                    act.wait_ge(turned2, span * NB8 + n + 1)
                    act.activation(hT_v[:, 4 * k4:4 * k4 + 4, PAD + b * P:PAD + (b + 1) * P],
                                   banks[n][:, :].rearrange("p (k t) -> p k t", k=4), ACT.Copy).then_inc(turned2_out, 1)
                def score_copy(s):
                    n = span * SIDES + s
                    act.wait_ge(score_mm, n + 1)
                    if s >= 2:
                        act.wait_ge(pick, side_after(span, s - 2))
                    act.activation(sc[s % 2], banks[4 + s % 2][:, 0:SPAN].rearrange("p (b n) -> p b n", b=BLOCKS),
                                   ACT.Copy).then_inc(score_out, 1)

                for i in range(Q_TILES):
                    act.wait_ge(ring_used, span * RING_PER_SPAN + W_TILES + 1 + KT + i + 1)
                    if i >= 4:
                        act.wait_ge(score_mm, span * SIDES + (i - 4) // 2 + 1)
                    act.activation(q_T[i % 4], banks[i % 4][:, 0:SPAN], ACT.Copy).then_inc(tile_out, 1)
                    if i % 2 == 0 and i:
                        score_copy(i // 2 - 1)
                score_copy(SIDES - 1)
                if span:
                    final_roots(span - 1)
                for b in range(BLOCKS):
                    act.wait_ge(pick, picked(span, b, "shifted"))
                    act.activation(g_e, g_e, ACT.Exp).then_inc(pick_act, 1)
                if span:
                    act.wait_ge(stored, 16 * BLOCKS * span)
                act.wait_ge(norm2_dve, NORM2.after(span * BLOCKS + BLOCKS - 1, "sum3"))
                for b in range(BLOCKS):
                    act.activation(acc[:, b, :], x_mid[:, b, :], ACT.Copy).then_inc(acc_set, 1)
            gelu_tanhs(SPANS - 1)
            final_roots(SPANS - 1)

        @block.vector
        def _(dve):
            def chain(signal, start):
                n = [start]

                def step(ins):
                    n[0] += 1
                    ins.then_inc(signal, 1)
                    dve.wait_ge(signal, n[0])
                step.count = n
                return step

            def by_head(ap):
                return ap.rearrange("p (h t) -> p h t", h=PAIRS)

            def each_head(name):
                return c_(name).unsqueeze(1).to_broadcast([P, PAIRS, CHUNK])

            def row(r):
                slot, n = r % GATHERS, r // GATHERS
                span, r_span = divmod(r, ROWS_SPAN)
                table, b, k = r_span // (BLOCKS * PICKS), r_span // PICKS % BLOCKS, r_span % PICKS
                dve.wait_ge(gathered[slot], 16 * (n + 1))
                if table == 0:
                    ins = dve.tensor_tensor_reduce(gath[:, slot, :], gath[:, slot, :], h2[:, b, :], 1.0, 0.0,
                                                   ALU.mult, ALU.add, dots[:, b, k:k + 1])
                else:
                    if r_span == BLOCKS * PICKS:
                        dve.wait_ge(acc_set, BLOCKS * (span + 1))
                    dve.wait_ge(row_used, r)
                    ins = dve.scalar_tensor_tensor(out=acc[:, b, :], in0=gath[:, slot, :], scalar=gates[:, b, k:k + 1],
                                                   in1=acc[:, b, :], op0=ALU.mult, op1=ALU.add)
                ins.then_inc(row_used, 1)

            next_row = 0

            def rows(count):
                nonlocal next_row
                for _ in range(count):
                    row(next_row)
                    next_row += 1

            def between(span, count):
                if span:
                    rows(count)

            def rows_over(span, i, n, count):
                if span:
                    rows((i + 1) * count // n - i * count // n)

            def gelus(span):
                dve.wait_ge(row_used, span * ROWS_SPAN + BLOCKS * PICKS)
                for b in range(BLOCKS):
                    n = span * BLOCKS + b
                    step = chain(gelu, n * len(GELU))
                    x, g0, g1 = dots[:, b, :], gel[:, 0, :], gel[:, 1, :]
                    step(dve.tensor_tensor(g0, x, x, ALU.mult))
                    step(dve.tensor_tensor(g1, g0, x, ALU.mult))
                    step(dve.scalar_tensor_tensor(out=g0, in0=g1, scalar=GELU_C, in1=x, op0=ALU.mult, op1=ALU.add))
                    dve.wait_ge(gelu_act, n + 1)
                    step(dve.scalar_tensor_tensor(out=g1, in0=g0, scalar=1.0, in1=x, op0=ALU.add, op1=ALU.mult))
                    step(dve.scalar_tensor_tensor(out=gates[:, b, :], in0=g1, scalar=0.5, in1=gates[:, b, :],
                                                  op0=ALU.mult, op1=ALU.mult))

            def final(span):
                for b in range(BLOCKS):
                    n = span * BLOCKS + b
                    step = chain(fin_dve, n * len(FIN))
                    dve.wait_ge(fin_act, 2 * n + 1)
                    step(dve.tensor_scalar(ssq[:, 6 + b:7 + b], ssq[:, 4 + b:5 + b], 1.0 / D, RMS_EPS, ALU.mult, ALU.add))
                    dve.wait_ge(fin_act, 2 * n + 2)
                    step(dve.reciprocal(rstd[:, 6 + b:7 + b], rstd[:, 4 + b:5 + b]))
                    dve.wait_ge(fin_gain, 16 * (span + 1))
                    step(dve.scalar_tensor_tensor(out=acc[:, b, :], in0=acc[:, b, :], scalar=rstd[:, 6 + b:7 + b],
                                                  in1=gain_last, op0=ALU.mult, op1=ALU.mult))

            dve.wait_ge(consts_in, 48)
            dve.memset(state[:, 0, :], 0.0).then_inc(zeroed, 1)
            dve.memset(h_pad[:, :, :], 0.0).then_inc(zeroed, 1)
            dve.wait_ge(zeroed, 2)
            for span in range(SPANS):
                step = chain(lora_split, 4 * span)
                dve.wait_ge(lora_loaded, 16 * (span + 1))
                for j, (c0, c1) in enumerate(((0, 64), (64, 128), (128, LORA))):
                    mu = v("mu_lora", j * KT, KT).unsqueeze(2).to_broadcast([P, KT, c1 - c0])
                    step(dve.tensor_tensor(lora_prev[:, :, c0:c1], lora_cur[:, :, c0:c1], mu, ALU.mult))
                step(dve.tensor_tensor(lora_cur, lora_cur, lora_prev, ALU.subtract))
                rows_over(span, 0, 1, ROWS["lora"])
                if span:
                    dve.wait_ge(ring_used, span * RING_PER_SPAN)
                dve.tensor_copy(hT_v[:, :, 0:PAD], h_pad[:, :, :]).then_inc(pad_set, 1)
                step = chain(norm_dve, span * BLOCKS * len(NORM1))
                for b in range(BLOCKS):
                    n = span * 2 * BLOCKS
                    dve.wait_ge(norm_act, n + b + 1)
                    step(dve.tensor_scalar(ssq[:, 2 + b:3 + b], ssq[:, b:b + 1], 1.0 / D, RMS_EPS, ALU.mult, ALU.add))
                    dve.wait_ge(norm_act, n + BLOCKS + b + 1)
                    step(dve.reciprocal(rstd[:, 2 + b:3 + b], rstd[:, b:b + 1]))
                    step(dve.tensor_scalar(x_in[:, b, :], x_in[:, b, :], rstd[:, 2 + b:3 + b], None, ALU.mult))
                for n in range(NB8):
                    b, k4 = divmod(n, 4)
                    dve.wait_ge(turned, span * NB8 + n + 1)
                    gain = v("norm_mix", 4 * k4, 4).unsqueeze(2).to_broadcast([P, 4, P])
                    dve.tensor_tensor(hT_v[:, 4 * k4:4 * k4 + 4, PAD + b * P:PAD + (b + 1) * P],
                                      banks[n][:, :].rearrange("p (k t) -> p k t", k=4), gain, ALU.mult)\
                       .then_inc(turned_out, 1)
                    rows_over(span, n, NB8, ROWS["turn"])
                step = chain(mix, span * PAIRS * len(MIX))
                for h in range(PAIRS):
                    n = span * PAIRS + h
                    if h == 0:
                        dve.wait_ge(lora_mm, 3 * (span + 1))
                    dve.wait_ge(z_act, 2 * n + 1)
                    step(dve.tensor_scalar(lw, sig_w, -EXP_M_HALF, None, ALU.mult))
                    step(dve.tensor_tensor_scan(lp, c_("keep"), lw, 0.0, ALU.mult, ALU.add))
                    step(dve.tensor_tensor(lm, lp, lw, ALU.subtract))
                    between(span, 1)
                    outs = (r_s, k_s, yT[:, h, :])
                    for j in range(3):
                        src = raw[h % 2][j]
                        dve.wait_ge(*tile_taken(span, 3 * h + j))
                        step(dve.tensor_tensor(diff, src[:, PAD - 1:PAD - 1 + SPAN], src[:, PAD:PAD + SPAN], ALU.subtract))
                        step(dve.scalar_tensor_tensor(out=outs[j], in0=diff, scalar=v("mu_rkv", j * PAIRS + h),
                                                      in1=src[:, PAD:PAD + SPAN], op0=ALU.mult, op1=ALU.add))
                        between(span, 2)
                    step(dve.tensor_scalar(kk_raw, k_s, v("k_k", h), None, ALU.mult))
                    step(dve.tensor_tensor(kk_sq, kk_raw, kk_raw, ALU.mult))
                    dve.wait_ge(z_act, 2 * n + 2)
                    step(dve.tensor_scalar(a_gain, sig_a, 1.0, v("k_a", h), ALU.subtract, ALU.mult))
                    step(dve.scalar_tensor_tensor(out=k_new, in0=a_gain, scalar=1.0, in1=k_s, op0=ALU.add, op1=ALU.mult))
                    step(dve.scalar_tensor_tensor(out=rk, in0=r_s, scalar=v("r_k", h), in1=k_new, op0=ALU.mult, op1=ALU.mult))
                    between(span, 1)
                    dve.wait_ge(exp_act, 3 * n + 3)
                    step(dve.tensor_tensor(R_c[:, h, :], r_s, e_p, ALU.mult))
                    step(dve.tensor_tensor(K_c[:, h, :], k_new, e_n, ALU.mult))
                    step(dve.tensor_copy(p_end[:, h, :], e_p[:, CHUNK - 1:SPAN:CHUNK]))
                    between(span, 1)
                    dve.wait_ge(sqrt_act, n + 1)
                    step(dve.tensor_scalar(nrm, nrm, 1e-12, None, ALU.max))
                    step(dve.reciprocal(nrm, nrm))
                    step(dve.tensor_tensor(kk, kk_raw, nrm, ALU.mult))
                    step(dve.tensor_tensor(kk_sq, kk, sig_a, ALU.mult))
                    step(dve.tensor_tensor(B_c[:, h, :], kk_sq, e_n, ALU.mult))
                    step(dve.scalar_tensor_tensor(out=A_c[:, h, :], in0=kk, scalar=-1.0, in1=e_m, op0=ALU.mult, op1=ALU.mult))
                    dve.wait_ge(sums_mm, n + 1)
                    step(dve.tensor_tensor(bonus[:, h, :], banks[6][:, 0:SPAN], yT[:, h, :], ALU.mult))
                    between(span, ROWS["head"] - 9)
                assert step.count[0] == (span + 1) * PAIRS * len(MIX)
                step = chain(conv, span * CONVS * len(CONV))
                for t in range(CONVS):
                    n = span * CONVS + t
                    i = 3 * PAIRS + 3 * t
                    bx, bb = (i + 1) % 4, (i + 2) % 4
                    dve.wait_ge(*tile_taken(span, i))
                    dve.wait_ge(ring_used, span * RING_PER_SPAN + 3 * PAIRS + 3 * t + 2)
                    step(dve.tensor_tensor(u_c, banks[bx][:, 0:WID], c_raw, ALU.mult))
                    between(span, 3)
                    step(dve.tensor_scalar(conv_o[0], u_c[:, 0:SPAN], v("conv_w", t), None, ALU.mult))
                    step(dve.scalar_tensor_tensor(out=conv_o[1], in0=u_c[:, 1:1 + SPAN], scalar=v("conv_w", CONVS + t),
                                                  in1=conv_o[0], op0=ALU.mult, op1=ALU.add))
                    step(dve.scalar_tensor_tensor(out=conv_o[2], in0=u_c[:, 2:2 + SPAN], scalar=v("conv_w", 2 * CONVS + t),
                                                  in1=conv_o[1], op0=ALU.mult, op1=ALU.add))
                    between(span, 3)
                    dve.wait_ge(ring_used, span * RING_PER_SPAN + 3 * PAIRS + 3 * t + 3)
                    step(dve.tensor_tensor(yT[:, PAIRS + t, :], banks[bb][:, PAD:PAD + SPAN], conv_o[2], ALU.mult))
                    between(span, ROWS["conv"] - 6)
                dve.tensor_copy(h_pad[:, :, :], hT_v[:, :, SPAN:SPAN + PAD]).then_inc(pad_saved, 1)
                dve.wait_ge(pad_saved, span + 1)
                step = chain(scan_dve, span * len(DVE_OPS))
                for i, (what, c, name, l) in enumerate(DVE_OPS):
                    rows_over(span, i, len(DVE_OPS), ROWS["scan"])
                    q, n = c % 2, span * CHUNKS + c
                    ts = slice(c * CHUNK, (c + 1) * CHUNK)
                    if what == "mask":
                        if l > 1:
                            dve.wait_ge(scan_mm, span * len(ORDER) + ORDER.index((c, "W", l - 1)) + 1)
                        mask = c_("up", l * CHUNK, CHUNK).unsqueeze(1).to_broadcast([P, PAIRS, CHUNK])
                        step(dve.tensor_tensor(by_head(M_b[q]), by_head(L_T[q]), mask, ALU.mult))
                        continue
                    if what == "eye":
                        src, dst = (M_b[q], X_T[q]) if name == "X_T" else (X[q], X[q])
                        step(dve.tensor_tensor(by_head(dst), by_head(src), each_head("eye"), ALU.add))
                        continue
                    if what == "decay":
                        end = p_end[:, :, c:c + 1].to_broadcast([P, PAIRS, CHUNK])
                        step(dve.tensor_tensor(by_head(state[:, (n + 1) % 2, :]), by_head(sum_b), end, ALU.mult))
                        continue
                    k = ORDER.index((c, name, l))
                    dve.wait_ge(scan_mm, span * len(ORDER) + k + 1)
                    src = banks[k % 8][:, :]
                    if name in ("L_T", "LK_T"):
                        step(dve.tensor_tensor(by_head((L_T if name == "L_T" else LK_T)[q]), by_head(src),
                                               each_head("before"), ALU.mult))
                    elif name == "L":
                        step(dve.tensor_tensor(by_head(X[q]), by_head(src), each_head("low0"), ALU.mult))
                    elif name in ("RB_T", "RK_T"):
                        step(dve.tensor_tensor((B_c if name == "RB_T" else K_c)[:, :, ts], by_head(src),
                                               each_head("upto"), ALU.mult))
                    elif name in ("X", "X_T"):
                        dst = (X if name == "X" else X_T)[q]
                        step(dve.tensor_tensor(dst, src, dst, ALU.add))
                    elif name == "dS":
                        step(dve.tensor_tensor(sum_b, src, state[:, n % 2, :], ALU.add))
                if span:
                    gelus(span - 1)
                step = chain(outn, span * PAIRS * len(OUTN))
                for h in range(PAIRS):
                    n = span * PAIRS + h
                    dve.wait_ge(mean_mm, n + 1)
                    step(dve.tensor_tensor(y_c[h % 2], yT[:, h, :], banks[h % 2][:, 0:SPAN], ALU.subtract))
                    dve.wait_ge(outn_act, 2 * n + 2)
                    step(dve.reciprocal(y_t[0], y_sd[h % 2]))
                    step(dve.tensor_tensor(y_t[1], y_c[h % 2], y_t[0], ALU.mult))
                    step(dve.tensor_scalar(y_t[2], y_t[1], v("gn_w", h), v("gn_b", h), ALU.mult, ALU.add))
                    step(dve.tensor_tensor(y_t[3], y_t[2], bonus[:, h, :], ALU.add))
                    dve.wait_ge(gate_mm, n + 1)
                    step(dve.tensor_tensor(yT[:, h, :], y_t[3], banks[4 + h % 2][:, 0:SPAN], ALU.mult))
                    between(span, ROWS["outn"])
                between(span, ROWS["w_out"])
                step = chain(norm2_dve, span * BLOCKS * len(NORM2))
                dve.wait_ge(res_loaded, 16 * 4 * (span + 1))
                dve.wait_ge(ring_used, span * RING_PER_SPAN + W_TILES + 1 + KT)
                for b in range(BLOCKS):
                    for n in range(4):
                        cs = slice(n * 512, (n + 1) * 512)
                        step(dve.tensor_tensor(x_mid[:, b, cs], banks[4 * b + n][:, :], x_mid[:, b, cs], ALU.add))
                    n = span * 2 * BLOCKS + 2 * b
                    dve.wait_ge(norm2_act, n + 1)
                    step(dve.tensor_scalar(ssq[:, 2 + b:3 + b], ssq[:, b:b + 1], 1.0 / D, RMS_EPS, ALU.mult, ALU.add))
                    dve.wait_ge(norm2_act, n + 2)
                    step(dve.reciprocal(rstd[:, 2 + b:3 + b], rstd[:, b:b + 1]))
                    step(dve.scalar_tensor_tensor(out=h2[:, b, :], in0=x_mid[:, b, :], scalar=rstd[:, 2 + b:3 + b],
                                                  in1=gain_f, op0=ALU.mult, op1=ALU.mult))
                    between(span, ROWS["norm2"] // BLOCKS)
                step = chain(pick, span * PICK_SPAN)
                eights = (slice(0, 8), slice(8, 16))
                for s in range(SIDES):
                    dve.wait_ge(score_out, span * SIDES + s + 1)
                    src = sc[s % 2]
                    for b in range(BLOCKS):
                        step(dve.max(top_s[:, b, s, 0:8], src[:, b, :]))
                    for b in range(BLOCKS):
                        step(dve.match_replace(rest[:, b, :], top_s[:, b, s, 0:8], src[:, b, :], FAR))
                    for b in range(BLOCKS):
                        step(dve.max(top_s[:, b, s, 8:16], rest[:, b, :]))
                    for b in range(BLOCKS):
                        step(dve.max_index(top_i[:, b, s, 0:8], top_s[:, b, s, 0:8], src[:, b, :]))
                    for b in range(BLOCKS):
                        step(dve.max_index(top_i[:, b, s, 8:16], top_s[:, b, s, 8:16], rest[:, b, :]))
                    between(span, ROWS["side"])
                    if s % 2 == 0:
                        continue
                    hs = slice((s // 2) * TOPK, (s // 2) * TOPK + 8), slice((s // 2) * TOPK + 8, (s // 2 + 1) * TOPK)
                    for b in range(BLOCKS):
                        first = top_s[:, b, s - 1, :].unsqueeze(2).to_broadcast([P, TOPK, TOPK])
                        second = top_s[:, b, s, :].unsqueeze(1).to_broadcast([P, TOPK, TOPK])
                        step(dve.tensor_tensor(cand[:, b, :].rearrange("p (i j) -> p i j", i=TOPK), first, second, ALU.add))
                    for b in range(BLOCKS):
                        step(dve.max(cand_s[:, b, hs[0]], cand[:, b, :]))
                    for b in range(BLOCKS):
                        step(dve.match_replace(cand2[:, b, :], cand_s[:, b, hs[0]], cand[:, b, :], FAR))
                    for b in range(BLOCKS):
                        step(dve.max(cand_s[:, b, hs[1]], cand2[:, b, :]))
                    for b in range(BLOCKS):
                        step(dve.max_index(cand_i[:, b, hs[0]], cand_s[:, b, hs[0]], cand[:, b, :]))
                    for b in range(BLOCKS):
                        step(dve.max_index(cand_i[:, b, hs[1]], cand_s[:, b, hs[1]], cand2[:, b, :]))
                if span:
                    final(span - 1)
                dve.wait_ge(score_mm, span * SIDES + SIDES)
                kview = lambda ap: ap.rearrange("p (h k) -> p h k", h=HEADS)
                for b in range(BLOCKS):
                    top = cand_s[:, b, 0:PICKS:TOPK].unsqueeze(2).to_broadcast([P, HEADS, TOPK])
                    step(dve.tensor_tensor(kview(g_e), kview(cand_s[:, b, :]), top, ALU.subtract))
                    step(dve.tensor_copy(top_f, top_i[:, b, :, :].rearrange("p s k -> p (s k)")))
                    for half, dst in ((0, e_1), (1, e_2)):
                        if half == 0:
                            step(dve.tensor_scalar(sl_u, cand_i[:, b, :], 4, None, ALU.logical_shift_right))
                        else:
                            step(dve.tensor_scalar(sl_u, cand_i[:, b, :], TOPK - 1, None, ALU.bitwise_and))
                        step(dve.tensor_copy(sl_f, sl_u))
                        step(dve.tensor_tensor(hot.rearrange("p (n j) -> p n j", j=TOPK),
                                               sl_f.unsqueeze(2).to_broadcast([P, PICKS, TOPK]),
                                               c_("iota16").unsqueeze(1).to_broadcast([P, PICKS, TOPK]), ALU.is_equal))
                        part = top_f.rearrange("p (h c j) -> p h c j", h=HEADS, c=2)[:, :, half, :]\
                            .unsqueeze(2).to_broadcast([P, HEADS, TOPK, TOPK])
                        step(dve.tensor_tensor(hot_v.rearrange("p (h k j) -> p h k j", h=HEADS, k=TOPK),
                                               hot.rearrange("p (h k j) -> p h k j", h=HEADS, k=TOPK), part, ALU.mult))
                        step(dve.tensor_reduce(dst, hot_v.rearrange("p (n j) -> p n j", j=TOPK), AX_X, ALU.add))
                    step(dve.scalar_tensor_tensor(out=pick_i[:, b, :], in0=e_1, scalar=float(NKEYS), in1=e_2,
                                                  op0=ALU.mult, op1=ALU.add))
                    dve.wait_ge(pick_act, span * BLOCKS + b + 1)
                    step(dve.tensor_reduce(g_s, kview(g_e), AX_X, ALU.add))
                    step(dve.reciprocal(g_r, g_s))
                    step(dve.tensor_tensor(kview(gates[:, b, :]), kview(g_e),
                                           g_r.unsqueeze(2).to_broadcast([P, HEADS, TOPK]), ALU.mult))
                assert step.count[0] == (span + 1) * PICK_SPAN
            rows(BLOCKS * PICKS)
            gelus(SPANS - 1)
            rows(BLOCKS * PICKS)
            final(SPANS - 1)

        @block.gpsimd
        def _(pool):
            for span in range(SPANS):
                rows = span * BLOCKS * 2 * PICKS
                for table in ("peer_u", "peer_v"):
                    for b in range(BLOCKS):
                        if table == "peer_u":
                            pool.wait_ge(pick, picked(span, b, "expert"))
                        for k in range(PICKS):
                            slot = rows % GATHERS
                            if rows >= GATHERS:
                                pool.wait_ge(row_used, rows - GATHERS + 1)
                            pool.indirect_dma_start(gath[:, slot, :], None, A[table],
                                                    bass.IndirectOffsetOnAxis(ap=pick_i[:, b, k:k + 1], axis=0))\
                                .then_inc(gathered[slot], 16)
                            rows += 1


def _layouts(inp):
    import numpy as np

    f = np.float32

    def col(a, n):
        return np.asarray(a, f).reshape(n, P).T

    def tiles(w, cols):
        w = np.asarray(w, f).reshape(KT, P, -1, P)[:, :, cols, :]
        return np.ascontiguousarray(w.transpose(2, 1, 0, 3)).reshape(len(cols), P, D)

    order = [g * PAIRS + h for h in range(PAIRS) for g in range(3)]
    order += [3 * PAIRS + g * CONVS + t for t in range(CONVS) for g in (1, 2, 0)]
    vecs = {"norm_mix": col(inp["norm_mix"], KT), "mu_rkv": col(inp["mu_rkv"], 3 * PAIRS), "w0": col(inp["w0"], PAIRS),
            "a0": col(inp["a0"], PAIRS), "k_k": col(inp["k_k"], PAIRS), "k_a": col(inp["k_a"], PAIRS),
            "r_k": col(inp["r_k"], PAIRS), "gn_w": col(inp["gn_w"], PAIRS), "gn_b": col(inp["gn_b"], PAIRS),
            "conv_w": col(inp["conv_w"], 3 * CONVS), "mu_lora": col(inp["mu_lora"], 3 * KT),
            "eps": np.tile(np.array([[RMS_EPS, GN_EPS]], f), (P, 1))}
    lora = np.concatenate([np.asarray(inp[n], f)[0] for n in ("w1", "a1", "g1")], axis=1)
    g2 = np.asarray(inp["g2"], f)[0]
    g2p = np.zeros((P, D), f)
    g2p[:, :D_RWKV] = g2[:P]
    g2p[:LORA_G - P, D_RWKV:] = g2[P:]
    keys = np.asarray(inp["peer_keys"], f)[0].reshape(SIDES, NKEYS, 2, P).transpose(3, 0, 2, 1)

    i = np.arange(CHUNK)
    s_, t_ = np.meshgrid(i, i, indexing="ij")

    def low(l):
        return ((s_ >> (l + 1) == t_ >> (l + 1)) & (s_ >> l & 1 == 1) & (t_ >> l & 1 == 0)).astype(f)

    two = lambda m: np.tile(m.astype(f), (2, 1))
    head = np.kron(np.eye(2), np.ones((HALF, HALF)))
    cons = {"ident": np.eye(P), "head_ones": head, "head_mean": head / HALF, "eye": two(np.eye(CHUNK)),
            "before": two(s_ < t_), "upto": two(s_ <= t_), "low0": two(low(0)),
            "up": np.concatenate([two(low(l).T) for l in range(LEVELS)], axis=1),
            "keep": np.tile((np.arange(SPAN) % CHUNK != 0)[None], (P, 1)), "iota16": np.tile(np.arange(TOPK)[None], (P, 1))}
    return {
        "x": np.asarray(inp["x"], f).reshape(T, D),
        "vecs": np.ascontiguousarray(np.concatenate([vecs[n] for n in VEC], axis=1)),
        "consts": np.ascontiguousarray(np.concatenate([cons[n].astype(f) for n in CON], axis=1)),
        "w_in": tiles(np.asarray(inp["w_in"])[0], order),
        "lora_in": np.ascontiguousarray(lora.reshape(KT, P, LORA).transpose(1, 0, 2)),
        "w2a2": np.ascontiguousarray(np.concatenate([np.asarray(inp["w2"], f)[0], np.asarray(inp["a2"], f)[0]])),
        "g2": g2p,
        "w_out": np.asarray(inp["w_out"], f)[0],
        "norm_ffn": np.asarray(inp["norm_ffn"], f).reshape(D),
        "wq": tiles(np.asarray(inp["peer_wq"])[0], list(range(Q_TILES))),
        "keys": np.ascontiguousarray(keys),
        "peer_u": np.asarray(inp["peer_u"], f)[0],
        "peer_v": np.asarray(inp["peer_v"], f)[0],
        "norm_final": np.asarray(inp["norm_final"], f).reshape(D),
    }


def kernel(**inputs):
    import concourse.bacc as bacc
    from concourse.bass_utils import run_bass_kernel_spmd

    arrays = _layouts(inputs)
    nc = bacc.Bacc("TRN2", target_bir_lowering=False, num_devices=1)
    A = {n: nc.dram_tensor("in_" + n, a.shape, F32, kind="ExternalInput").ap() for n, a in arrays.items()}
    A["out"] = nc.dram_tensor("out", (T, D), F32, kind="ExternalOutput").ap()
    hymba(nc, A)
    r = run_bass_kernel_spmd(nc, [{"in_" + n: a for n, a in arrays.items()}], core_ids=[0])
    return r.results[0]["out"].reshape(1, T, D)
```

```python
from contextlib import ExitStack

import concourse.bass as bass
from concourse import mybir

F32 = mybir.dt.float32
F32R = mybir.dt.float32r
I32 = mybir.dt.int32
U32 = mybir.dt.uint32
ALU = mybir.AluOpType
ACT = mybir.ActivationFunctionType
AX_X = mybir.AxisListType.X

P = 128
T, D = 512, 2048
SPAN = 256
SPANS = T // SPAN
BLOCKS = SPAN // P
KT = D // P
CHUNK = 64
CHUNKS = SPAN // CHUNK
HALF = 64
D_RWKV = D // 2
PAIRS = D_RWKV // P
CONVS = D_RWKV // P
LEVELS = 6
W_TILES = 6 * PAIRS
LORA_W, LORA_A, LORA_G = 64, 64, 160
LORA = LORA_W + LORA_A + LORA_G
HEADS, HALVES, NKEYS, TOPK = 8, 2, 128, 16
SIDES = HEADS * HALVES
Q_TILES = 2 * SIDES
PICKS = HEADS * TOPK
RMS_EPS, GN_EPS = 1e-6, 64e-5
EXP_M_HALF = 0.6065306597126334
FAR = -3.0e38
GELU_C, GELU_S = 0.044715, 0.7978845608028654
PAD = 2

VEC = {}
for _name, _n in (("norm_mix", KT), ("mu_rkv", 3 * PAIRS), ("w0", PAIRS), ("a0", PAIRS), ("k_k", PAIRS),
                  ("k_a", PAIRS), ("r_k", PAIRS), ("gn_w", PAIRS), ("gn_b", PAIRS), ("conv_w", 3 * CONVS),
                  ("mu_lora", 3 * KT), ("eps", 2)):
    VEC[_name] = (sum(n for _, n in VEC.values()), _n)
N_VEC = sum(n for _, n in VEC.values())
CON = {}
for _name, _n in (("ident", P), ("head_ones", P), ("head_mean", P), ("eye", CHUNK), ("before", CHUNK),
                  ("upto", CHUNK), ("low0", CHUNK), ("up", LEVELS * CHUNK), ("keep", SPAN), ("iota16", TOPK)):
    CON[_name] = (sum(n for _, n in CON.values()), _n)
N_CON = sum(n for _, n in CON.values())

WOUT_K = list(range(PAIRS, KT)) + list(range(PAIRS))
WOUT_HEAD, WOUT_TAIL = 2, 3
WOUT_ORDER = [(i, 1) for i in range(WOUT_HEAD)] + [(i, 0) for i in range(WOUT_HEAD)]
WOUT_ORDER += [(i, b) for i in range(WOUT_HEAD, KT - WOUT_TAIL) for b in range(BLOCKS)]
WOUT_ORDER += [(i, b) for b in range(BLOCKS) for i in range(KT - WOUT_TAIL, KT)]

RING = 3
RING_PER_SPAN = W_TILES + 1 + KT + Q_TILES
GATHERS = 4
ROWS_SPAN = BLOCKS * 2 * PICKS
U = ROWS_SPAN // 2
ROWS = {"norm": 10, "lora": 8, "turn": 8, "low": 14, "head": 40, "conv": 30, "scan": 104,
        "scan_v": 14, "gate": 14, "w_out": 46, "norm2": 24, "side": 196}
POINTS = 4
OWN = [max(0, 3 * (i - POINTS) // 2 + 2) for i in range(HEADS * POINTS)]
assert OWN[-1] + sum(ROWS[n] for n in ("norm", "lora", "turn", "low", "head", "conv", "scan")) == U
assert sum(ROWS[n] for n in ("scan_v", "gate", "w_out", "norm2", "side")) >= U


def row_of(r):
    table, i = divmod(r, U)
    if table == 0:
        h, b, k = i // (BLOCKS * TOPK), i // TOPK % BLOCKS, i % TOPK
        return table, b, h * TOPK + k
    return table, i // PICKS, i % PICKS


class Steps:

    def __init__(self, *names):
        self.names = list(names)

    def __len__(self):
        return len(self.names)

    def after(self, n, name):
        return n * len(self.names) + self.names.index(name) + 1


MIX = Steps("log_decay", "log_prod", "log_prev", "r_step", "r", "k_step", "k", "v_step", "v", "kk_raw", "kk_sq",
            "a_gain", "k_new", "bonus_raw", "R", "K", "p_end", "norm", "inv_norm", "kk", "B", "B_scaled", "A",
            "bonus")
CONV = Steps("u", "tap0", "tap1", "tap2", "gate")
NORM1 = Steps("mean_sq", "inv", "scaled")
NORM2 = Steps("sum0", "sum1", "sum2", "sum3", "mean_sq", "inv", "scaled")
EXPERTS = Steps("numbers", "row", "row_f", "row_hot", "row_part", "row_expert", "col", "col_f", "col_hot", "col_part",
                "col_expert", "expert")
GATES = Steps("shifted", "sum", "inv", "gates")
GELU = Steps("square", "cube", "inner", "half", "coef")
FIN = Steps("mean_sq", "inv", "out")


def scan_order():
    order = []
    for pair in range(CHUNKS // 2):
        both = (2 * pair, 2 * pair + 1)
        for name in ("B_t", "K_t", "V_t", "L_T", "L", "LK_T", "RB_T", "RK_T"):
            order += [(c, name, 0) for c in both]
        for l in range(1, LEVELS):
            for name in ("W", "X", "X_T") if l < LEVELS - 1 else ("W", "X_T"):
                order += [(c, name, l) for c in both]
        c, d = both
        order += [(c, "rhs", 0), (c, "SA", 0), (c, "Y", 0), (c, "dS", 0), (d, "rhs", 0), (c, "mean", 0), (d, "SA", 0),
                  (c, "var", 0), (d, "Y", 0), (d, "dS", 0), (d, "mean", 0)]
    for d in range(1, CHUNKS, 2):
        at = order.index((d, "mean", 0)) + 1
        order.insert(min(at + 4, len(order)), (d, "var", 0))
    return order


ORDER = scan_order()
BY_ACT = ("B_t", "K_t", "V_t", "W", "rhs", "SA", "Y")
ACT_STEPS = [(c, {"mean": "squares", "var": "root"}.get(name, name), l) for c, name, l in ORDER
             if name in BY_ACT + ("mean", "var")]


def dve_ops():
    ops = []
    for c, name, l in ORDER:
        if name in BY_ACT:
            if name == "W" and l < LEVELS - 1:
                ops.append(("mask", c, "M", l + 1))
            continue
        if name == "var":
            ops += [(what, c, name, l) for what in ("inverse", "scaled", "gain", "offset", "bonus")]
            continue
        ops.append(("take", c, name, l))
        if name == "L_T":
            ops += [("mask", c, "M", 0), ("eye", c, "X_T", 0), ("mask", c, "M", 1)]
        elif name == "L":
            ops.append(("eye", c, "L", 0))
        elif name == "dS":
            ops.append(("decay", c, "dS", 0))
    return ops


DVE_OPS = dve_ops()
TERMS = {"rhs": 2, "Y": 3, "dS": 2, "mean": 0, "var": 0}
LAST_STATE = ORDER.index((CHUNKS - 1, "rhs", 0))


def scan_time(k0, k1):
    return sum(TERMS.get(name, 1) for _, name, _ in ORDER[k0:k1])


CONV_TILES = 3 * CONVS
FIRST_TILES = 3


def tiles_first(span):
    return CONV_TILES if span else FIRST_TILES


def quarters_after(span, k):
    total, steps = 4 * (CONV_TILES - tiles_first(span)), len(ORDER) - 8
    return range(min(k, steps) * total // steps, min(k + 1, steps) * total // steps)


FIRST_SPLIT = 3
HI_SLOTS = 3
X_PIECES = ((0, 4), (4, 8), (8, 12), (12, 15), (15, 16))


def splits_due(k, quarters):
    done = quarters_after(0, k - 1).stop if k else 0
    return min(3 * PAIRS + FIRST_TILES - 1 + (done + quarters) // 4 + 3, W_TILES)


def tiles_done(span, k):
    return tiles_first(span) + (quarters_after(span, k - 1).stop // 4 if k else 0)


def hymba(nc, A):
    with ExitStack() as ctx:
        def sb(name, shape, dt=F32):
            return ctx.enter_context(nc.sbuf_tensor(name, shape, dt))

        def sem(name):
            return ctx.enter_context(nc.semaphore(name))

        S_COLS = 33 * CHUNK * PAIRS
        with ExitStack() as views:
            hT_r, _, yT_r, ring_r, gath_r, acc_r, h2_r, S_r = (
                views.enter_context(nc.sbuf_tensor(name, shape, F32R)) for name, shape in (
                    ("hT_r", [P, KT * (PAD + SPAN)]), ("h_pad_r", [P, KT, PAD]), ("yT_r", [P, KT, SPAN]),
                    ("ring_r", [P, RING, D]), ("gath_r", [P, GATHERS, D]), ("acc_r", [P, BLOCKS, D]),
                    ("h2_r", [P, BLOCKS, D]), ("S_r", [P, S_COLS])))
        hT = sb("hT", [P, KT * (PAD + SPAN)])
        hT_v = hT[:, :].rearrange("p (k t) -> p k t", k=KT)
        h_pad = sb("h_pad", [P, KT, PAD])
        yT = sb("yT", [P, KT, SPAN])
        ring = sb("ring", [P, RING, D])
        gath = sb("gath", [P, GATHERS, D])
        acc = sb("acc", [P, BLOCKS, D])
        h2 = sb("h2", [P, BLOCKS, D])
        S = sb("S", [P, S_COLS])
        w2a2 = sb("w2a2", [P, D_RWKV])
        vec = sb("vec", [P, N_VEC])
        con = sb("con", [P, N_CON])
        wa_in = sb("wa_in", [P, SPAN])
        g_in = sb("g_in", [P, 2, SPAN])
        state = sb("state", [P, 2, PAIRS * CHUNK])
        ssq = sb("ssq", [P, 8])
        rstd = sb("rstd", [P, 8])
        pick_i = sb("pick_i", [P, 2, BLOCKS, PICKS], I32)
        gates = sb("gates", [P, BLOCKS, PICKS])
        dots = sb("dots", [P, BLOCKS, PICKS])
        gel = sb("gel", [P, PICKS])
        p_end = sb("p_end", [P, PAIRS, CHUNKS])
        banks = [ctx.enter_context(nc.psum_tensor(f"bank{i}", [P, 512], F32)) for i in range(8)]

        def v(name, i, n=1):
            return vec[:, VEC[name][0] + i:VEC[name][0] + i + n]

        def c_(name, i=0, n=None):
            o, w = CON[name]
            return con[:, o + i:o + i + (w if n is None else n)]

        ident = c_("ident")

        x_in = S[:, 0:BLOCKS * D].rearrange("p (b d) -> p b d", b=BLOCKS)
        lora_cur = S[:, BLOCKS * D:BLOCKS * D + KT * LORA].rearrange("p (k n) -> p k n", k=KT)
        lora_prev = S[:, BLOCKS * D + KT * LORA:BLOCKS * D + 2 * KT * LORA].rearrange("p (k n) -> p k n", k=KT)
        chan = [S[:, i * PAIRS * SPAN:(i + 1) * PAIRS * SPAN].rearrange("p (h t) -> p h t", h=PAIRS)
                for i in range(5)]
        R_c, A_c, B_c, K_c, bonus = chan
        BUF = PAIRS * CHUNK
        wide = [S[:, 5 * PAIRS * SPAN + i * BUF:5 * PAIRS * SPAN + (i + 1) * BUF] for i in range(13)]
        spare = [hT[:, i * BUF:(i + 1) * BUF] for i in range(8)]
        tmp0 = 5 * PAIRS * SPAN
        WID = PAD + SPAN
        TMP = [S[:, tmp0 + i * WID:tmp0 + (i + 1) * WID] for i in range(24)]
        raw = [[TMP[3 * (i % 2) + j] for j in range(3)] for i in range(2)]
        sig_w, sig_a = TMP[6][:, 0:SPAN], TMP[7][:, 0:SPAN]
        lw, lp, lm = (TMP[8 + i][:, 0:SPAN] for i in range(3))
        diff, r_s, k_s, kk_raw, kk_sq, a_gain, k_new, rk = (TMP[11 + i][:, 0:SPAN] for i in range(8))
        e_p, e_n, e_m = (TMP[19 + i][:, 0:SPAN] for i in range(3))
        nrm, kk = TMP[22][:, 0:SPAN], TMP[23][:, 0:SPAN]
        c_raw, u_c, conv_o = TMP[0], TMP[1], [TMP[2 + i][:, 0:SPAN] for i in range(3)]

        def chunk_buffers(span):
            if span:
                return spare + wide
            return [gath[:, i // 4, i % 4 * BUF:(i % 4 + 1) * BUF] for i in range(4 * (GATHERS - 1))] + wide[3:12]

        w_hi_r = [h2_r[:, 0, :], h2_r[:, 1, :], gath_r[:, GATHERS - 1, :]]
        def x_hi_r(k0, k1):
            if k0 == KT - 1:
                return S_r[:, S_COLS - WID:S_COLS]
            return acc_r[:, :, :].rearrange("p b d -> p (b d)")[:, k0 * WID:k1 * WID]

        y_hi_r = acc_r[:, :, :].rearrange("p b d -> p (b d)").rearrange("p (k t) -> p k t", k=KT)

        def out_hi_r(i):
            return gath_r[:, (i + GATHERS - 1) % GATHERS, :]

        N_SPLIT = W_TILES - FIRST_SPLIT
        Y_PIECES = [(PAIRS, KT)] + [(2 * i, 2 * i + 2) for i in range(PAIRS // 2)]

        x_mid = S[:, 0:BLOCKS * D].rearrange("p (b d) -> p b d", b=BLOCKS)
        gain_f = S[:, BLOCKS * D:(BLOCKS + 1) * D]
        keys = S[:, (BLOCKS + 1) * D:(BLOCKS + 3) * D].rearrange("p (s k n) -> p s k n", s=SIDES, k=2)
        q0 = (BLOCKS + 3) * D
        q_T = [S[:, q0 + i * SPAN:q0 + (i + 1) * SPAN] for i in range(4)]
        sc = [S[:, q0 + 4 * SPAN + i * SPAN:q0 + 4 * SPAN + (i + 1) * SPAN].rearrange("p (b n) -> p b n", b=BLOCKS)
              for i in range(2)]
        t0 = q0 + 6 * SPAN

        def take(n):
            nonlocal t0
            t0 += n
            return S[:, t0 - n:t0]

        top_s = take(BLOCKS * SIDES * TOPK).rearrange("p (b s k) -> p b s k", b=BLOCKS, s=SIDES)
        top_i = take(BLOCKS * SIDES * TOPK).bitcast(U32).rearrange("p (b s k) -> p b s k", b=BLOCKS, s=SIDES)
        cand_s = take(BLOCKS * PICKS).rearrange("p (b n) -> p b n", b=BLOCKS)
        cand_i = take(BLOCKS * PICKS).bitcast(U32).rearrange("p (b n) -> p b n", b=BLOCKS)
        rest = take(BLOCKS * NKEYS).rearrange("p (b n) -> p b n", b=BLOCKS)
        cand = take(BLOCKS * TOPK * TOPK).rearrange("p (b n) -> p b n", b=BLOCKS)
        cand2 = take(BLOCKS * TOPK * TOPK).rearrange("p (b n) -> p b n", b=BLOCKS)
        N_HOT = BLOCKS * TOPK * TOPK
        hot, hot_v = take(N_HOT), take(N_HOT)
        top_f = take(BLOCKS * 2 * TOPK)
        sl_u, sl_f = take(BLOCKS * TOPK).bitcast(U32), take(BLOCKS * TOPK)
        e_1, e_2 = take(BLOCKS * TOPK), take(BLOCKS * TOPK)
        g_e = take(BLOCKS * PICKS)
        g_s, g_r = take(BLOCKS * HEADS), take(BLOCKS * HEADS)
        assert t0 <= S_COLS

        fin_junk = yT[:, 0:KT // 2, :]
        gain_last = yT[:, KT // 2:KT, :].rearrange("p k t -> p (k t)")

        consts_in = sem("consts_in")
        x_loaded = [sem(f"x_loaded{b}") for b in range(BLOCKS)]
        lora_loaded = sem("lora_loaded")
        ring_ready = [sem(f"ring_ready{i}") for i in range(RING)]
        ring_used = sem("ring_used")
        norm_act, norm_dve = sem("norm_act"), sem("norm_dve")
        turned = sem("turned")
        turned_out = sem("turned_out")
        lora_split = sem("lora_split")
        lora_mm, lora_act = sem("lora_mm"), sem("lora_act")
        tile_out = sem("tile_out")
        z_mm, z_act = sem("z_mm"), sem("z_act")
        exp_act = sem("exp_act")
        mix = sem("mix")
        sums_mm, sqrt_act = sem("sums_mm"), sem("sqrt_act")
        conv = sem("conv")
        pad_set, pad_saved = sem("pad_set"), sem("pad_saved")
        scan_mm, scan_act, scan_dve = sem("scan_mm"), sem("scan_act"), sem("scan_dve")
        gate_mm = sem("gate_mm")
        gated = sem("gated")
        wout_mm = sem("wout_mm")
        res_loaded = sem("res_loaded")
        keys_loaded = sem("keys_loaded")
        norm2_act, norm2_dve = sem("norm2_act"), sem("norm2_dve")
        turned2, turned2_out = sem("turned2"), sem("turned2_out")
        score_mm, score_out = sem("score_mm"), sem("score_out")
        pick = sem("pick")
        pick_act = sem("pick_act")
        gathered = [sem(f"gathered{i}") for i in range(GATHERS)]
        row_used = sem("row_used")
        gelu, gelu_act = sem("gelu"), sem("gelu_act")
        fin_dve, fin_act = sem("fin_dve"), sem("fin_act")
        fin_gain = sem("fin_gain")
        acc_set = sem("acc_set")
        stored = sem("stored")
        zeroed = sem("zeroed")
        w_hi_made, w_lo_made = sem("w_hi_made"), sem("w_lo_made")
        y_hi_made, y_lo_made = sem("y_hi_made"), sem("y_lo_made")
        x_hi_made, x_lo_made = sem("x_hi_made"), sem("x_lo_made")

        NB8 = BLOCKS * 4
        TK_SIDE = 5 * BLOCKS
        TK_HEAD = 6 * BLOCKS + len(EXPERTS)
        TK_SPAN = SIDES * TK_SIDE + HEADS * TK_HEAD
        PICK_SPAN = TK_SPAN + len(GATES)
        ACT_TILES = 3 * PAIRS + CONVS + Q_TILES

        def head_picked(span, h):
            return span * PICK_SPAN + (h + 1) * (2 * TK_SIDE + TK_HEAD)

        def tile_taken(span, i):
            if i < 3 * PAIRS:
                return tile_out, span * ACT_TILES + i + 1
            if i < W_TILES:
                t, j = divmod(i - 3 * PAIRS, 3)
                if j == 0:
                    return tile_out, span * ACT_TILES + 3 * PAIRS + t + 1
                return conv, CONV.after(span * CONVS + t, "u" if j == 1 else "gate")
            return tile_out, span * ACT_TILES + 3 * PAIRS + CONVS + (i - W_TILES) + 1

        def side_after(span, side):
            return span * PICK_SPAN + (side + 1) * TK_SIDE + (side // 2) * TK_HEAD

        def scan_done(span, c, name, l=0):
            if (c, name, l) in ACT_STEPS:
                return scan_act, span * len(ACT_STEPS) + ACT_STEPS.index((c, name, l)) + 1
            return scan_dve, span * len(DVE_OPS) + max(i for i, o in enumerate(DVE_OPS) if o[1:] == (c, name, l)) + 1

        def scan_bank(span, i):
            c, name, l = ORDER[i]
            return scan_done(span, c, "root" if name == "var" else name, l)

        GATED = PAIRS // 2

        def ring_item(span, i):
            m = span * RING_PER_SPAN + i
            return m, m % RING, 16 * (m // RING + 1)

        block = ctx.enter_context(nc.Block())

        @block.sync
        def _(sp):
            def gain_and_store(span, front):
                sp.wait_ge(ring_used, front * RING_PER_SPAN + W_TILES + 1 + KT)
                sp.dma_start(gain_last, A["norm_final"].partition_broadcast(P)).then_inc(fin_gain, 16)
                for b in range(BLOCKS):
                    n = span * BLOCKS + b
                    sp.wait_ge(fin_dve, FIN.after(n, "out"))
                    sp.dma_start(A["out"][n * P:(n + 1) * P, :], acc[:, b, :]).then_inc(stored, 16)

            for span in range(SPANS):
                rows = slice(span * SPAN, (span + 1) * SPAN)
                if span:
                    sp.wait_ge(acc_set, span * BLOCKS)
                xs = A["x"][rows, :].rearrange("(b p) d -> b p d", p=P)
                for b in range(BLOCKS):
                    sp.dma_start(x_in[:, b, :], xs[b]).then_inc(x_loaded[b], 16)
                if span == 0:
                    sp.dma_start(con[:, :], A["consts"]).then_inc(consts_in, 16)
                    sp.dma_start(vec[:, :], A["vecs"]).then_inc(consts_in, 16)
                    sp.dma_start(w2a2[:, :], A["w2a2"]).then_inc(consts_in, 16)
                if span:
                    sp.wait_ge(score_mm, span * SIDES)
                sp.dma_start(lora_cur, A["lora_in"]).then_inc(lora_loaded, 16)
                for i in range(W_TILES):
                    m, slot, _ = ring_item(span, i)
                    if m >= RING:
                        sp.wait_ge(ring_used, m - RING + 1)
                    sp.dma_start(ring[:, slot, :], A["w_in"][i]).then_inc(ring_ready[slot], 16)
                m, slot, _ = ring_item(span, W_TILES)
                sp.wait_ge(ring_used, m - RING + 1)
                sp.dma_start(ring[:, slot, :], A["g2"]).then_inc(ring_ready[slot], 16)
                for i, k in enumerate(WOUT_K):
                    m, slot, _ = ring_item(span, W_TILES + 1 + i)
                    sp.wait_ge(ring_used, m - RING + 1)
                    sp.dma_start(ring[:, slot, :], A["w_out"][k * P:(k + 1) * P, :]).then_inc(ring_ready[slot], 16)
                    if i == 3:
                        sp.wait_ge(gated, (span + 1) * GATED)
                    if i in (3, 5):
                        b = (i - 3) // 2
                        sp.dma_start(x_mid[:, b, :], xs[b]).then_inc(res_loaded, 16)
                    if i == 8:
                        sp.dma_start(gain_f, A["norm_ffn"].partition_broadcast(P)).then_inc(res_loaded, 16)
                for i in range(Q_TILES):
                    m, slot, _ = ring_item(span, W_TILES + 1 + KT + i)
                    sp.wait_ge(ring_used, m - RING + 1)
                    sp.dma_start(ring[:, slot, :], A["wq"][i]).then_inc(ring_ready[slot], 16)
                    if i == 0:
                        sp.dma_start(keys, A["keys"]).then_inc(keys_loaded, 16)
                if span:
                    gain_and_store(span - 1, span)
            gain_and_store(SPANS - 1, SPANS - 1)
            sp.wait_ge(stored, 16 * SPANS * BLOCKS)

        @block.tensor
        def _(pe):
            pe.wait_ge(consts_in, 48)

            def tile(span, i, item, rhs, n, k0=0, k1=KT):
                _, slot, ready = ring_item(span, item)
                split = span == 0 and FIRST_SPLIT <= item < W_TILES
                if k0 == 0:
                    if i >= 4:
                        pe.wait_ge(*tile_taken(span, i - 4))
                    if split:
                        pe.wait_ge(w_lo_made, item - FIRST_SPLIT + 1)
                    else:
                        pe.wait_ge(ring_ready[slot], ready)
                if split and item == FIRST_SPLIT:
                    pe.wait_ge(x_lo_made, len(X_PIECES))
                for k in range(k0, k1):
                    if split:
                        out, hi, x = banks[i % 4][:, 0:WID], w_hi_r[item % HI_SLOTS][:, k * P:(k + 1) * P], x_hi_r(k, k + 1)
                        pe.matmul(out, hi, x, start=(k == 0), stop=False)
                        pe.matmul(out, hi, hT_r[:, k * WID:(k + 1) * WID], start=False, stop=False)
                        mm = pe.matmul(out, ring_r[:, slot, k * P:(k + 1) * P], x, start=False, stop=(k == KT - 1))
                        continue
                    mm = pe.matmul(banks[i % 4][:, 0:n], ring[:, slot, k * P:(k + 1) * P], rhs(k),
                                   start=(k == 0), stop=(k == KT - 1))
                if k1 == KT:
                    mm.then_inc(ring_used, 1)

            def turn(src, sem_in, ready, done):
                for n in range(NB8):
                    b, k4 = divmod(n, 4)
                    if k4 == 0:
                        pe.wait_ge(sem_in, ready(b))
                    for j in range(4):
                        k = 4 * k4 + j
                        mm = pe.transpose(banks[n][:, j * P:(j + 1) * P], src[:, b, k * P:(k + 1) * P], ident)
                    mm.then_inc(done, 1)

            def pair_mm(bank, lhsT, rhs, terms=1):
                for h in range(PAIRS):
                    for q in range(2):
                        rows = slice(q * HALF, (q + 1) * HALF)
                        for i in range(terms):
                            mm = pe.matmul(bank[rows, h * CHUNK:(h + 1) * CHUNK], lhsT[i](h)[rows, :],
                                           rhs[i](h, q)[rows, :], start=(i == 0), stop=(i == terms - 1))
                return mm

            def gate_sums(span):
                _, g_slot, g_ready = ring_item(span, W_TILES)
                pe.wait_ge(ring_ready[g_slot], g_ready)
                for i in range(4):
                    pe.wait_ge(*tile_taken(span, W_TILES - 1 - i))
                for h in range(PAIRS):
                    out = banks[h // 2][:, h % 2 * SPAN:(h % 2 + 1) * SPAN]
                    pe.matmul(out, ring[:, g_slot, h * P:(h + 1) * P], g_in[:, 0, :], start=True, stop=False)
                    mm = pe.matmul(out, ring[0:32, g_slot, D_RWKV + h * P:D_RWKV + (h + 1) * P], g_in[0:32, 1, :],
                                   start=False, stop=True)
                    if h % 2:
                        mm.then_inc(gate_mm, 1)

            for span in range(SPANS):
                if span:
                    pe.wait_ge(*tile_taken(span - 1, W_TILES + Q_TILES - 1))
                    pe.wait_ge(score_out, span * SIDES)
                turn(x_in, norm_dve, lambda b: NORM1.after(span * BLOCKS + b, "scaled"), turned)

                pe.wait_ge(turned_out, NB8 * (span + 1))
                pe.wait_ge(pad_set, span + 1)
                for j in range(3):
                    tile(span, j, j, lambda k: hT_v[:, k, :], WID)

                pe.wait_ge(lora_split, 4 * (span + 1))
                for n, (c0, c1) in enumerate(((0, P), (P, 2 * P), (2 * P, LORA))):
                    out = banks[4 + n][0:c1 - c0, 0:SPAN]
                    for k in range(KT):
                        pe.matmul(out, lora_cur[:, k, c0:c1], hT_v[:, k, PAD:PAD + SPAN], start=(k == 0), stop=False)
                        mm = pe.matmul(out, lora_prev[:, k, c0:c1], hT_v[:, k, PAD - 1:PAD - 1 + SPAN],
                                       start=False, stop=(k == KT - 1))
                    mm.then_inc(lora_mm, 1)

                def sums(h):
                    n = span * PAIRS + h
                    pe.wait_ge(mix, MIX.after(n, "bonus_raw"))
                    if n >= 1:
                        pe.wait_ge(mix, MIX.after(n - 1, "bonus"))
                    pe.matmul(banks[5][:, 0:SPAN], c_("head_ones"), kk_sq, start=True, stop=True)
                    pe.matmul(banks[6][:, 0:SPAN], c_("head_ones"), rk, start=True, stop=True).then_inc(sums_mm, 1)

                pe.wait_ge(lora_act, 4 * (span + 1))
                for h in range(PAIRS):
                    n = span * PAIRS + h
                    zb = banks[4 if h % 2 else 7]
                    if h >= 2:
                        pe.wait_ge(z_act, 2 * (n - 1))
                    pe.matmul(zb[:, 0:SPAN], w2a2[0:HALF, h * P:(h + 1) * P], wa_in[0:HALF, :],
                              start=True, stop=True).then_inc(z_mm, 1)
                    pe.wait_ge(z_mm, 2 * n + 1)
                    pe.matmul(zb[:, SPAN:2 * SPAN], w2a2[HALF:P, h * P:(h + 1) * P], wa_in[HALF:P, :],
                              start=True, stop=True).then_inc(z_mm, 1)
                    for j in range(3 if h else 0):
                        tile(span, 3 * h + j, 3 * h + j, lambda k: hT_v[:, k, :], WID)
                        if j == 0:
                            sums(h - 1)
                for i in range(tiles_first(span)):
                    tile(span, 3 * PAIRS + i, 3 * PAIRS + i, lambda k: hT_v[:, k, :], WID)
                    if i == 0:
                        sums(PAIRS - 1)

                bufs = chunk_buffers(span)
                B_t, K_t, V_t, L_T, LK_T, X, X_T, W_b, M_b = ([bufs[9 * q + i] for q in range(2)] for i in range(9))
                rhs_b, SA_b, _ = bufs[18:21]
                pe.wait_ge(mix, MIX.after(span * PAIRS + PAIRS - 1, "bonus"))
                if span:
                    pe.wait_ge(conv, CONV.after(span * CONVS + CONVS - 1, "gate"))
                for i, (c, name, l) in enumerate(ORDER):
                    q = c % 2
                    n = span * CHUNKS + c
                    ts = slice(c * CHUNK, (c + 1) * CHUNK)
                    bank = banks[4 + i % 4]
                    if i >= 4:
                        pe.wait_ge(*scan_bank(span, i - 4))
                    if (c, name) == (CHUNKS - 1, "var"):
                        gate_sums(span)

                    def cols(buf):
                        return lambda h, _=0: buf[:, h * CHUNK:(h + 1) * CHUNK]

                    def chn(buf):
                        return lambda h, _=0: buf[:, h, ts]

                    def eye(h, par):
                        return con[:, CON["ident"][0] + par * HALF:CON["ident"][0] + (par + 1) * HALF]

                    if name == "B_t":
                        mm = pair_mm(bank, [chn(B_c)], [eye])
                    elif name == "K_t":
                        mm = pair_mm(bank, [chn(K_c)], [eye])
                    elif name == "V_t":
                        mm = pair_mm(bank, [chn(yT)], [eye])
                    elif name == "L_T":
                        mm = pair_mm(bank, [chn(B_c)], [chn(A_c)])
                    elif name == "L":
                        mm = pair_mm(bank, [chn(A_c)], [chn(B_c)])
                    elif name == "LK_T":
                        mm = pair_mm(bank, [chn(K_c)], [chn(A_c)])
                    elif name == "RB_T":
                        mm = pair_mm(bank, [chn(B_c)], [chn(R_c)])
                    elif name == "RK_T":
                        mm = pair_mm(bank, [chn(K_c)], [chn(R_c)])
                    elif name == "W":
                        pe.wait_ge(*scan_done(span, c, "M", l))
                        pe.wait_ge(*scan_done(span, c, "X" if l > 1 else "L", l - 1 if l > 1 else 0))
                        mm = pair_mm(bank, [cols(M_b[q])], [cols(X[q])])
                    elif name == "X":
                        pe.wait_ge(*scan_done(span, c, "W", l))
                        if l > 1:
                            pe.wait_ge(*scan_done(span, c, "X_T", l - 1))
                        mm = pair_mm(bank, [cols(X_T[q])], [cols(W_b[q])])
                    elif name == "X_T":
                        pe.wait_ge(*scan_done(span, c, "W", l))
                        if l > 1:
                            pe.wait_ge(*scan_done(span, c, "X_T", l - 1))
                        mm = pair_mm(bank, [cols(W_b[q])], [cols(X_T[q])])
                    elif name == "rhs":
                        if c:
                            pe.wait_ge(*scan_done(span, c - 1, "dS"))
                        pe.wait_ge(*scan_done(span, c, "LK_T"))
                        pe.wait_ge(*scan_done(span, c, "V_t"))
                        mm = pair_mm(bank, [chn(A_c), cols(LK_T[q])], [cols(state[:, n % 2, :]), cols(V_t[q])], 2)
                    elif name == "SA":
                        pe.wait_ge(*scan_done(span, c, "rhs"))
                        pe.wait_ge(*scan_done(span, c, "X_T", LEVELS - 1))
                        mm = pair_mm(bank, [cols(X_T[q])], [cols(rhs_b)])
                    elif name == "Y":
                        pe.wait_ge(*scan_done(span, c, "SA"))
                        mm = pair_mm(bank, [cols(state[:, n % 2, :]), cols(SA_b), cols(V_t[q])],
                                     [chn(R_c), chn(B_c), chn(K_c)], 3)
                    elif name == "dS":
                        mm = pair_mm(bank, [cols(B_t[q]), cols(K_t[q])], [cols(SA_b), cols(V_t[q])], 2)
                    elif name == "mean":
                        pe.wait_ge(*scan_done(span, c, "Y"))
                        mm = pe.matmul(bank[:, :], c_("head_mean"), yT[:, 0:PAIRS, ts], start=True, stop=True)
                    elif name == "var":
                        pe.wait_ge(*scan_done(span, c, "squares"))
                        mm = pe.matmul(bank[:, :], c_("head_mean"), W_b[q], start=True, stop=True)
                    mm.then_inc(scan_mm, 1)
                    for part in quarters_after(span, i):
                        t, k4 = 3 * PAIRS + tiles_first(span) + part // 4, part % 4 * KT // 4
                        tile(span, t, t, lambda k: hT_v[:, k, :], WID, k4, k4 + KT // 4)

                pe.wait_ge(*scan_done(span, CHUNKS - 1, "dS"))
                pe.wait_ge(*scan_done(span, CHUNKS - 1, "root"))
                for at, (i, b) in enumerate(WOUT_ORDER):
                    k = WOUT_K[i]
                    _, slot, ready = ring_item(span, W_TILES + 1 + i)
                    if span:
                        pe.wait_ge(ring_ready[slot], ready)
                    else:
                        pe.wait_ge(w_lo_made, N_SPLIT + i + 1)
                        pe.wait_ge(y_lo_made, 1 if k >= PAIRS else len(Y_PIECES))
                    if at == WOUT_HEAD:
                        pe.wait_ge(gated, (span + 1) * GATED)
                    for n in range(4):
                        out, ts, cs = banks[4 * b + n][:, :], slice(b * P, (b + 1) * P), slice(n * 512, (n + 1) * 512)
                        y, w = yT[:, k, ts], ring[:, slot, cs]
                        if span:
                            mm = pe.matmul(out, y, w, start=(i == 0), stop=(i == KT - 1))
                        else:
                            mm = pe.matmul(out, y_hi_r[:, k, ts], out_hi_r(i)[:, cs], start=(i == 0), stop=False)
                            pe.matmul(out, y_hi_r[:, k, ts], ring_r[:, slot, cs], start=False, stop=False)
                            last = pe.matmul(out, yT_r[:, k, ts], out_hi_r(i)[:, cs], start=False, stop=(i == KT - 1))
                        if at == 0 and n == 0:
                            mm.then_inc(ring_used, 1)
                    if span == 0:
                        mm = last
                    if (i, b) == (KT - 1, 0):
                        mm.then_inc(wout_mm, 1)
                    elif at > WOUT_ORDER.index((i, 1 - b)):
                        mm.then_inc(ring_used, 1)

                turn(h2, norm2_dve, lambda b: NORM2.after(span * BLOCKS + b, "scaled"), turned2)

                def scores(s):
                    n = span * SIDES + s
                    pe.wait_ge(keys_loaded, 16 * (span + 1))
                    pe.wait_ge(*tile_taken(span, W_TILES + 2 * s + 1))
                    if s >= 2:
                        pe.wait_ge(score_out, n - 1)
                    for b in range(BLOCKS):
                        for j in range(2):
                            mm = pe.matmul(banks[4 + s % 2][:, b * P:(b + 1) * P], q_T[(2 * s + j) % 4][:, b * P:(b + 1) * P],
                                           keys[:, s, j, :], start=(j == 0), stop=(j == 1))
                    mm.then_inc(score_mm, 1)

                pe.wait_ge(turned2_out, NB8 * (span + 1))
                for i in range(Q_TILES):
                    tile(span, W_TILES + i, W_TILES + 1 + KT + i, lambda k: hT_v[:, k, PAD:PAD + SPAN], SPAN)
                    if i % 2 == 0 and i:
                        scores(i // 2 - 1)
                scores(SIDES - 1)

        @block.scalar
        def _(act):
            def gelu_tanhs(span):
                for b in range(BLOCKS):
                    n = span * BLOCKS + b
                    act.wait_ge(gelu, GELU.after(n, "inner"))
                    act.activation(gel[:, :], gel[:, :], ACT.Tanh, scale=GELU_S).then_inc(gelu_act, 1)

            def final_roots(span):
                for b in range(BLOCKS):
                    n = span * BLOCKS + b
                    act.wait_ge(row_used, span * ROWS_SPAN + (BLOCKS + b + 1) * PICKS)
                    if b:
                        act.wait_ge(fin_act, 2 * n)
                    act.activation(fin_junk, acc[:, b, :].rearrange("p (k t) -> p k t", t=SPAN), ACT.Square,
                                   accum_out=ssq[:, 4 + b:5 + b]).then_inc(fin_act, 1)
                    act.wait_ge(fin_dve, FIN.after(n, "mean_sq"))
                    act.activation(rstd[:, 4 + b:5 + b], ssq[:, 6 + b:7 + b], ACT.Sqrt).then_inc(fin_act, 1)

            def split_hi(tile):
                _, slot, ready = ring_item(0, tile)
                act.wait_ge(ring_ready[slot], ready)
                if tile >= FIRST_SPLIT + HI_SLOTS:
                    act.wait_ge(ring_used, tile - HI_SLOTS + 1)
                act.activation(w_hi_r[tile % HI_SLOTS], ring[:, slot, :], ACT.Copy).then_inc(w_hi_made, 1)

            def out_split_hi(i):
                m, slot, ready = ring_item(0, W_TILES + 1 + i)
                act.wait_ge(ring_ready[slot], ready)
                if i < GATHERS:
                    act.wait_ge(scan_mm, ORDER.index(((CHUNKS - 1, "dS", 0) if i > 1 else (CHUNKS - 1, "rhs", 0))) + 1)
                else:
                    act.wait_ge(ring_used, m - GATHERS + 1)
                act.activation(out_hi_r(i), ring[:, slot, :], ACT.Copy).then_inc(w_hi_made, 1)

            def y_split_hi(piece):
                k0, k1 = Y_PIECES[piece]
                act.activation(y_hi_r[:, k0:k1, :], yT[:, k0:k1, :], ACT.Copy).then_inc(y_hi_made, 1)

            def squares(span):
                for b in range(BLOCKS):
                    act.wait_ge(x_loaded[b], 16 * (span + 1))
                    if span:
                        act.wait_ge(turned2_out, NB8 * span)
                    act.activation(yT[:, 8 * b:8 * b + 8, :], x_in[:, b, :].rearrange("p (k t) -> p k t", k=8),
                                   ACT.Square, accum_out=ssq[:, b:b + 1]).then_inc(norm_act, 1)

            def move_residual(span):
                if span:
                    act.wait_ge(stored, 16 * BLOCKS * span)
                act.wait_ge(norm2_dve, NORM2.after(span * BLOCKS + BLOCKS - 1, "scaled"))
                for b in range(BLOCKS):
                    act.activation(acc[:, b, :], x_mid[:, b, :], ACT.Copy).then_inc(acc_set, 1)

            for span in range(SPANS):
                if span == 0:
                    squares(span)
                for b in range(BLOCKS):
                    act.wait_ge(norm_dve, NORM1.after(span * BLOCKS + b, "mean_sq"))
                    act.activation(rstd[:, b:b + 1], ssq[:, 2 + b:3 + b], ACT.Sqrt).then_inc(norm_act, 1)
                if span == 0:
                    act.wait_ge(consts_in, 48)
                else:
                    act.wait_ge(lora_mm, 3 * span + 1)
                if span == 0:
                    act.wait_ge(turned_out, NB8)
                    act.wait_ge(pad_set, 1)
                    for k0, k1 in X_PIECES:
                        act.activation(x_hi_r(k0, k1), hT[:, k0 * WID:k1 * WID], ACT.Copy).then_inc(x_hi_made, 1)
                    for tile in range(FIRST_SPLIT, 6):
                        split_hi(tile)
                    act.wait_ge(lora_mm, 1)
                if span:
                    act.wait_ge(gate_mm, span * GATED)
                act.activation(wa_in[0:HALF, :], banks[4][0:HALF, 0:SPAN], ACT.Tanh).then_inc(lora_act, 1)
                act.activation(wa_in[HALF:P, :], banks[4][HALF:P, 0:SPAN], ACT.Copy).then_inc(lora_act, 1)
                act.wait_ge(lora_mm, 3 * span + 2)
                act.activation(g_in[:, 0, :], banks[5][:, 0:SPAN], ACT.Sigmoid).then_inc(lora_act, 1)
                act.wait_ge(lora_mm, 3 * span + 3)
                act.activation(g_in[0:32, 1, :], banks[6][0:32, 0:SPAN], ACT.Sigmoid).then_inc(lora_act, 1)
                for h in range(PAIRS):
                    n = span * PAIRS + h
                    zb = banks[4 if h % 2 else 7]
                    act.wait_ge(z_mm, 2 * n + 2)
                    if h:
                        act.wait_ge(mix, MIX.after(n - 1, "bonus"))
                    act.activation(sig_w, zb[:, 0:SPAN], ACT.Sigmoid, bias=v("w0", h)).then_inc(z_act, 1)
                    act.activation(sig_a, zb[:, SPAN:2 * SPAN], ACT.Sigmoid, bias=v("a0", h)).then_inc(z_act, 1)
                    for j in range(3):
                        act.wait_ge(ring_used, span * RING_PER_SPAN + 3 * h + j + 1)
                        if j == 0 and h == 0:
                            act.wait_ge(lora_mm, 3 * (span + 1))
                        if span == 0 and h and j:
                            split_hi(3 * h + j + 2)
                        act.activation(raw[h % 2][j], banks[(3 * h + j) % 4][:, 0:WID], ACT.Copy).then_inc(tile_out, 1)
                    if span == 0 and h:
                        split_hi(3 * h + 5)
                    act.wait_ge(mix, MIX.after(n, "log_prod"))
                    act.activation(e_p, lp, ACT.Exp).then_inc(exp_act, 1)
                    act.activation(e_n, lp, ACT.Exp, scale=-1.0).then_inc(exp_act, 1)
                    act.wait_ge(mix, MIX.after(n, "log_prev"))
                    act.activation(e_m, lm, ACT.Exp).then_inc(exp_act, 1)
                    act.wait_ge(sums_mm, n + 1)
                    act.activation(nrm, banks[5][:, 0:SPAN], ACT.Sqrt).then_inc(sqrt_act, 1)
                act.wait_ge(mix, MIX.after(span * PAIRS + PAIRS - 1, "bonus"))
                next_tile = 0

                def conv_c(until):
                    nonlocal next_tile
                    for i in range(next_tile, until):
                        t, j = divmod(i, 3)
                        if j == 0:
                            if t:
                                act.wait_ge(conv, CONV.after(span * CONVS + t - 1, "u"))
                            act.wait_ge(ring_used, span * RING_PER_SPAN + 3 * PAIRS + i + 1)
                            act.activation(c_raw, banks[(3 * PAIRS + i) % 4][:, 0:WID], ACT.Copy).then_inc(tile_out, 1)
                    next_tile = until

                next_split = 3 * PAIRS + 3
                bufs = chunk_buffers(span)
                B_t, K_t, V_t, L_T, LK_T, X, X_T, W_b, M_b = ([bufs[9 * q + i] for q in range(2)] for i in range(9))
                rhs_b, SA_b, _ = bufs[18:21]
                for i, (c, name, l) in enumerate(ORDER):
                    conv_c(tiles_done(span, i))
                    while span == 0 and next_split < splits_due(i, 2):
                        split_hi(next_split)
                        next_split += 1
                    if span == 0 and (c, name) == (CHUNKS - 2, "var"):
                        act.wait_ge(ring_used, W_TILES)
                        act.wait_ge(conv, CONV.after(CONVS - 1, "gate"))
                        y_split_hi(0)
                    if span == 0 and (c, name) in ((CHUNKS - 1, "Y"), (CHUNKS - 1, "mean")):
                        out_split_hi(0 if name == "Y" else 1)
                    q = c % 2
                    if name == "mean":
                        act.wait_ge(*scan_done(span, c, "mean"))
                        act.activation(W_b[q], X[q], ACT.Square).then_inc(scan_act, 1)
                    if name == "var":
                        act.wait_ge(scan_mm, span * len(ORDER) + i + 1)
                        act.activation(M_b[q], banks[4 + i % 4][:, :], ACT.Sqrt, bias=v("eps", 1)).then_inc(scan_act, 1)
                    if name not in BY_ACT:
                        continue
                    act.wait_ge(scan_mm, span * len(ORDER) + i + 1)
                    src = banks[4 + i % 4][:, :]
                    if name == "Y":
                        dst = yT[:, 0:PAIRS, c * CHUNK:(c + 1) * CHUNK]
                        src = src.rearrange("p (h t) -> p h t", h=PAIRS)
                    else:
                        dst = {"B_t": B_t[q], "K_t": K_t[q], "V_t": V_t[q], "W": W_b[q], "rhs": rhs_b, "SA": SA_b}[name]
                    if span and i < 4:
                        act.wait_ge(pad_saved, span + 1)
                    act.activation(dst, src, ACT.Copy).then_inc(scan_act, 1)
                    if span and i == LAST_STATE:
                        gelu_tanhs(span - 1)
                if span == 0:
                    out_split_hi(2)
                    out_split_hi(3)
                    for i in range(GATED):
                        act.wait_ge(gated, i + 1)
                        y_split_hi(1 + i)
                    for i in range(4, KT):
                        out_split_hi(i)
                for b in range(BLOCKS):
                    act.wait_ge(norm2_dve, NORM2.after(span * BLOCKS + b, "sum3"))
                    act.activation(h2[:, b, :], x_mid[:, b, :], ACT.Square, accum_out=ssq[:, b:b + 1]).then_inc(norm2_act, 1)
                    act.wait_ge(norm2_dve, NORM2.after(span * BLOCKS + b, "mean_sq"))
                    act.activation(rstd[:, b:b + 1], ssq[:, 2 + b:3 + b], ACT.Sqrt).then_inc(norm2_act, 1)
                for n in range(NB8):
                    b, k4 = divmod(n, 4)
                    act.wait_ge(turned2, span * NB8 + n + 1)
                    act.activation(hT_v[:, 4 * k4:4 * k4 + 4, PAD + b * P:PAD + (b + 1) * P],
                                   banks[n][:, :].rearrange("p (k t) -> p k t", k=4), ACT.Copy).then_inc(turned2_out, 1)
                if span == 0:
                    move_residual(span)
                def score_copy(s):
                    n = span * SIDES + s
                    act.wait_ge(score_mm, n + 1)
                    if s >= 2:
                        act.wait_ge(pick, side_after(span, s - 2))
                    act.activation(sc[s % 2], banks[4 + s % 2][:, 0:SPAN].rearrange("p (b n) -> p b n", b=BLOCKS),
                                   ACT.Copy).then_inc(score_out, 1)

                for i in range(Q_TILES):
                    act.wait_ge(ring_used, span * RING_PER_SPAN + W_TILES + 1 + KT + i + 1)
                    if i >= 4:
                        act.wait_ge(score_mm, span * SIDES + (i - 4) // 2 + 1)
                    act.activation(q_T[i % 4], banks[i % 4][:, 0:SPAN], ACT.Copy).then_inc(tile_out, 1)
                    if i % 2 == 0 and i:
                        score_copy(i // 2 - 1)
                score_copy(SIDES - 1)
                if span:
                    final_roots(span - 1)
                if span + 1 < SPANS:
                    squares(span + 1)
                act.wait_ge(pick, span * PICK_SPAN + TK_SPAN + GATES.after(0, "shifted"))
                act.activation(g_e, g_e, ACT.Exp).then_inc(pick_act, 1)
                if span:
                    move_residual(span)
            gelu_tanhs(SPANS - 1)
            final_roots(SPANS - 1)

        @block.vector
        def _(dve):
            def chain(signal, start):
                n = [start]

                def step(ins):
                    n[0] += 1
                    ins.then_inc(signal, 1)
                    dve.wait_ge(signal, n[0])
                step.count = n
                return step

            def by_head(ap):
                return ap.rearrange("p (h t) -> p h t", h=PAIRS)

            def each_head(name):
                return c_(name).unsqueeze(1).to_broadcast([P, PAIRS, CHUNK])

            def row(r):
                slot, n = r % GATHERS, r // GATHERS
                span, r_span = divmod(r, ROWS_SPAN)
                table, b, k = row_of(r_span)
                dve.wait_ge(gathered[slot], 16 * (n + 1))
                if table == 0:
                    ins = dve.tensor_tensor_reduce(gath[:, slot, :], gath[:, slot, :], h2[:, b, :], 1.0, 0.0,
                                                   ALU.mult, ALU.add, dots[:, b, k:k + 1])
                else:
                    if r_span == BLOCKS * PICKS:
                        dve.wait_ge(acc_set, BLOCKS * (span + 1))
                    dve.wait_ge(row_used, r)
                    ins = dve.scalar_tensor_tensor(out=acc[:, b, :], in0=gath[:, slot, :], scalar=gates[:, b, k:k + 1],
                                                   in1=acc[:, b, :], op0=ALU.mult, op1=ALU.add)
                ins.then_inc(row_used, 1)

            next_row = 0

            def split_lo(tile):
                _, slot, _ = ring_item(0, tile)
                dve.wait_ge(w_hi_made, tile - FIRST_SPLIT + 1)
                dve.tensor_tensor(ring_r[:, slot, :], ring[:, slot, :], w_hi_r[tile % HI_SLOTS].bitcast(F32), ALU.subtract)\
                   .then_inc(w_lo_made, 1)

            def out_split_lo(i):
                _, slot, _ = ring_item(0, W_TILES + 1 + i)
                dve.wait_ge(w_hi_made, N_SPLIT + i + 1)
                dve.tensor_tensor(ring_r[:, slot, :], ring[:, slot, :], out_hi_r(i).bitcast(F32), ALU.subtract).then_inc(w_lo_made, 1)

            def y_split_lo(piece):
                k0, k1 = Y_PIECES[piece]
                dve.wait_ge(y_hi_made, piece + 1)
                dve.tensor_tensor(yT_r[:, k0:k1, :], yT[:, k0:k1, :], y_hi_r[:, k0:k1, :].bitcast(F32), ALU.subtract)\
                   .then_inc(y_lo_made, 1)

            def rows(count):
                nonlocal next_row
                for _ in range(count):
                    row(next_row)
                    next_row += 1

            def rows_over(span, i, n, count):
                if span:
                    rows((i + 1) * count // n - i * count // n)

            def gelus(span):
                dve.wait_ge(row_used, span * ROWS_SPAN + BLOCKS * PICKS)
                for b in range(BLOCKS):
                    n = span * BLOCKS + b
                    step = chain(gelu, n * len(GELU))
                    x, g = dots[:, b, :], gel[:, :]
                    step(dve.tensor_tensor(g, x, x, ALU.mult))
                    step(dve.tensor_tensor(g, g, x, ALU.mult))
                    step(dve.scalar_tensor_tensor(out=g, in0=g, scalar=GELU_C, in1=x, op0=ALU.mult, op1=ALU.add))
                    dve.wait_ge(gelu_act, n + 1)
                    step(dve.scalar_tensor_tensor(out=g, in0=g, scalar=1.0, in1=x, op0=ALU.add, op1=ALU.mult))
                    step(dve.scalar_tensor_tensor(out=gates[:, b, :], in0=g, scalar=0.5, in1=gates[:, b, :],
                                                  op0=ALU.mult, op1=ALU.mult))

            def final(span):
                for b in range(BLOCKS):
                    n = span * BLOCKS + b
                    step = chain(fin_dve, n * len(FIN))
                    dve.wait_ge(fin_act, 2 * n + 1)
                    step(dve.tensor_scalar(ssq[:, 6 + b:7 + b], ssq[:, 4 + b:5 + b], 1.0 / D, RMS_EPS, ALU.mult, ALU.add))
                    dve.wait_ge(fin_act, 2 * n + 2)
                    step(dve.reciprocal(rstd[:, 6 + b:7 + b], rstd[:, 4 + b:5 + b]))
                    dve.wait_ge(fin_gain, 16 * (span + 1))
                    step(dve.scalar_tensor_tensor(out=acc[:, b, :], in0=acc[:, b, :], scalar=rstd[:, 6 + b:7 + b],
                                                  in1=gain_last, op0=ALU.mult, op1=ALU.mult))

            dve.memset(state[:, 0, :], 0.0).then_inc(zeroed, 1)
            dve.memset(h_pad[:, :, :], 0.0).then_inc(zeroed, 1)
            dve.wait_ge(zeroed, 2)
            for span in range(SPANS):
                if span:
                    dve.wait_ge(ring_used, span * RING_PER_SPAN)
                dve.tensor_copy(hT_v[:, :, 0:PAD], h_pad[:, :, :]).then_inc(pad_set, 1)
                step = chain(norm_dve, span * BLOCKS * len(NORM1))
                for b in range(BLOCKS):
                    n = span * 2 * BLOCKS
                    dve.wait_ge(norm_act, n + b + 1)
                    step(dve.tensor_scalar(ssq[:, 2 + b:3 + b], ssq[:, b:b + 1], 1.0 / D, RMS_EPS, ALU.mult, ALU.add))
                    dve.wait_ge(norm_act, n + BLOCKS + b + 1)
                    step(dve.reciprocal(rstd[:, 2 + b:3 + b], rstd[:, b:b + 1]))
                    step(dve.tensor_scalar(x_in[:, b, :], x_in[:, b, :], rstd[:, 2 + b:3 + b], None, ALU.mult))
                    rows_over(span, b, BLOCKS, ROWS["norm"])
                if span == 0:
                    dve.wait_ge(consts_in, 48)
                for n in range(NB8):
                    b, k4 = divmod(n, 4)
                    dve.wait_ge(turned, span * NB8 + n + 1)
                    gain = v("norm_mix", 4 * k4, 4).unsqueeze(2).to_broadcast([P, 4, P])
                    dve.tensor_tensor(hT_v[:, 4 * k4:4 * k4 + 4, PAD + b * P:PAD + (b + 1) * P],
                                      banks[n][:, :].rearrange("p (k t) -> p k t", k=4), gain, ALU.mult)\
                       .then_inc(turned_out, 1)
                    rows_over(span, n, NB8, ROWS["turn"])
                dve.wait_ge(turned_out, NB8 * (span + 1))
                dve.tensor_copy(h_pad[:, :, :], hT_v[:, :, SPAN:SPAN + PAD]).then_inc(pad_saved, 1)
                step = chain(lora_split, 4 * span)
                dve.wait_ge(lora_loaded, 16 * (span + 1))
                for j, (c0, c1) in enumerate(((0, 64), (64, 128), (128, LORA))):
                    mu = v("mu_lora", j * KT, KT).unsqueeze(2).to_broadcast([P, KT, c1 - c0])
                    step(dve.tensor_tensor(lora_prev[:, :, c0:c1], lora_cur[:, :, c0:c1], mu, ALU.mult))
                    rows_over(span, j, 4, ROWS["lora"])
                step(dve.tensor_tensor(lora_cur, lora_cur, lora_prev, ALU.subtract))
                rows_over(span, 3, 4, ROWS["lora"])
                rows_over(span, 0, 1, ROWS["low"])
                if span == 0:
                    for tile in range(FIRST_SPLIT, 6):
                        split_lo(tile)
                    dve.wait_ge(lora_mm, 3)
                    dve.wait_ge(pad_saved, 1)
                    dve.wait_ge(pad_set, 1)
                    for i, (k0, k1) in enumerate(X_PIECES):
                        dve.wait_ge(x_hi_made, i + 1)
                        dve.tensor_tensor(hT_r[:, k0 * WID:k1 * WID], hT[:, k0 * WID:k1 * WID], x_hi_r(k0, k1).bitcast(F32),
                                          ALU.subtract).then_inc(x_lo_made, 1)
                step = chain(mix, span * PAIRS * len(MIX))
                for h in range(PAIRS):
                    n = span * PAIRS + h
                    spread = lambda i: rows_over(span, 7 * h + i, 7 * PAIRS, ROWS["head"])
                    if h == 0:
                        dve.wait_ge(lora_mm, 3 * (span + 1))
                    dve.wait_ge(z_act, 2 * n + 1)
                    step(dve.tensor_scalar(lw, sig_w, -EXP_M_HALF, None, ALU.mult))
                    step(dve.tensor_tensor_scan(lp, c_("keep"), lw, 0.0, ALU.mult, ALU.add))
                    step(dve.tensor_tensor(lm, lp, lw, ALU.subtract))
                    spread(0)
                    outs = (r_s, k_s, yT[:, h, :])
                    for j in range(3):
                        if span == 0 and h and j:
                            split_lo(3 * h + j + 2)
                        src = raw[h % 2][j]
                        dve.wait_ge(*tile_taken(span, 3 * h + j))
                        step(dve.tensor_tensor(diff, src[:, PAD - 1:PAD - 1 + SPAN], src[:, PAD:PAD + SPAN], ALU.subtract))
                        step(dve.scalar_tensor_tensor(out=outs[j], in0=diff, scalar=v("mu_rkv", j * PAIRS + h),
                                                      in1=src[:, PAD:PAD + SPAN], op0=ALU.mult, op1=ALU.add))
                        spread(1 + j)
                    step(dve.tensor_scalar(kk_raw, k_s, v("k_k", h), None, ALU.mult))
                    step(dve.tensor_tensor(kk_sq, kk_raw, kk_raw, ALU.mult))
                    dve.wait_ge(z_act, 2 * n + 2)
                    step(dve.tensor_scalar(a_gain, sig_a, 1.0, v("k_a", h), ALU.subtract, ALU.mult))
                    step(dve.scalar_tensor_tensor(out=k_new, in0=a_gain, scalar=1.0, in1=k_s, op0=ALU.add, op1=ALU.mult))
                    step(dve.scalar_tensor_tensor(out=rk, in0=r_s, scalar=v("r_k", h), in1=k_new, op0=ALU.mult, op1=ALU.mult))
                    spread(4)
                    dve.wait_ge(exp_act, 3 * n + 3)
                    step(dve.tensor_tensor(R_c[:, h, :], r_s, e_p, ALU.mult))
                    step(dve.tensor_tensor(K_c[:, h, :], k_new, e_n, ALU.mult))
                    step(dve.tensor_copy(p_end[:, h, :], e_p[:, CHUNK - 1:SPAN:CHUNK]))
                    spread(5)
                    if span == 0 and h:
                        split_lo(3 * h + 5)
                    dve.wait_ge(sqrt_act, n + 1)
                    step(dve.tensor_scalar(nrm, nrm, 1e-12, None, ALU.max))
                    step(dve.reciprocal(nrm, nrm))
                    step(dve.tensor_tensor(kk, kk_raw, nrm, ALU.mult))
                    step(dve.tensor_tensor(kk_sq, kk, sig_a, ALU.mult))
                    step(dve.tensor_tensor(B_c[:, h, :], kk_sq, e_n, ALU.mult))
                    step(dve.scalar_tensor_tensor(out=A_c[:, h, :], in0=kk, scalar=-1.0, in1=e_m, op0=ALU.mult, op1=ALU.mult))
                    dve.wait_ge(sums_mm, n + 1)
                    step(dve.tensor_tensor(bonus[:, h, :], banks[6][:, 0:SPAN], yT[:, h, :], ALU.mult))
                    spread(6)
                assert step.count[0] == (span + 1) * PAIRS * len(MIX)
                step = chain(conv, span * CONVS * len(CONV))
                next_tile = 0

                def conv_steps(until):
                    nonlocal next_tile
                    for i in range(next_tile, until):
                        t, j = divmod(i, 3)
                        spread = lambda i: rows_over(span, 3 * t + i, 3 * CONVS, ROWS["conv"])
                        bank = banks[(3 * PAIRS + i) % 4]
                        if j:
                            dve.wait_ge(ring_used, span * RING_PER_SPAN + 3 * PAIRS + i + 1)
                        if j == 1:
                            dve.wait_ge(*tile_taken(span, 3 * PAIRS + i - 1))
                            conv_step(dve.tensor_tensor(u_c, bank[:, 0:WID], c_raw, ALU.mult))
                            spread(0)
                            conv_step(dve.tensor_scalar(conv_o[0], u_c[:, 0:SPAN], v("conv_w", t), None, ALU.mult))
                            for tap in (1, 2):
                                conv_step(dve.scalar_tensor_tensor(
                                    out=conv_o[tap], in0=u_c[:, tap:tap + SPAN], scalar=v("conv_w", tap * CONVS + t),
                                    in1=conv_o[tap - 1], op0=ALU.mult, op1=ALU.add))
                            spread(1)
                        if j == 2:
                            conv_step(dve.tensor_tensor(yT[:, PAIRS + t, :], bank[:, PAD:PAD + SPAN], conv_o[2], ALU.mult))
                            spread(2)
                    next_tile = until

                conv_step = step
                conv_steps(tiles_first(span))
                step = chain(scan_dve, span * len(DVE_OPS))
                bufs = chunk_buffers(span)
                B_t, K_t, V_t, L_T, LK_T, X, X_T, W_b, M_b = ([bufs[9 * q + i] for q in range(2)] for i in range(9))
                sum_b = bufs[20]
                next_split = 3 * PAIRS + 3
                k_before = 0
                for what, c, name, l in DVE_OPS:
                    if name == "M":
                        k = ORDER.index((c, "W", l - 1) if l > 1 else (c, "L_T", 0))
                    else:
                        k = ORDER.index((c, "L_T", 0) if (what, name) == ("eye", "X_T") else (c, name, l))
                    conv_steps(max(next_tile, tiles_done(span, k)))
                    while span == 0 and next_split < splits_due(k, 1):
                        split_lo(next_split)
                        next_split += 1
                    if span and k > k_before:
                        if k_before < LAST_STATE:
                            total = scan_time(0, LAST_STATE)
                            rows(scan_time(0, min(k, LAST_STATE)) * ROWS["scan"] // total
                                 - scan_time(0, k_before) * ROWS["scan"] // total)
                        if k > LAST_STATE:
                            if k_before < LAST_STATE:
                                gelus(span - 1)
                                k_before = LAST_STATE
                            total = scan_time(LAST_STATE, len(ORDER))
                            rows(scan_time(LAST_STATE, k) * ROWS["scan_v"] // total
                                 - scan_time(LAST_STATE, k_before) * ROWS["scan_v"] // total)
                        k_before = k
                    if span == 0 and (what, c, name) == ("take", CHUNKS - 1, "dS"):
                        y_split_lo(0)
                        out_split_lo(0)
                    if span == 0 and (what, c, name) == ("inverse", CHUNKS - 1, "var"):
                        out_split_lo(1)
                    q, n = c % 2, span * CHUNKS + c
                    ts = slice(c * CHUNK, (c + 1) * CHUNK)
                    if what == "mask":
                        if l > 1:
                            dve.wait_ge(scan_mm, span * len(ORDER) + ORDER.index((c, "W", l - 1)) + 1)
                        mask = c_("up", l * CHUNK, CHUNK).unsqueeze(1).to_broadcast([P, PAIRS, CHUNK])
                        step(dve.tensor_tensor(by_head(M_b[q]), by_head(L_T[q]), mask, ALU.mult))
                        continue
                    if what == "eye":
                        src, dst = (M_b[q], X_T[q]) if name == "X_T" else (X[q], X[q])
                        step(dve.tensor_tensor(by_head(dst), by_head(src), each_head("eye"), ALU.add))
                        continue
                    if what == "decay":
                        end = p_end[:, :, c:c + 1].to_broadcast([P, PAIRS, CHUNK])
                        step(dve.tensor_tensor(by_head(state[:, (n + 1) % 2, :]), by_head(sum_b), end, ALU.mult))
                        continue
                    y_ts = yT[:, 0:PAIRS, ts]
                    if name == "var":
                        vec3 = lambda n: v(n, 0, PAIRS).unsqueeze(2).to_broadcast([P, PAIRS, CHUNK])
                        if what == "inverse":
                            dve.wait_ge(*scan_done(span, c, "root"))
                            step(dve.reciprocal(M_b[q], M_b[q]))
                        elif what == "scaled":
                            step(dve.tensor_tensor(X[q], X[q], M_b[q], ALU.mult))
                        elif what == "gain":
                            step(dve.tensor_tensor(by_head(X[q]), by_head(X[q]), vec3("gn_w"), ALU.mult))
                        elif what == "offset":
                            step(dve.tensor_tensor(by_head(X[q]), by_head(X[q]), vec3("gn_b"), ALU.add))
                        elif what == "bonus":
                            step(dve.tensor_tensor(y_ts, by_head(X[q]), bonus[:, :, ts], ALU.add))
                        continue
                    dve.wait_ge(scan_mm, span * len(ORDER) + k + 1)
                    src = banks[4 + k % 4][:, :]
                    if name == "mean":
                        dve.wait_ge(*scan_done(span, c, "Y"))
                        step(dve.tensor_tensor(by_head(X[q]), y_ts, by_head(src), ALU.subtract))
                    if name in ("L_T", "LK_T"):
                        step(dve.tensor_tensor(by_head((L_T if name == "L_T" else LK_T)[q]), by_head(src),
                                               each_head("before"), ALU.mult))
                    elif name == "L":
                        step(dve.tensor_tensor(by_head(X[q]), by_head(src), each_head("low0"), ALU.mult))
                    elif name in ("RB_T", "RK_T"):
                        step(dve.tensor_tensor((B_c if name == "RB_T" else K_c)[:, :, ts], by_head(src),
                                               each_head("upto"), ALU.mult))
                    elif name in ("X", "X_T"):
                        dst = (X if name == "X" else X_T)[q]
                        step(dve.tensor_tensor(dst, src, dst, ALU.add))
                    elif name == "dS":
                        step(dve.tensor_tensor(sum_b, src, state[:, n % 2, :], ALU.add))
                if span:
                    total = scan_time(LAST_STATE, len(ORDER))
                    rows(ROWS["scan_v"] - scan_time(LAST_STATE, k_before) * ROWS["scan_v"] // total)
                conv_steps(CONV_TILES)
                for i in range(GATED):
                    dve.wait_ge(gate_mm, span * GATED + i + 1)
                    hs = slice(2 * i, 2 * i + 2)
                    dve.tensor_tensor(yT[:, hs, :], yT[:, hs, :], banks[i][:, :].rearrange("p (h t) -> p h t", h=2), ALU.mult)\
                       .then_inc(gated, 1)
                    rows_over(span, i, GATED, ROWS["gate"])
                if span == 0:
                    out_split_lo(2)
                    out_split_lo(3)
                    for i in range(GATED):
                        y_split_lo(1 + i)
                    for i in range(4, KT):
                        out_split_lo(i)
                rows_over(span, 0, 1, ROWS["w_out"])
                step = chain(norm2_dve, span * BLOCKS * len(NORM2))
                dve.wait_ge(res_loaded, 16 * (BLOCKS + 1) * (span + 1))
                for b in range(BLOCKS):
                    if b == 0:
                        dve.wait_ge(wout_mm, span + 1)
                    else:
                        dve.wait_ge(ring_used, span * RING_PER_SPAN + W_TILES + 1 + KT)
                    for n in range(4):
                        cs = slice(n * 512, (n + 1) * 512)
                        step(dve.tensor_tensor(x_mid[:, b, cs], banks[4 * b + n][:, :], x_mid[:, b, cs], ALU.add))
                    n = span * 2 * BLOCKS + 2 * b
                    dve.wait_ge(norm2_act, n + 1)
                    step(dve.tensor_scalar(ssq[:, 2 + b:3 + b], ssq[:, b:b + 1], 1.0 / D, RMS_EPS, ALU.mult, ALU.add))
                    dve.wait_ge(norm2_act, n + 2)
                    step(dve.reciprocal(rstd[:, 2 + b:3 + b], rstd[:, b:b + 1]))
                    step(dve.scalar_tensor_tensor(out=h2[:, b, :], in0=x_mid[:, b, :], scalar=rstd[:, 2 + b:3 + b],
                                                  in1=gain_f, op0=ALU.mult, op1=ALU.mult))
                    rows_over(span, b, BLOCKS, ROWS["norm2"])
                step = chain(pick, span * PICK_SPAN)

                def rows_at(h, point):
                    i = POINTS * h + point
                    if span:
                        rows_over(span, i, POINTS * HEADS, ROWS["side"])
                    elif i:
                        rows(OWN[i] - OWN[i - 1])

                for s in range(SIDES):
                    dve.wait_ge(score_out, span * SIDES + s + 1)
                    src = sc[s % 2]
                    for b in range(BLOCKS):
                        step(dve.max(top_s[:, b, s, 0:8], src[:, b, :]))
                    for b in range(BLOCKS):
                        step(dve.match_replace(rest[:, b, :], top_s[:, b, s, 0:8], src[:, b, :], FAR))
                    for b in range(BLOCKS):
                        step(dve.max(top_s[:, b, s, 8:16], rest[:, b, :]))
                    for b in range(BLOCKS):
                        step(dve.max_index(top_i[:, b, s, 0:8], top_s[:, b, s, 0:8], src[:, b, :]))
                    for b in range(BLOCKS):
                        step(dve.max_index(top_i[:, b, s, 8:16], top_s[:, b, s, 8:16], rest[:, b, :]))
                    rows_at(s // 2, s % 2)
                    if s % 2 == 0:
                        continue
                    hs = slice((s // 2) * TOPK, (s // 2) * TOPK + 8), slice((s // 2) * TOPK + 8, (s // 2 + 1) * TOPK)
                    for b in range(BLOCKS):
                        first = top_s[:, b, s - 1, :].unsqueeze(2).to_broadcast([P, TOPK, TOPK])
                        second = top_s[:, b, s, :].unsqueeze(1).to_broadcast([P, TOPK, TOPK])
                        step(dve.tensor_tensor(cand[:, b, :].rearrange("p (i j) -> p i j", i=TOPK), first, second, ALU.add))
                    for b in range(BLOCKS):
                        step(dve.max(cand_s[:, b, hs[0]], cand[:, b, :]))
                    for b in range(BLOCKS):
                        step(dve.match_replace(cand2[:, b, :], cand_s[:, b, hs[0]], cand[:, b, :], FAR))
                    for b in range(BLOCKS):
                        step(dve.max(cand_s[:, b, hs[1]], cand2[:, b, :]))
                    for b in range(BLOCKS):
                        step(dve.max_index(cand_i[:, b, hs[0]], cand_s[:, b, hs[0]], cand[:, b, :]))
                    for b in range(BLOCKS):
                        step(dve.max_index(cand_i[:, b, hs[1]], cand_s[:, b, hs[1]], cand2[:, b, :]))
                    rows_at(s // 2, 2)
                    hk = slice(s // 2 * TOPK, (s // 2 + 1) * TOPK)
                    bk = lambda ap: ap.rearrange("p (b k) -> p b k", b=BLOCKS)
                    step(dve.tensor_copy(top_f.rearrange("p (b j) -> p b j", b=BLOCKS),
                                         top_i[:, :, s - 1:s + 1, :].rearrange("p b s j -> p b (s j)")))
                    for half, dst in ((0, e_1), (1, e_2)):
                        if half == 0:
                            step(dve.tensor_scalar(bk(sl_u), cand_i[:, :, hk], 4, None, ALU.logical_shift_right))
                        else:
                            step(dve.tensor_scalar(bk(sl_u), cand_i[:, :, hk], TOPK - 1, None, ALU.bitwise_and))
                        step(dve.tensor_copy(sl_f, sl_u))
                        n_bk = BLOCKS * TOPK
                        step(dve.tensor_tensor(hot.rearrange("p (n j) -> p n j", j=TOPK),
                                               sl_f.unsqueeze(2).to_broadcast([P, n_bk, TOPK]),
                                               c_("iota16").unsqueeze(1).to_broadcast([P, n_bk, TOPK]), ALU.is_equal))
                        part = top_f.rearrange("p (b c j) -> p b c j", b=BLOCKS, c=2)[:, :, half, :]\
                            .unsqueeze(2).to_broadcast([P, BLOCKS, TOPK, TOPK])
                        step(dve.tensor_tensor(hot_v.rearrange("p (b k j) -> p b k j", b=BLOCKS, k=TOPK),
                                               hot.rearrange("p (b k j) -> p b k j", b=BLOCKS, k=TOPK), part, ALU.mult))
                        step(dve.tensor_reduce(dst, hot_v.rearrange("p (n j) -> p n j", j=TOPK), AX_X, ALU.add))
                    step(dve.scalar_tensor_tensor(out=pick_i[:, span % 2, :, hk], in0=bk(e_1), scalar=float(NKEYS),
                                                  in1=bk(e_2), op0=ALU.mult, op1=ALU.add))
                    assert step.count[0] == head_picked(span, s // 2)
                    rows_at(s // 2, 3)
                assert next_row >= span * ROWS_SPAN
                if span:
                    final(span - 1)
                by_pick = lambda ap: ap.rearrange("p (n k) -> p n k", k=TOPK)
                all_s = cand_s.rearrange("p b n -> p (b n)")
                top = all_s[:, 0:BLOCKS * PICKS:TOPK].unsqueeze(2).to_broadcast([P, BLOCKS * HEADS, TOPK])
                step(dve.tensor_tensor(by_pick(g_e), by_pick(all_s), top, ALU.subtract))
                dve.wait_ge(pick_act, span + 1)
                step(dve.tensor_reduce(g_s, by_pick(g_e), AX_X, ALU.add))
                step(dve.reciprocal(g_r, g_s))
                step(dve.tensor_tensor(by_pick(gates[:, :, :].rearrange("p b n -> p (b n)")), by_pick(g_e),
                                       g_r.unsqueeze(2).to_broadcast([P, BLOCKS * HEADS, TOPK]), ALU.mult))
                assert step.count[0] == (span + 1) * PICK_SPAN
            rows((SPANS - 1) * ROWS_SPAN + U - next_row)
            gelus(SPANS - 1)
            rows(BLOCKS * PICKS)
            final(SPANS - 1)

        @block.gpsimd
        def _(pool):
            for r in range(SPANS * ROWS_SPAN):
                slot = r % GATHERS
                span, r_span = divmod(r, ROWS_SPAN)
                table, b, k = row_of(r_span)
                if table == 0 and b == 0 and k % TOPK == 0:
                    pool.wait_ge(pick, head_picked(span, k // TOPK))
                if r >= GATHERS:
                    pool.wait_ge(row_used, r - GATHERS + 1)
                pool.indirect_dma_start(gath[:, slot, :], None, A[("peer_u", "peer_v")[table]],
                                        bass.IndirectOffsetOnAxis(ap=pick_i[:, span % 2, b, k:k + 1], axis=0))\
                    .then_inc(gathered[slot], 16)


def _layouts(inp):
    import numpy as np

    f = np.float32

    def col(a, n):
        return np.asarray(a, f).reshape(n, P).T

    def tiles(w, cols):
        w = np.asarray(w, f).reshape(KT, P, -1, P)[:, :, cols, :]
        return np.ascontiguousarray(w.transpose(2, 1, 0, 3)).reshape(len(cols), P, D)

    order = [g * PAIRS + h for h in range(PAIRS) for g in range(3)]
    order += [3 * PAIRS + g * CONVS + t for t in range(CONVS) for g in (1, 2, 0)]
    vecs = {"norm_mix": col(inp["norm_mix"], KT), "mu_rkv": col(inp["mu_rkv"], 3 * PAIRS), "w0": col(inp["w0"], PAIRS),
            "a0": col(inp["a0"], PAIRS), "k_k": col(inp["k_k"], PAIRS), "k_a": col(inp["k_a"], PAIRS),
            "r_k": col(inp["r_k"], PAIRS), "gn_w": col(inp["gn_w"], PAIRS), "gn_b": col(inp["gn_b"], PAIRS),
            "conv_w": col(inp["conv_w"], 3 * CONVS), "mu_lora": col(inp["mu_lora"], 3 * KT),
            "eps": np.tile(np.array([[RMS_EPS, GN_EPS]], f), (P, 1))}
    lora = np.concatenate([np.asarray(inp[n], f)[0] for n in ("w1", "a1", "g1")], axis=1)
    g2 = np.asarray(inp["g2"], f)[0]
    g2p = np.zeros((P, D), f)
    g2p[:, :D_RWKV] = g2[:P]
    g2p[:LORA_G - P, D_RWKV:] = g2[P:]
    keys = np.asarray(inp["peer_keys"], f)[0].reshape(SIDES, NKEYS, 2, P).transpose(3, 0, 2, 1)

    i = np.arange(CHUNK)
    s_, t_ = np.meshgrid(i, i, indexing="ij")

    def low(l):
        return ((s_ >> (l + 1) == t_ >> (l + 1)) & (s_ >> l & 1 == 1) & (t_ >> l & 1 == 0)).astype(f)

    two = lambda m: np.tile(m.astype(f), (2, 1))
    head = np.kron(np.eye(2), np.ones((HALF, HALF)))
    cons = {"ident": np.eye(P), "head_ones": head, "head_mean": head / HALF, "eye": two(np.eye(CHUNK)),
            "before": two(s_ < t_), "upto": two(s_ <= t_), "low0": two(low(0)),
            "up": np.concatenate([two(low(l).T) for l in range(LEVELS)], axis=1),
            "keep": np.tile((np.arange(SPAN) % CHUNK != 0)[None], (P, 1)), "iota16": np.tile(np.arange(TOPK)[None], (P, 1))}
    return {
        "x": np.asarray(inp["x"], f).reshape(T, D),
        "vecs": np.ascontiguousarray(np.concatenate([vecs[n] for n in VEC], axis=1)),
        "consts": np.ascontiguousarray(np.concatenate([cons[n].astype(f) for n in CON], axis=1)),
        "w_in": tiles(np.asarray(inp["w_in"])[0], order),
        "lora_in": np.ascontiguousarray(lora.reshape(KT, P, LORA).transpose(1, 0, 2)),
        "w2a2": np.ascontiguousarray(np.concatenate([np.asarray(inp["w2"], f)[0], np.asarray(inp["a2"], f)[0]])),
        "g2": g2p,
        "w_out": np.asarray(inp["w_out"], f)[0],
        "norm_ffn": np.asarray(inp["norm_ffn"], f).reshape(D),
        "wq": tiles(np.asarray(inp["peer_wq"])[0], list(range(Q_TILES))),
        "keys": np.ascontiguousarray(keys),
        "peer_u": np.asarray(inp["peer_u"], f)[0],
        "peer_v": np.asarray(inp["peer_v"], f)[0],
        "norm_final": np.asarray(inp["norm_final"], f).reshape(D),
    }


def kernel(**inputs):
    import concourse.bacc as bacc
    from concourse.bass_utils import run_bass_kernel_spmd

    arrays = _layouts(inputs)
    nc = bacc.Bacc("TRN2", target_bir_lowering=False, num_devices=1)
    A = {n: nc.dram_tensor("in_" + n, a.shape, F32, kind="ExternalInput").ap() for n, a in arrays.items()}
    A["out"] = nc.dram_tensor("out", (T, D), F32, kind="ExternalOutput").ap()
    hymba(nc, A)
    r = run_bass_kernel_spmd(nc, [{"in_" + n: a for n, a in arrays.items()}], core_ids=[0])
    return r.results[0]["out"].reshape(1, T, D)
```
